# Optimizing a Trainium2 kernel written in Bass

```python
import jax
import jax.numpy as jnp
from jax import lax
import numpy as np
import math
import jax, jax.numpy as jnp

D_MODEL = 1024
BATCH = 1
SEQ = 256
DEPTH = 2

CTX_LEN = 256
GRID_W = 64
N_EVEN = (DEPTH + 1) // 2
N_ODD = DEPTH // 2
EPS = 1e-6

MLA_HEADS = 8
QK_NOPE = 64
QK_ROPE = 32
QK_HEAD = QK_NOPE + QK_ROPE
V_HEAD = 64
Q_LORA = 384
KV_LORA = 256
ROPE_BASE = 10000.0
Q_BLOCK = 128

FNET_GROUPS = 4
FNET_GROUP_W = 128
FNET_W = FNET_GROUPS * FNET_GROUP_W

CONF_GROUPS = 4
CONF_W = 512
CONF_WIDTH = 31
SC_W = 512
SC_WIDTH = 3

D_FF = -(-8 * D_MODEL // (3 * 256)) * 256

EVEN_KV_END = Q_LORA + KV_LORA + QK_ROPE
EVEN_IN = EVEN_KV_END + FNET_W
EVEN_MIX = MLA_HEADS * V_HEAD + FNET_W
ODD_IN = 2 * CONF_W + 3 * SC_W
ODD_MIX = CONF_W + SC_W


def rms_norm(x, g):
    xf = x.astype(jnp.float32)
    y = xf * lax.rsqrt(jnp.mean(jnp.square(xf), axis=-1, keepdims=True) + EPS)
    return (y * g.astype(jnp.float32)).astype(x.dtype)

def group_layer_norm(x, g, b, groups):
    bsz, n, w = x.shape
    xf = x.astype(jnp.float32).reshape(bsz, n, groups, w // groups)
    mu = jnp.mean(xf, axis=-1, keepdims=True)
    var = jnp.mean(jnp.square(xf - mu), axis=-1, keepdims=True)
    y = ((xf - mu) * lax.rsqrt(var + EPS)).reshape(bsz, n, w)
    return (y * g.astype(jnp.float32) + b.astype(jnp.float32)).astype(x.dtype)

def modulate(h, shift, scale):
    return h * (1.0 + scale) + shift

def ada_mod(cvec, w, b):
    return jnp.split(jax.nn.silu(cvec) @ w + b, 6, axis=-1)

def axial_rope_tables(n):
    rows = n // GRID_W
    row = jnp.broadcast_to(jnp.arange(rows, dtype=jnp.float32)[:, None], (rows, GRID_W)).reshape(n)
    col = jnp.broadcast_to(jnp.arange(GRID_W, dtype=jnp.float32)[None, :], (rows, GRID_W)).reshape(n)
    per_axis = QK_ROPE // 4
    inv_freq = ROPE_BASE ** (-jnp.arange(per_axis, dtype=jnp.float32) / per_axis)
    ang = jnp.concatenate([row[:, None] * inv_freq, col[:, None] * inv_freq], axis=-1)
    return jnp.cos(ang), jnp.sin(ang)

def rope_tail(t, rope):
    if rope is None:
        return t
    cos, sin = rope
    half = QK_ROPE // 2
    r = t[..., QK_NOPE:].astype(jnp.float32)
    r1, r2 = r[..., :half], r[..., half:]
    rot = jnp.concatenate([r1 * cos - r2 * sin, r2 * cos + r1 * sin], axis=-1).astype(t.dtype)
    return jnp.concatenate([t[..., :QK_NOPE], rot], axis=-1)

def mla_queries(cq, q_ln_g, w_uq, q_norm_g, rope):
    q = jnp.einsum('bsr,rhd->bshd', rms_norm(cq, q_ln_g), w_uq)
    return rope_tail(rms_norm(q, q_norm_g), rope)

def mla_keys_values(ckv, kr, kv_ln_g, w_uk, w_uv, k_norm_g, rope):
    ckv = rms_norm(ckv, kv_ln_g)
    k_nope = jnp.einsum('bsr,rhd->bshd', ckv, w_uk)
    v = jnp.einsum('bsr,rhd->bshd', ckv, w_uv)
    k_rope = jnp.broadcast_to(kr[:, :, None, :], k_nope.shape[:-1] + (QK_ROPE,))
    k = rope_tail(rms_norm(jnp.concatenate([k_nope, k_rope], axis=-1), k_norm_g), rope)
    return k, v

def latent_attention(q, k, v, k_ctx, v_ctx):
    bsz, n, heads, dq = q.shape
    kt = jnp.concatenate([k_ctx, k], axis=1).transpose(0, 2, 1, 3)
    vt = jnp.concatenate([v_ctx, v], axis=1).transpose(0, 2, 1, 3)
    qb = q.reshape(bsz, n // Q_BLOCK, Q_BLOCK, heads, dq).transpose(1, 0, 2, 3, 4)
    scale = dq ** -0.5

    def block(qi):
        s = jnp.einsum('bqhd,bhkd->bhqk', qi, kt).astype(jnp.float32) * scale
        p = jax.nn.softmax(s, axis=-1).astype(vt.dtype)
        return jnp.einsum('bhqk,bhkd->bqhd', p, vt)

    o = lax.map(block, qb)
    return o.transpose(1, 0, 2, 3, 4).reshape(bsz, n, heads * V_HEAD)

def context_attention(q, k, v):
    bsz, n, heads, dq = q.shape
    s = jnp.einsum('bqhd,bkhd->bhqk', q, k).astype(jnp.float32) * (dq ** -0.5)
    p = jax.nn.softmax(s, axis=-1).astype(v.dtype)
    return jnp.einsum('bhqk,bkhd->bqhd', p, v).reshape(bsz, n, heads * V_HEAD)

def fourier_mix(u):
    bsz, n, _ = u.shape
    ug = u.astype(jnp.float32).reshape(bsz, n, FNET_GROUPS, FNET_GROUP_W)
    y = jnp.fft.fft2(ug, axes=(1, 3), norm='ortho').real
    return y.reshape(bsz, n, FNET_W).astype(u.dtype)

def depthwise_conv(u, w):
    width, ch = w.shape
    pad = (width - 1) // 2
    return lax.conv_general_dilated(
        u, w[:, None, :].astype(u.dtype), window_strides=(1,), padding=[(pad, pad)],
        dimension_numbers=('NWC', 'WIO', 'NWC'), feature_group_count=ch)

def odd_mixer(u, conf_dw, conf_dw_b, conf_ln_g, conf_ln_b, sc_dw):
    a, gate, sb, scc, sx = jnp.split(
        u, [CONF_W, 2 * CONF_W, 2 * CONF_W + SC_W, 2 * CONF_W + 2 * SC_W], axis=-1)
    conf = a * jax.nn.sigmoid(gate)
    conf = depthwise_conv(conf, conf_dw) + conf_dw_b
    conf = jax.nn.silu(group_layer_norm(conf, conf_ln_g, conf_ln_b, CONF_GROUPS))
    sc = sb * depthwise_conv(scc * sx, sc_dw)
    return jnp.concatenate([conf, sc], axis=-1)

def swiglu(h, w1, w3, w2):
    return (jax.nn.silu(h @ w1) * (h @ w3)) @ w2

def first_inputs(seed: int = 0) -> dict:
    key = jax.random.key(seed)
    keys = iter(jax.random.split(key, 40))

    def normal(shape, scale):
        return jax.random.normal(next(keys), shape, jnp.float32) * scale

    def gain(shape):
        return 1.0 + 0.05 * jax.random.normal(next(keys), shape, jnp.float32)

    E, O, L, D = N_EVEN, N_ODD, DEPTH, D_MODEL
    return {
        'x': normal((BATCH, SEQ, D), 1.0),
        'c': normal((BATCH, D), 1.0),
        'ctx': normal((BATCH, CTX_LEN, D), 1.0),
        'c_ctx': normal((D,), 1.0),
        'ada_w': normal((L, D, 6 * D), 0.5 * D ** -0.5),
        'ada_b': normal((L, 6 * D), 0.02),
        'norm1_g': gain((L, D)),
        'norm2_g': gain((L, D)),
        'ffn_w1': normal((L, D, D_FF), D ** -0.5),
        'ffn_w3': normal((L, D, D_FF), D ** -0.5),
        'ffn_w2': normal((L, D_FF, D), D_FF ** -0.5),
        'a_w_in': normal((E, D, EVEN_IN), D ** -0.5),
        'a_q_ln_g': gain((E, Q_LORA)),
        'a_kv_ln_g': gain((E, KV_LORA)),
        'a_w_uq': normal((E, Q_LORA, MLA_HEADS, QK_HEAD), Q_LORA ** -0.5),
        'a_w_uk': normal((E, KV_LORA, MLA_HEADS, QK_NOPE), KV_LORA ** -0.5),
        'a_w_uv': normal((E, KV_LORA, MLA_HEADS, V_HEAD), KV_LORA ** -0.5),
        'a_q_norm_g': gain((E, QK_HEAD)),
        'a_k_norm_g': gain((E, QK_HEAD)),
        'a_w_out': normal((E, EVEN_MIX, D), EVEN_MIX ** -0.5),
        'b_w_in': normal((O, D, ODD_IN), D ** -0.5),
        'b_conf_dw': normal((O, CONF_WIDTH, CONF_W), CONF_WIDTH ** -0.5),
        'b_conf_dw_b': normal((O, CONF_W), 0.02),
        'b_conf_ln_g': gain((O, CONF_W)),
        'b_conf_ln_b': normal((O, CONF_W), 0.02),
        'b_sc_dw': normal((O, SC_WIDTH, SC_W), SC_WIDTH ** -0.5),
        'b_w_out': normal((O, ODD_MIX, D), ODD_MIX ** -0.5),
    }

def first_block(x, c, ctx, c_ctx, ada_w, ada_b, norm1_g, norm2_g, ffn_w1, ffn_w3, ffn_w2,
              a_w_in, a_q_ln_g, a_kv_ln_g, a_w_uq, a_w_uk, a_w_uv, a_q_norm_g, a_k_norm_g, a_w_out,
              b_w_in, b_conf_dw, b_conf_dw_b, b_conf_ln_g, b_conf_ln_b, b_sc_dw, b_w_out):
    n = x.shape[1]
    cos, sin = axial_rope_tables(n)
    rope = (cos[:, None, :], sin[:, None, :])
    for i in range(DEPTH):
        ctx_needed = any(l % 2 == 0 for l in range(i + 1, DEPTH))
        j = i // 2
        sh1, sc1, g1, sh2, sc2, g2 = [t[:, None, :] for t in ada_mod(c, ada_w[i], ada_b[i])]
        h = modulate(rms_norm(x, norm1_g[i]), sh1, sc1)
        if i % 2 == 0 or ctx_needed:
            csh1, csc1, cg1, csh2, csc2, cg2 = ada_mod(c_ctx, ada_w[i], ada_b[i])
            hc = modulate(rms_norm(ctx, norm1_g[i]), csh1, csc1)
        if i % 2 == 0:
            w_in = a_w_in[j]
            u = h @ w_in
            ukc = hc @ w_in[:, Q_LORA:EVEN_KV_END]
            k_c, v_c = mla_keys_values(ukc[..., :KV_LORA], ukc[..., KV_LORA:], a_kv_ln_g[j],
                                       a_w_uk[j], a_w_uv[j], a_k_norm_g[j], None)
            k, v = mla_keys_values(u[..., Q_LORA:Q_LORA + KV_LORA], u[..., Q_LORA + KV_LORA:EVEN_KV_END],
                                   a_kv_ln_g[j], a_w_uk[j], a_w_uv[j], a_k_norm_g[j], rope)
            q = mla_queries(u[..., :Q_LORA], a_q_ln_g[j], a_w_uq[j], a_q_norm_g[j], rope)
            o = jnp.concatenate([latent_attention(q, k, v, k_c, v_c), fourier_mix(u[..., EVEN_KV_END:])], axis=-1)
            mix = o @ a_w_out[j]
            if ctx_needed:
                q_c = mla_queries(hc @ w_in[:, :Q_LORA], a_q_ln_g[j], a_w_uq[j], a_q_norm_g[j], None)
                oc = jnp.concatenate([context_attention(q_c, k_c, v_c),
                                      fourier_mix(hc @ w_in[:, EVEN_KV_END:])], axis=-1)
                mix_c = oc @ a_w_out[j]
        else:
            mix = odd_mixer(h @ b_w_in[j], b_conf_dw[j], b_conf_dw_b[j], b_conf_ln_g[j],
                            b_conf_ln_b[j], b_sc_dw[j]) @ b_w_out[j]
            if ctx_needed:
                mix_c = odd_mixer(hc @ b_w_in[j], b_conf_dw[j], b_conf_dw_b[j], b_conf_ln_g[j],
                                  b_conf_ln_b[j], b_sc_dw[j]) @ b_w_out[j]
        x = x + g1 * mix
        x = x + g2 * swiglu(modulate(rms_norm(x, norm2_g[i]), sh2, sc2), ffn_w1[i], ffn_w3[i], ffn_w2[i])
        if ctx_needed:
            ctx = ctx + cg1 * mix_c
            ctx = ctx + cg2 * swiglu(modulate(rms_norm(ctx, norm2_g[i]), csh2, csc2),
                                     ffn_w1[i], ffn_w3[i], ffn_w2[i])
    return x


DEPTH_2 = 1

N_MIXERS = 2
N_MOD = 6
NORM_EPS = 1e-6

NA_HEADS = 16
NA_HEAD_DIM = D_MODEL // NA_HEADS
NA_WIN_H = 8
NA_WIN_W = 16

HY_FILTER_WIDTH = 64
HY_EMB_DIM = 33
HY_BANDS = (HY_EMB_DIM - 1) // 2
HY_SHORT_WIDTH = 3
HY_DECAY_TARGET = 1e-2
HY_SHORT_DECAY_PCT = 0.3
HY_LONG_DECAY_PCT = 1.5

D_FF_2 = 2816
FFN_CONV_WIDTH = 3


def rms_norm_2(x, gain):
    xf = x.astype(jnp.float32)
    y = xf * lax.rsqrt(jnp.mean(xf * xf, axis=-1, keepdims=True) + NORM_EPS)
    return (y * gain.astype(jnp.float32)).astype(x.dtype)

def adaln(cond, w_mod, b_mod):
    return jnp.split(jax.nn.silu(cond) @ w_mod + b_mod, N_MOD, axis=-1)

def modulate_2(h, shift, scale):
    return h * (1.0 + scale) + shift

def dwconv_centred(x, w, b):
    k = w.shape[0]
    L = x.shape[1]
    pad = k // 2
    xp = jnp.pad(x, ((0, 0), (pad, k - 1 - pad), (0, 0)))
    out = xp[:, 0:L] * w[0]
    for i in range(1, k):
        out = out + xp[:, i:i + L] * w[i]
    return out + b

def split_heads(t):
    return t.reshape(t.shape[0], t.shape[1], NA_HEADS, NA_HEAD_DIM)

def neighbourhood_attention(q, k, v, k_ctx, v_ctx, rpb):
    B, L, H, Dh = q.shape
    rows = L // GRID_W
    kh = min(NA_WIN_H, rows)
    kw = NA_WIN_W
    scale = Dh ** -0.5
    cols = np.arange(GRID_W)
    col_idx = (np.clip(cols - kw // 2, 0, GRID_W - kw)[:, None] + np.arange(kw)[None, :]).astype(np.int32)
    dc_idx = (col_idx - cols[:, None] + (NA_WIN_W - 1)).astype(np.int32)
    qg = jnp.moveaxis(q.reshape(B, rows, GRID_W, H, Dh), 1, 0)
    kg = k.reshape(B, rows, GRID_W, H, Dh)
    vg = v.reshape(B, rows, GRID_W, H, Dh)

    def one_row(args):
        r, q_row = args
        r0 = jnp.clip(r - kh // 2, 0, rows - kh)
        k_win = lax.dynamic_slice_in_dim(kg, r0, kh, axis=1)[:, :, col_idx]
        v_win = lax.dynamic_slice_in_dim(vg, r0, kh, axis=1)[:, :, col_idx]
        dr_idx = r0 + jnp.arange(kh, dtype=jnp.int32) - r + (NA_WIN_H - 1)
        bias = rpb[:, dr_idx[:, None, None], dc_idx[None, :, :]]
        s_loc = jnp.einsum('bqhd,biqjhd->bhqij', q_row, k_win) * scale + jnp.transpose(bias, (0, 2, 1, 3))[None]
        s_ctx = jnp.einsum('bqhd,bkhd->bhqk', q_row, k_ctx) * scale
        s = jnp.concatenate([s_loc.reshape(B, H, GRID_W, kh * kw), s_ctx], axis=-1)
        p = jax.nn.softmax(s.astype(jnp.float32), axis=-1).astype(v.dtype)
        p_loc = p[..., :kh * kw].reshape(B, H, GRID_W, kh, kw)
        return (jnp.einsum('bhqij,biqjhd->bqhd', p_loc, v_win)
                + jnp.einsum('bhqk,bkhd->bqhd', p[..., kh * kw:], v_ctx))

    out = lax.map(one_row, (jnp.arange(rows, dtype=jnp.int32), qg))
    return jnp.moveaxis(out, 0, 1).reshape(B, L, H * Dh)

def context_attention_2(q, k, v):
    s = jnp.einsum('bqhd,bkhd->bhqk', q, k) * (q.shape[-1] ** -0.5)
    p = jax.nn.softmax(s.astype(jnp.float32), axis=-1).astype(v.dtype)
    o = jnp.einsum('bhqk,bkhd->bqhd', p, v)
    return o.reshape(o.shape[0], o.shape[1], -1)

def hyena_filters(L, w1, b1, w2, b2, w3, b3, w_out, sin_freq):
    f32 = jnp.float32
    t = jnp.linspace(0.0, 1.0, L, dtype=f32)[:, None]
    w = (2.0 * math.pi / L) * jnp.arange(L, dtype=f32)[:, None]
    bands = jnp.linspace(1e-4, HY_BANDS - 1, HY_BANDS, dtype=f32)[None, :]
    z = jnp.concatenate([t, jnp.cos(bands * w), -jnp.sin(bands * w)], axis=-1)
    freq = sin_freq.astype(f32)
    hdn = jnp.sin(freq * (z @ w1.astype(f32) + b1.astype(f32)))
    hdn = jnp.sin(freq * (hdn @ w2.astype(f32) + b2.astype(f32)))
    hdn = jnp.sin(freq * (hdn @ w3.astype(f32) + b3.astype(f32)))
    h = (hdn @ w_out.astype(f32)).reshape(L, 2, D_MODEL)
    deltas = jnp.abs(jnp.linspace(math.log(HY_DECAY_TARGET) / HY_SHORT_DECAY_PCT,
                                  math.log(HY_DECAY_TARGET) / HY_LONG_DECAY_PCT, D_MODEL, dtype=f32))
    h = h * jnp.exp(-t * deltas)[:, None, :]
    h = h * lax.rsqrt(jnp.sum(h * h, axis=(0, 1), keepdims=True) + NORM_EPS)
    return jnp.concatenate([h[:, 0], jnp.zeros((1, D_MODEL), f32), h[:0:-1, 1]], axis=0)

def hyena_mixer(h, w_in, b_in, short_w, short_b, f_w1, f_b1, f_w2, f_b2, f_w3, f_b3, f_wout, f_freq,
                d_bias, w_out, b_out):
    L = h.shape[1]
    u = dwconv_centred(h @ w_in + b_in, short_w, short_b)
    x0, x1, v = jnp.split(u, 3, axis=-1)
    filt = hyena_filters(L, f_w1, f_b1, f_w2, f_b2, f_w3, f_b3, f_wout, f_freq)
    z = (v * x1).astype(jnp.float32)
    zf = jnp.fft.rfft(z, n=2 * L, axis=1)
    ff = jnp.fft.rfft(filt, n=2 * L, axis=0)
    y = jnp.fft.irfft(zf * ff[None], n=2 * L, axis=1)[:, :L] + z * d_bias.astype(jnp.float32)
    return (x0 * y.astype(h.dtype)) @ w_out + b_out

def conv_ffn(h, w_up, conv_w, conv_b, w_down):
    a, g = jnp.split(h @ w_up, 2, axis=-1)
    return (a * jax.nn.gelu(dwconv_centred(g, conv_w, conv_b), approximate=False)) @ w_down

def second_inputs(seed: int = 0) -> dict:
    key = jax.random.key(seed)
    ks = iter(jax.random.split(key, 48))

    def nrm(shape, scale):
        return scale * jax.random.normal(next(ks), shape, jnp.float32)

    D = D_MODEL
    inp = {}
    inp['x'] = nrm((BATCH, SEQ, D), 1.0)
    inp['c'] = nrm((BATCH, D), 1.0)
    inp['ctx'] = nrm((BATCH, CTX_LEN, D), 1.0)
    inp['c_ctx'] = nrm((D,), 1.0)
    inp['l0_w_mod'] = nrm((D, N_MOD * D), D ** -0.5)
    inp['l0_b_mod'] = nrm((N_MOD * D,), 0.02)
    inp['l0_norm1'] = 1.0 + nrm((D,), 0.05)
    inp['l0_norm2'] = 1.0 + nrm((D,), 0.05)
    inp['l0_na_w_qkv'] = nrm((D, 3 * D), D ** -0.5)
    inp['l0_na_q_gain'] = 1.0 + nrm((NA_HEAD_DIM,), 0.05)
    inp['l0_na_k_gain'] = 1.0 + nrm((NA_HEAD_DIM,), 0.05)
    inp['l0_na_rpb'] = nrm((NA_HEADS, 2 * NA_WIN_H - 1, 2 * NA_WIN_W - 1), 0.1)
    inp['l0_na_w_o'] = nrm((D, D), D ** -0.5)
    inp['l0_ffn_w_up'] = nrm((D, 2 * D_FF_2), D ** -0.5)
    inp['l0_ffn_conv_w'] = nrm((FFN_CONV_WIDTH, D_FF_2), FFN_CONV_WIDTH ** -0.5)
    inp['l0_ffn_conv_b'] = nrm((D_FF_2,), 0.02)
    inp['l0_ffn_w_down'] = nrm((D_FF_2, D), D_FF_2 ** -0.5)
    inp['l1_w_mod'] = nrm((D, N_MOD * D), D ** -0.5)
    inp['l1_b_mod'] = nrm((N_MOD * D,), 0.02)
    inp['l1_norm1'] = 1.0 + nrm((D,), 0.05)
    inp['l1_norm2'] = 1.0 + nrm((D,), 0.05)
    inp['l1_hy_w_in'] = nrm((D, 3 * D), D ** -0.5)
    inp['l1_hy_b_in'] = nrm((3 * D,), 0.02)
    inp['l1_hy_short_w'] = nrm((HY_SHORT_WIDTH, 3 * D), HY_SHORT_WIDTH ** -0.5)
    inp['l1_hy_short_b'] = nrm((3 * D,), 0.02)
    inp['l1_hy_f_w1'] = nrm((HY_EMB_DIM, HY_FILTER_WIDTH), HY_EMB_DIM ** -0.5)
    inp['l1_hy_f_b1'] = nrm((HY_FILTER_WIDTH,), 0.1)
    inp['l1_hy_f_w2'] = nrm((HY_FILTER_WIDTH, HY_FILTER_WIDTH), HY_FILTER_WIDTH ** -0.5)
    inp['l1_hy_f_b2'] = nrm((HY_FILTER_WIDTH,), 0.1)
    inp['l1_hy_f_w3'] = nrm((HY_FILTER_WIDTH, HY_FILTER_WIDTH), HY_FILTER_WIDTH ** -0.5)
    inp['l1_hy_f_b3'] = nrm((HY_FILTER_WIDTH,), 0.1)
    inp['l1_hy_f_wout'] = nrm((HY_FILTER_WIDTH, 2 * D), HY_FILTER_WIDTH ** -0.5)
    inp['l1_hy_f_freq'] = 1.0 + nrm((HY_FILTER_WIDTH,), 0.05)
    inp['l1_hy_d_bias'] = nrm((D,), 1.0)
    inp['l1_hy_w_out'] = nrm((D, D), D ** -0.5)
    inp['l1_hy_b_out'] = nrm((D,), 0.02)
    inp['l1_ffn_w_up'] = nrm((D, 2 * D_FF_2), D ** -0.5)
    inp['l1_ffn_conv_w'] = nrm((FFN_CONV_WIDTH, D_FF_2), FFN_CONV_WIDTH ** -0.5)
    inp['l1_ffn_conv_b'] = nrm((D_FF_2,), 0.02)
    inp['l1_ffn_w_down'] = nrm((D_FF_2, D), D_FF_2 ** -0.5)
    return inp

def second_block(x, c, ctx, c_ctx,
              l0_w_mod, l0_b_mod, l0_norm1, l0_norm2, l0_na_w_qkv, l0_na_q_gain, l0_na_k_gain, l0_na_rpb,
              l0_na_w_o, l0_ffn_w_up, l0_ffn_conv_w, l0_ffn_conv_b, l0_ffn_w_down,
              l1_w_mod, l1_b_mod, l1_norm1, l1_norm2, l1_hy_w_in, l1_hy_b_in, l1_hy_short_w, l1_hy_short_b,
              l1_hy_f_w1, l1_hy_f_b1, l1_hy_f_w2, l1_hy_f_b2, l1_hy_f_w3, l1_hy_f_b3, l1_hy_f_wout, l1_hy_f_freq,
              l1_hy_d_bias, l1_hy_w_out, l1_hy_b_out, l1_ffn_w_up, l1_ffn_conv_w, l1_ffn_conv_b, l1_ffn_w_down):
    layers = [
        dict(w_mod=l0_w_mod, b_mod=l0_b_mod, norm1=l0_norm1, norm2=l0_norm2,
             mixer=(l0_na_w_qkv, l0_na_q_gain, l0_na_k_gain, l0_na_rpb, l0_na_w_o),
             ffn=(l0_ffn_w_up, l0_ffn_conv_w, l0_ffn_conv_b, l0_ffn_w_down)),
        dict(w_mod=l1_w_mod, b_mod=l1_b_mod, norm1=l1_norm1, norm2=l1_norm2,
             mixer=(l1_hy_w_in, l1_hy_b_in, l1_hy_short_w, l1_hy_short_b, l1_hy_f_w1, l1_hy_f_b1,
                    l1_hy_f_w2, l1_hy_f_b2, l1_hy_f_w3, l1_hy_f_b3, l1_hy_f_wout, l1_hy_f_freq,
                    l1_hy_d_bias, l1_hy_w_out, l1_hy_b_out),
             ffn=(l1_ffn_w_up, l1_ffn_conv_w, l1_ffn_conv_b, l1_ffn_w_down)),
    ]
    xc = ctx
    for i in range(DEPTH_2):
        p = layers[i]
        ctx_read_later = any(j % N_MIXERS == 0 for j in range(i + 1, DEPTH_2))
        sh1, sc1, g1, sh2, sc2, g2 = adaln(c[:, None, :], p['w_mod'], p['b_mod'])
        csh1, csc1, cg1, csh2, csc2, cg2 = adaln(c_ctx[None, None, :], p['w_mod'], p['b_mod'])
        h = modulate_2(rms_norm_2(x, p['norm1']), sh1, sc1)
        hc = modulate_2(rms_norm_2(xc, p['norm1']), csh1, csc1)
        if i % N_MIXERS == 0:
            w_qkv, q_gain, k_gain, rpb, w_o = p['mixer']
            w_q, w_k, w_v = jnp.split(w_qkv, 3, axis=1)
            q = rms_norm_2(split_heads(h @ w_q), q_gain)
            k = rms_norm_2(split_heads(h @ w_k), k_gain)
            v = split_heads(h @ w_v)
            kc = rms_norm_2(split_heads(hc @ w_k), k_gain)
            vc = split_heads(hc @ w_v)
            y = neighbourhood_attention(q, k, v, kc, vc, rpb) @ w_o
            if ctx_read_later:
                qc = rms_norm_2(split_heads(hc @ w_q), q_gain)
                yc = context_attention_2(qc, kc, vc) @ w_o
        else:
            y = hyena_mixer(h, *p['mixer'])
            if ctx_read_later:
                yc = hyena_mixer(hc, *p['mixer'])
        x = x + g1 * y
        x = x + g2 * conv_ffn(modulate_2(rms_norm_2(x, p['norm2']), sh2, sc2), *p['ffn'])
        if ctx_read_later:
            xc = xc + cg1 * yc
            xc = xc + cg2 * conv_ffn(modulate_2(rms_norm_2(xc, p['norm2']), csh2, csc2), *p['ffn'])
    return x


def setup_inputs(seed=0):
    out = dict(first_inputs(seed))
    for name, value in second_inputs(seed + 1).items():
        if name != "x":
            out[name + "_2"] = value
    return out


def reference(
    x, c, ctx, c_ctx, ada_w, ada_b, norm1_g, norm2_g, ffn_w1, ffn_w3, ffn_w2, a_w_in, a_q_ln_g,
    a_kv_ln_g, a_w_uq, a_w_uk, a_w_uv, a_q_norm_g, a_k_norm_g, a_w_out, b_w_in, b_conf_dw,
    b_conf_dw_b, b_conf_ln_g, b_conf_ln_b, b_sc_dw, b_w_out, c_2, ctx_2, c_ctx_2, l0_w_mod_2,
    l0_b_mod_2, l0_norm1_2, l0_norm2_2, l0_na_w_qkv_2, l0_na_q_gain_2, l0_na_k_gain_2,
    l0_na_rpb_2, l0_na_w_o_2, l0_ffn_w_up_2, l0_ffn_conv_w_2, l0_ffn_conv_b_2, l0_ffn_w_down_2,
    l1_w_mod_2, l1_b_mod_2, l1_norm1_2, l1_norm2_2, l1_hy_w_in_2, l1_hy_b_in_2, l1_hy_short_w_2,
    l1_hy_short_b_2, l1_hy_f_w1_2, l1_hy_f_b1_2, l1_hy_f_w2_2, l1_hy_f_b2_2, l1_hy_f_w3_2,
    l1_hy_f_b3_2, l1_hy_f_wout_2, l1_hy_f_freq_2, l1_hy_d_bias_2, l1_hy_w_out_2, l1_hy_b_out_2,
    l1_ffn_w_up_2, l1_ffn_conv_w_2, l1_ffn_conv_b_2, l1_ffn_w_down_2,
):
    x = first_block(
        x, c, ctx, c_ctx, ada_w, ada_b, norm1_g, norm2_g, ffn_w1, ffn_w3, ffn_w2, a_w_in,
        a_q_ln_g, a_kv_ln_g, a_w_uq, a_w_uk, a_w_uv, a_q_norm_g, a_k_norm_g, a_w_out, b_w_in,
        b_conf_dw, b_conf_dw_b, b_conf_ln_g, b_conf_ln_b, b_sc_dw, b_w_out,
    )
    return second_block(
        x, c_2, ctx_2, c_ctx_2, l0_w_mod_2, l0_b_mod_2, l0_norm1_2, l0_norm2_2, l0_na_w_qkv_2,
        l0_na_q_gain_2, l0_na_k_gain_2, l0_na_rpb_2, l0_na_w_o_2, l0_ffn_w_up_2,
        l0_ffn_conv_w_2, l0_ffn_conv_b_2, l0_ffn_w_down_2, l1_w_mod_2, l1_b_mod_2, l1_norm1_2,
        l1_norm2_2, l1_hy_w_in_2, l1_hy_b_in_2, l1_hy_short_w_2, l1_hy_short_b_2, l1_hy_f_w1_2,
        l1_hy_f_b1_2, l1_hy_f_w2_2, l1_hy_f_b2_2, l1_hy_f_w3_2, l1_hy_f_b3_2, l1_hy_f_wout_2,
        l1_hy_f_freq_2, l1_hy_d_bias_2, l1_hy_w_out_2, l1_hy_b_out_2, l1_ffn_w_up_2,
        l1_ffn_conv_w_2, l1_ffn_conv_b_2, l1_ffn_w_down_2,
    )


_drawn_inputs = setup_inputs


def setup_inputs(seed=0):
    import zlib

    import numpy as np

    out = dict(_drawn_inputs(seed))
    spreads = {}
    factors = {'ctx': 4.611,
     'a_q_ln_g': 8.0,
     'a_kv_ln_g': 8.0,
     'a_w_uq': 2.678,
     'a_w_uk': 2.957,
     'a_q_norm_g': 8.0,
     'a_k_norm_g': 8.0,
     'b_conf_dw_b': 8.0,
     'b_conf_ln_g': 7.388,
     'b_conf_ln_b': 8.0,
     'l0_norm1_2': 8.0,
     'l0_na_q_gain_2': 8.0,
     'l0_na_k_gain_2': 8.0,
     'l0_na_rpb_2': 8.0,
     'l0_ffn_conv_b_2': 31.669,
     'l0_norm2_2': 8.0}
    for name, (base, spread) in spreads.items():
        noise = np.random.default_rng([zlib.crc32(name.encode()), seed]).standard_normal(out[name].shape)
        drawn = base * np.exp(spread * noise) if base else spread * noise
        out[name] = jnp.asarray(drawn.astype(out[name].dtype))
    for name, factor in factors.items():
        out[name] = (out[name] * factor).astype(out[name].dtype)
    return out
```

```python
import math
from contextlib import ExitStack

import numpy as np

import concourse.bass as bass
from concourse import mybir

P = 128
D = 1024
KT = D // P
T = 256
F_FF = 2816
FT = F_FF // P
EPS = 1e-6
LAYERS = 3
MODS = 6 * KT

MLA_H, NOPE, ROPE_D, QK, VH = 8, 64, 32, 96, 64
QL_T, KVL_T, FN_T = 3, 2, 4
CONF_K, SC_K, CG = 31, 3, 4
NA_H, NA_D, GRID_W, WIN = 16, 64, 64, 16
ROWS = T // GRID_W
TOEP = 2 * GRID_W - 1
DRS = 2 * ROWS - 1
MASKED = -1e30

BLK = KT * P
RING = 6
AGRP = 4
LEAD = 4

W_IN0, N_IN0 = 0, 10
W_UQ, N_UQ, UQ_HEADS = 10, 3, 3
W_UK, N_UK, UK_HEADS = 13, 2, 4
W_UV = 15
W_OUT0 = 16
W_FF0 = 24
W_IN1, N_IN1 = 24 + 3 * FT, 20
W_OUT1 = W_IN1 + N_IN1
W_FF1 = W_OUT1 + KT
W_K2 = W_FF1 + 3 * FT
W_Q2 = W_K2 + KT
W_V2 = W_Q2 + KT
W_OUT2 = W_V2 + KT
W_FF2 = W_OUT2 + KT
N_W = W_FF2 + 3 * FT
N_A = LAYERS * MODS
assert N_W % RING == 0 and N_A % AGRP == 0 and FT % 2 == 0


def columns(sizes):
    out, at = {}, 0
    for name, n in sizes:
        out[name] = (at, at + n)
        at += n
    return out, at


PARAMS, N_PARAMS = columns([
    ("c", LAYERS * KT * 2), ("ada_b", LAYERS * MODS), ("norm1", LAYERS * KT), ("norm2", LAYERS * KT),
    ("q_ln", QL_T), ("kv_ln", KVL_T), ("q_norm", 1), ("k_norm", 1),
    ("conf_dw", CG * CONF_K), ("conf_b", CG), ("ln_g", CG), ("ln_b", CG), ("sc_dw", CG * SC_K),
    ("na_q", 1), ("na_k", 1), ("ff_conv", FT * 4)])
CONSTS, N_CONSTS = columns([
    ("ident", P), ("ones", P), ("ones64", P), ("swap", QK), ("place", QK), ("cos", T), ("sin", T),
    ("dft_c", 2 * P), ("dft_n", 2 * 2 * T), ("mask", GRID_W)])


def constant_table():
    t = np.zeros((P, N_CONSTS), np.float32)

    def put(name, a):
        c0, _ = CONSTS[name]
        t[:a.shape[0], c0:c0 + a.shape[1]] = a

    put("ident", np.eye(P))
    put("ones", np.ones((P, P)))
    half = np.arange(P) // NA_D
    put("ones64", (half[:, None] == half[None, :]).astype(np.float32))
    swap = np.zeros((QK, QK))
    h = ROPE_D // 2
    for i in range(h):
        swap[NOPE + h + i, NOPE + i] = -1.0
        swap[NOPE + i, NOPE + h + i] = 1.0
    put("swap", swap)
    place = np.zeros((P, QK))
    place[np.arange(ROPE_D), NOPE + np.arange(ROPE_D)] = 1.0
    put("place", place)
    per_axis = ROPE_D // 4
    inv = np.float32(10000.0) ** (-np.arange(per_axis, dtype=np.float32) / np.float32(per_axis))
    n = np.arange(T)
    row, col = (n // GRID_W).astype(np.float32), (n % GRID_W).astype(np.float32)
    ang = np.concatenate([row[:, None] * inv, col[:, None] * inv], axis=1).astype(np.float32)
    for name, f in (("cos", np.cos), ("sin", np.sin)):
        a = np.zeros((QK, T), np.float32)
        a[NOPE:] = np.concatenate([f(ang), f(ang)], axis=1).T
        put(name, a)
    c = np.arange(P)
    w = 2 * np.pi * np.outer(c, c) / P
    put("dft_c", np.concatenate([np.cos(w), np.sin(w)], axis=1))
    w = 2 * np.pi * (np.outer(n, n) % T) / T
    norm = 1.0 / math.sqrt(T * P)
    both = np.stack([np.cos(w) * norm, -np.sin(w) * norm])
    put("dft_n", both.reshape(2, 2, P, T).transpose(2, 0, 1, 3).reshape(P, 4 * T))
    q = np.arange(P) % GRID_W
    k = np.arange(GRID_W)
    first = np.clip(q - WIN // 2, 0, GRID_W - WIN)[:, None]
    put("mask", np.where((k >= first) & (k < first + WIN), 0.0, MASKED))
    return t


def program(nc, weights, ada, xt_in, ctx1_in, ctx2_in, params_in, consts_in, rpb_in, out_t, upto=9):
    fp, fr = mybir.dt.float32, mybir.dt.float32r
    ALU, ACT, AX = mybir.AluOpType, mybir.ActivationFunctionType, mybir.AxisListType
    MUL, ADD, SUB = ALU.mult, ALU.add, ALU.subtract

    ctx = ExitStack()
    with ctx:
        def sb(name, shape, dt=fp):
            return ctx.enter_context(nc.sbuf_tensor(name, shape, dt))

        def sem(name):
            return ctx.enter_context(nc.semaphore(name))

        w_raw = sb("w_raw", [P, RING, BLK])
        w_hi = sb("w_hi", [P, RING, BLK], fr)
        w_lo = sb("w_lo", [P, RING, BLK], fr)
        a_raw = sb("a_raw", [P, AGRP, BLK])
        xT = sb("xT", [P, KT, T])
        h_hi = sb("h_hi", [P, KT, 2 * T], fr)
        h_lo = sb("h_lo", [P, KT, 2 * T], fr)
        par = sb("par", [P, N_PARAMS])
        con = sb("con", [P, N_CONSTS])
        cs = sb("cs", [P, LAYERS, KT, 2])
        mods = sb("mods", [P, LAYERS, MODS, 2])
        gain = sb("gain", [P, KT])
        eps = sb("eps", [P, 1])
        zero_r = sb("zero_r", [P, P], fr)
        std = sb("std", [P, 2, 2 * T])
        rstd = std
        big = sb("big", [P, 24 * 256])
        ctxT = big[:, 0:2048].rearrange("p (k t) -> p k t", k=KT)
        sq = big[:, 2048:4096].rearrange("p (k t) -> p k t", k=KT)
        tmp = big[:, 4096:6144].rearrange("p (k t) -> p k t", k=KT)
        keysT = big[:, 0:4096].rearrange("p (h t) -> p h t", h=8)
        querT = big[:, 4096:6144].rearrange("p (h t) -> p h t", h=8)
        vals = sb("vals", [P, 4, D])
        work = sb("work", [P, 12 * 256])
        prob = work[:, 0:1024].rearrange("p (b t) -> p b t", b=2)
        probT = work[:, 1024:3072].rearrange("p (b k t) -> p b k t", b=2, k=4)
        nmax = sb("nmax", [P, 32])
        rsum = sb("rsum", [P, 32])
        rinv = sb("rinv", [P, 32])
        place_r = sb("place_r", [P, QK], fr)
        act_f = work[:, 0:512].rearrange("p (b t) -> p b t", b=2)
        gate_f = work[:, 512:1024].rearrange("p (b t) -> p b t", b=2)
        cv = work[:, 1024:2560].rearrange("p (b m t) -> p b m t", b=2, m=3)
        g_hi = sb("g_hi", [P, 2, T], fr)
        g_lo = sb("g_lo", [P, 2, T], fr)
        kr_hi, kr_lo = (g[:, :, :].rearrange("p b t -> p (b t)") for g in (g_hi, g_lo))
        bank = [ctx.enter_context(nc.psum_tensor(f"bank{i}", [P, 2 * T], fp)) for i in range(8)]

        def pc(name, j=0, n=1):
            c0, _ = PARAMS[name]
            return par[:, c0 + j:c0 + j + n]

        def cc(name, lo=0, hi=None):
            c0, c1 = CONSTS[name]
            return con[:, c0 + lo:(c1 if hi is None else c0 + hi)]

        ident, ones = cc("ident"), cc("ones")

        cq = work[:, 0:768].rearrange("p (k t) -> p k t", k=3)
        ckv = work[:, 768:1792].rearrange("p (k t) -> p k t", k=2)
        fu = vals[:, 0, :].rearrange("p (g t) -> p g t", g=4)
        kr = vals[:, 1, 0:512]
        f1 = big[:, 0:2048].rearrange("p (g u c) -> p g u c", g=4, u=2)
        usq = vals[:, 2:4, 0:512]
        unit = work[:, 0:1024].rearrange("p (b t) -> p b t", b=2)
        rot1 = work[:, 1024:1536]
        rot2 = work[:, 1536:2048]
        vals0 = vals[:, :, 512:1024]
        sgate = work[:, 0:512].rearrange("p (b t) -> p b t", b=2)
        confp = vals[:, 0:2, :].rearrange("p a b -> p (a b)")[:, 0:CG * 288].rearrange("p (g t) -> p g t", g=CG)
        cacc = vals[:, 2, :].rearrange("p (g t) -> p g t", g=CG)
        ccen = vals[:, 3, :].rearrange("p (g t) -> p g t", g=CG)
        csq = work[:, 512:1536].rearrange("p (g t) -> p g t", g=CG)
        scp = big[:, 2048:2048 + CG * 264].rearrange("p (g t) -> p g t", g=CG)
        sacc = big[:, 4096:4096 + CG * T].rearrange("p (g t) -> p g t", g=CG)
        bias = sb("bias", [P, 3, GRID_W, DRS])
        nsq = work[:, 0:1024].rearrange("p (b t) -> p b t", b=2)
        gpad = vals[:, 0, 0:2 * (T + 2)].rearrange("p (b t) -> p b t", b=2)
        taps = sb("taps", [P, 2, 4])

        s_par, s_con, s_x, s_ctx = sem("params_loaded"), sem("consts_loaded"), sem("x_loaded"), sem("ctx_loaded")
        w_loaded = [sem(f"w_loaded{i}") for i in range(RING)]
        a_loaded = [sem(f"a_loaded{i}") for i in range(AGRP)]
        hi_done, split_done, w_used = sem("w_hi_done"), sem("w_split_done"), sem("w_used")
        a_used = sem("ada_block_used")
        full = [sem(f"bank{i}_full") for i in range(8)]
        free = [sem(f"bank{i}_free") for i in range(8)]
        cs_ready, mod_ready, gain_ready = sem("cond_ready"), sem("mods_ready"), sem("gain_ready")
        const_ready, pads_ready = sem("const_ready"), sem("pads_ready")
        sq_ready, std_ready, rstd_ready = sem("norm_sq"), sem("norm_std"), sem("norm_rstd")
        tmp_ready, hhi_ready, hlo_ready = sem("norm_scaled"), sem("h_hi_ready"), sem("h_lo_ready")
        x_updated = sem("x_updated")
        lat_ready, lsq_ready, lstd_ready = sem("latents_ready"), sem("latent_sq"), sem("latent_std")
        lrstd_ready, ltmp_ready = sem("latent_rstd"), sem("latent_scaled")
        lhi_ready, llo_ready = sem("latent_hi"), sem("latent_lo")
        f1_ready, o_hi, o_lo = sem("dft1_ready"), sem("mix_hi"), sem("mix_lo")
        v_ready = sem("values_ready")
        usq_ready, unit_ready, ustd_ready, head_ready = sem("unit_sq"), sem("unit_gained"), sem("unit_std"), sem("head_ready")
        nmax_ready, exp_ready, prob_ready, pT_ready, pv_done = (
            sem("nmax_ready"), sem("exp_ready"), sem("prob_ready"), sem("probT_ready"), sem("pv_done"))
        sg_ready, conf_ready, cen_ready, csq_ready, cstd_ready = (
            sem("sigmoid_ready"), sem("conv_ready"), sem("centred"), sem("centred_sq"), sem("conf_std"))
        cn_ready, conf_out, scc_ready, sc_out = sem("conf_normed"), sem("conf_silu"), sem("scc_ready"), sem("short_out")
        b_loaded = [sem(f"bias_loaded{i}") for i in range(3)]
        bias_ready, bias_used = sem("bias_masked"), sem("bias_used")
        ff_act, ff_mul, ff_hi, ff_lo = sem("ff_activated"), sem("ff_product"), sem("ff_hi"), sem("ff_lo")
        ff_pad, ff_cv = sem("ff_padded"), sem("ff_convolved")
        dve_seq, act_seq = sem("dve_step"), sem("act_step")
        stored = sem("stored")

        tiles, last_taken, made_count, free_count = {}, [None] * 8, [0] * 8, [0] * 8

        def place_tile(name, b, taken=None, made=None):
            if made is None:
                made_count[b] += 1
                made = (full[b], made_count[b])
            if taken is None:
                free_count[b] += 1
                taken = (free[b], free_count[b])
            tiles[name] = (b, made, last_taken[b])
            last_taken[b] = taken

        def used(w):
            return (w_used, w + 1)

        for n in (0, 1):
            place_tile(("ms", n), 7, (std_ready, n + 1))
        for j in range(N_IN0):
            place_tile(("in0", j), j % 4, (lat_ready, j + 1), used(W_IN0 + j))
        place_tile("kvss", 4, (lstd_ready, 1))
        place_tile("qss", 5, (lstd_ready, 2))
        for g in range(FN_T):
            place_tile(("dft1", g), g, (f1_ready, g + 1))
        for g in range(FN_T):
            place_tile(("dft2", g), 4 + g % 2, (o_lo, g + 1))
        for t in range(4):
            place_tile(("v0", t), t, (v_ready, t + 1))
        for u in range(12):
            place_tile(("pj", u), u % 2, (unit_ready, u + 1))
            place_tile(("ss", u), 2 + u % 2, (ustd_ready, u + 1))
            place_tile(("rot", u), 4 + u % 2)

        def place_attention(name, heads, at0, o0):
            for i in range(2 * heads):
                place_tile((name, "sc", i), i % 2, (exp_ready, at0 + i + 1))
                place_tile((name, "tr", i), 2 + i % 2, (pT_ready, at0 + i + 1))
            for p in range(heads // 2):
                place_tile((name, "o", p), 4 + p % 2, (o_lo, o0 + p + 1))

        def place_ffn(layer):
            for j in range(KT):
                place_tile(("out", layer, j), j % 4, (x_updated, 2 * KT * layer + j + 1),
                           used((W_OUT0, W_OUT1, W_OUT2)[layer] + j))
            place_tile(("ms", (2, 4, 7)[layer]), 7, (std_ready, (2, 4, 7)[layer] + 1))
            for b in range(4):
                place_tile(("acc", layer, b), b, (x_updated, KT * (2 * layer + 1) + 2 * b + 2))
            for s in range(2):
                place_tile(("up", layer, s), 4 + s, (ff_mul, FT * (layer + 1) + s + 1), used(-1))

        place_attention("mla", MLA_H, 0, 4)
        place_ffn(0)
        place_tile(("ms", 3), 7, (std_ready, 4))
        for j in range(N_IN1):
            g = j // 2
            taken = ((sc_out, j - 15) if j >= 16 else (conf_ready, g + 1) if j % 2
                     else (sg_ready, g + 1) if j < 8 else (scc_ready, g - 3))
            place_tile(("in1", j), j % 4, taken, used(W_IN1 + j))
        for half in range(2):
            place_tile(("csum", half), 4 + half, (cen_ready, half + 1))
        for half in range(2):
            place_tile(("cvar", half), 4 + half, (cstd_ready, half + 1))
        place_ffn(1)
        for n in (5, 6):
            place_tile(("ms", n), 7, (std_ready, n + 1))
        for j in range(16):
            place_tile(("qk", j), j % 2, (unit_ready, 12 + j + 1), used(W_K2 + j))
            place_tile(("qkss", j), 2 + j % 2, (ustd_ready, 12 + j + 1))
        for half in range(2):
            for t in range(4):
                place_tile(("v2", half, t), t, (v_ready, 4 + 4 * half + t + 1),
                           used(W_V2 + 4 * half + 3) if t == 3 else None)
        place_attention("na", NA_H, 16, 16)
        place_ffn(2)

        def write_tile(pe, name):
            b, _, before = tiles[name]
            if before:
                pe.wait_ge(*before)
            return bank[b]

        def wait_tile(eng, name):
            b, made, _ = tiles[name]
            eng.wait_ge(*made)
            return bank[b]

        def full_of(name):
            return full[tiles[name][0]]

        def free_of(name):
            return free[tiles[name][0]]

        NORMS = [("c", 0, 1, 0, 0), ("x", T, 0, 0, 0), ("x", T, 0, 0, 1), ("x", T, 0, 1, 0),
                 ("x", T, 0, 1, 1), ("c", 0, 1, 2, 0), ("x", T, 0, 2, 0), ("x", T, 0, 2, 1)]
        UPDATES = [0, 0, 1, 2, 3, 4, 4, 5]
        MOD_GROUPS = [4, 4, 10, 16, 22, 28, 28, 34]

        def ada_in_loop(layer):
            return (12, 24, None)[layer]

        block = ctx.enter_context(nc.Block())

        @block.sync
        def _(sp):
            sp.dma_start(par[:], params_in).then_inc(s_par, 16)
            sp.dma_start(ctxT, ctx1_in).then_inc(s_ctx, 16)
            sp.dma_start(xT[:], xt_in).then_inc(s_x, 16)
            sp.dma_start(con[:], consts_in).then_inc(s_con, 16)
            for s in range(RING):
                sp.dma_start(w_raw[:, s, :], weights[s]).then_inc(w_loaded[s], 16)
            with sp.Fori(1, N_W // RING) as i:
                for s in range(RING):
                    sp.wait_ge(split_done, RING * i + (s + 1 - RING))
                    sp.dma_start(w_raw[:, s, :], weights[bass.ds(RING * i + s, 1), :, :].rearrange("o p n -> (o p) n"))\
                        .then_inc(w_loaded[s], 16)
            sp.wait_ge(x_updated, 6 * KT)
            sp.dma_start(out_t, xT[:]).then_inc(stored, 16)
            sp.wait_ge(stored, 16)

        @block.gpsimd
        def _(pool):
            nc.gpsimd.memset(eps[:], EPS).then_inc(const_ready, 1)
            nc.gpsimd.memset(zero_r[:].bitcast(fp), 0.0).then_inc(const_ready, 1)
            for s in range(AGRP):
                pool.dma_start(a_raw[:, s, :], ada[s]).then_inc(a_loaded[s], 16)
            with pool.Fori(1, N_A // AGRP) as i:
                for s in range(AGRP):
                    pool.wait_ge(a_used, AGRP * i + (s + 1 - AGRP))
                    pool.dma_start(a_raw[:, s, :], ada[bass.ds(AGRP * i + s, 1), :, :].rearrange("o p n -> (o p) n"))\
                        .then_inc(a_loaded[s], 16)

            def load_bias(h):
                if h >= 3:
                    pool.wait_ge(bias_used, h - 2)
                src = bass.AP(rpb_in.tensor, h * TOEP * DRS + (GRID_W - 1) * DRS,
                              [[1, 2], [-DRS, GRID_W], [1, GRID_W * DRS]])
                pool.dma_start(bias[:, h % 3, :, :].rearrange("p c d -> p (c d)"), src).then_inc(b_loaded[h % 3], 16)

            for h in range(2):
                load_bias(h)
            for h in range(NA_H):
                if h + 2 < NA_H:
                    load_bias(h + 2)
                pool.wait_ge(b_loaded[h % 3], 16 * (h // 3 + 1))
                nc.gpsimd.tensor_tensor(bias[:, h % 3, :, :], bias[:, h % 3, :, :],
                                        cc("mask").unsqueeze(2).broadcast_to([P, GRID_W, DRS]), ADD)\
                    .then_inc(bias_ready, 1)

        @block.scalar
        def _(act):
            hi_next = [0]
            steps = [0]

            def split_hi(w, s, turn):
                act.wait_ge(w_loaded[s], 16 * turn)
                if not isinstance(w, int) or w >= RING:
                    act.wait_ge(w_used, w - (RING - 1))
                nc.scalar.copy(w_hi[:, s, :], w_raw[:, s, :]).then_inc(hi_done, 1)

            def split_to(w):
                while hi_next[0] <= min(w, N_W - 1):
                    n = hi_next[0]
                    split_hi(n, n % RING, n // RING + 1)
                    hi_next[0] += 1

            def norm(n):
                src, c0, col, layer, which = NORMS[n]
                if n == 0:
                    act.wait_ge(s_ctx, 16)
                if n == 1:
                    act.wait_ge(s_x, 16)
                if n == 5:
                    act.wait_ge(s_ctx, 32)
                v = ctxT if src == "c" else xT
                for half in range(2):
                    k0 = half * 4
                    if src == "x" and UPDATES[n]:
                        act.wait_ge(x_updated, KT * (UPDATES[n] - 1) + k0 + 4)
                    nc.scalar.activation(sq[:, k0:k0 + 4, :], v[:, k0:k0 + 4, :], ACT.Square).then_inc(sq_ready, 1)
                b = wait_tile(act, ("ms", n))
                act.wait_ge(const_ready, 2)
                nc.scalar.activation(std[:, 0, 0:T], b[:, 0:T], ACT.Sqrt, bias=eps[:], scale=1.0 / D)\
                    .then_inc(std_ready, 1)
                for k in range(KT):
                    act.wait_ge(tmp_ready, KT * n + k + 1)
                    sh = mods[:, layer, 3 * KT * which + k, col:col + 1]
                    nc.scalar.activation(h_hi[:, k, c0:c0 + T], tmp[:, k, :], ACT.Identity, bias=sh)\
                        .then_inc(hhi_ready, 1)

            def attention(name, heads, at0, o0):
                def turned(i):
                    b = wait_tile(act, (name, "tr", i))
                    h = i // 2
                    if h >= 2:
                        act.wait_ge(pv_done, at0 // 2 + h - 1)
                    nc.scalar.copy(probT[:, h % 2, :, (i % 2) * P:(i % 2 + 1) * P],
                                   b[:, :].rearrange("p (k q) -> p k q", k=4)).then_inc(pT_ready, 1)

                def out_hi(p):
                    b = wait_tile(act, (name, "o", p))
                    nc.scalar.copy(h_hi[:, p, 0:T], b[:, 0:T]).then_inc(o_hi, 1)

                for i in range(2 * heads):
                    b = wait_tile(act, (name, "sc", i))
                    act.wait_ge(nmax_ready, at0 + i + 1)
                    nc.scalar.activation(prob[:, i % 2, :], b[:, :], ACT.Exp, bias=nmax[:, i:i + 1],
                                         accum_out=rsum[:, i:i + 1]).then_inc(exp_ready, 1)
                    if i:
                        turned(i - 1)
                    if i >= 5 and i % 4 == 1:
                        out_hi((i - 5) // 4)
                turned(2 * heads - 1)
                out_hi(heads // 2 - 1)

            def ffn(layer):
                w0, g0 = (W_FF0, W_FF1, W_FF2)[layer], FT * layer
                split_to(w0 + LEAD - 1)
                def turn(i, splits_on=True):
                    def hi(j, on=True):
                        if on:
                            split_hi(3 * 2 * i + (w0 + j), (w0 + j) % RING, i + ((w0 + j) // RING + 1))

                    def activate(s):
                        b = tiles[("up", layer, s)][0]
                        act.wait_ge(w_used, 6 * i + (w0 + 2 * s + 2))
                        if layer < 2:
                            nc.scalar.activation(act_f[:, s, :], bank[b][:, 0:T], ACT.Silu).then_inc(ff_act, 1)
                        else:
                            act.wait_ge(pads_ready, 1)
                            nc.scalar.copy(gpad[:, s, 1:T + 1], bank[b][:, T:2 * T]).then_inc(ff_pad, 1)

                    def gelu(s):
                        act.wait_ge(ff_cv, 6 * i + 3 * (s + 1))
                        nc.scalar.activation(act_f[:, s, :], cv[:, s, 2, :], ACT.Gelu, bias=taps[:, s, 3:4])\
                            .then_inc(ff_act, 1)

                    def high(s):
                        act.wait_ge(ff_mul, 2 * i + (g0 + s + 3))
                        nc.scalar.copy(g_hi[:, s, :], gate_f[:, s, :]).then_inc(ff_hi, 1)

                    hi(4)
                    hi(5)
                    activate(0)
                    hi(6, splits_on)
                    if layer == 2:
                        gelu(0)
                    hi(7, splits_on)
                    high(0)
                    activate(1)
                    hi(8, splits_on)
                    if layer == 2:
                        gelu(1)
                    hi(9, splits_on)
                    high(1)

                with act.Fori(0, FT // 2 - (layer == 2)) as i:
                    turn(i)
                if layer == 2:
                    turn(FT // 2 - 1, splits_on=False)
                hi_next[0] = w0 + 3 * FT + LEAD

            act.wait_ge(s_par, 16)
            nc.scalar.activation(cs[:].rearrange("p l k c -> p (l k c)"), pc("c", 0, LAYERS * KT * 2), ACT.Silu)\
                .then_inc(cs_ready, 1)
            act.wait_ge(s_con, 16)
            nc.scalar.copy(place_r[:], cc("place")).then_inc(cs_ready, 1)
            split_to(2)
            norm(0)
            norm(1)
            for j in range(N_IN0):
                split_to(W_IN0 + j + LEAD)
                b = wait_tile(act, ("in0", j))
                if j < 2:
                    dst, n = ckv[:, j, :], 2 * T
                elif j == 2:
                    dst, n = kr, 2 * T
                elif j < 6:
                    dst, n = cq[:, j - 3, :], T
                else:
                    dst, n = fu[:, j - 6, :], T
                nc.scalar.copy(dst, b[:, 0:n]).then_inc(lat_ready, 1)
            split_to(W_UV)
            lsq = sq[:, :, :].rearrange("p k t -> p (k t)")
            nc.scalar.activation(lsq[:, 0:1024], ckv.rearrange("p k t -> p (k t)"), ACT.Square).then_inc(lsq_ready, 1)
            nc.scalar.activation(lsq[:, 1024:1792], cq.rearrange("p k t -> p (k t)"), ACT.Square).then_inc(lsq_ready, 1)
            nc.scalar.copy(kr_hi, kr).then_inc(lhi_ready, 1)
            b = wait_tile(act, "kvss")
            nc.scalar.activation(std[:, 0, :], b[:, :], ACT.Sqrt, bias=eps[:], scale=1.0 / (KVL_T * P))\
                .then_inc(lstd_ready, 1)
            b = wait_tile(act, "qss")
            nc.scalar.activation(std[:, 1, 0:T], b[:, 0:T], ACT.Sqrt, bias=eps[:], scale=1.0 / (QL_T * P))\
                .then_inc(lstd_ready, 1)
            for k in range(KVL_T):
                act.wait_ge(ltmp_ready, k + 1)
                nc.scalar.copy(h_hi[:, 2 * k:2 * k + 2, T:2 * T],
                               tmp[:, 2 * k:2 * k + 2, :]).then_inc(lhi_ready, 1)
            for k in range(QL_T):
                act.wait_ge(ltmp_ready, KVL_T + k + 1)
                nc.scalar.copy(h_hi[:, 4 + k, T:2 * T], tmp[:, 4 + k, :]).then_inc(lhi_ready, 1)
            for g in range(FN_T):
                b = wait_tile(act, ("dft1", g))
                nc.scalar.copy(f1[:, g, :, :].rearrange("p u c -> p (u c)"), b[:, :]).then_inc(f1_ready, 1)
            for g in range(FN_T):
                b = wait_tile(act, ("dft2", g))
                nc.scalar.copy(h_hi[:, 4 + g, 0:T], b[:, 0:T]).then_inc(o_hi, 1)
            for t in range(4):
                b = wait_tile(act, ("v0", t))
                nc.scalar.copy(vals0[:, t, :], b[:, :]).then_inc(v_ready, 1)
            for u in range(13):
                if u < 12:
                    b = wait_tile(act, ("pj", u))
                    nc.scalar.activation(usq[0:QK, u % 2, :], b[0:QK, :], ACT.Square).then_inc(usq_ready, 1)
                if u:
                    b = wait_tile(act, ("ss", u - 1))
                    if u > 2:
                        act.wait_ge(head_ready, u - 2)
                    nc.scalar.activation(std[0:QK, (u - 1) % 2, :], b[0:QK, :], ACT.Sqrt, bias=eps[0:QK, :],
                                         scale=1.0 / QK).then_inc(ustd_ready, 1)
            split_to(W_OUT0 + LEAD - 1)
            attention("mla", MLA_H, 0, 4)
            act.dma_start(ctxT, ctx2_in).then_inc(s_ctx, 16)
            split_to(W_FF0 + LEAD - 1)
            norm(2)
            ffn(0)
            norm(3)
            for j in range(N_IN1):
                split_to(W_IN1 + j + LEAD)
                if j < 8 and j % 2 == 0:
                    b = wait_tile(act, ("in1", j))
                    if j >= 4:
                        act.wait_ge(conf_ready, j // 2 - 1)
                    nc.scalar.activation(sgate[:, j // 2 % 2, :], b[:, 0:T], ACT.Sigmoid).then_inc(sg_ready, 1)
                elif 8 <= j < 16 and j % 2 == 0:
                    b = wait_tile(act, ("in1", j))
                    g = (j - 8) // 2
                    act.wait_ge(conf_ready, 4 if g < 2 else 4 + g - 1)
                    nc.scalar.copy(sgate[:, g % 2, :], b[:, 0:T]).then_inc(scc_ready, 1)
                elif j >= 16:
                    g = j - 16
                    act.wait_ge(sc_out, g + 1)
                    nc.scalar.copy(h_hi[:, 4 + g, 0:T], sacc[:, g, :]).then_inc(o_hi, 1)
            split_to(W_OUT1 + LEAD)
            for half in range(2):
                g = 2 * half
                act.wait_ge(cen_ready, half + 1)
                nc.scalar.activation(csq[:, g:g + 2, :], ccen[:, g:g + 2, :], ACT.Square).then_inc(csq_ready, 1)
            for half in range(2):
                b = wait_tile(act, ("cvar", half))
                nc.scalar.activation(std[:, half, :], b[:, :], ACT.Sqrt, bias=eps[:], scale=1.0 / P)\
                    .then_inc(cstd_ready, 1)
            for g in range(CG):
                act.wait_ge(cn_ready, g // 2 + 1)
                nc.scalar.activation(cacc[:, g, :], ccen[:, g, :], ACT.Silu, bias=pc("ln_b", g), scale=pc("ln_g", g))\
                    .then_inc(conf_out, 1)
            for g in range(CG):
                act.wait_ge(conf_out, g + 1)
                nc.scalar.copy(h_hi[:, g, 0:T], cacc[:, g, :]).then_inc(o_hi, 1)
            split_to(W_FF1 + LEAD - 1)
            norm(4)
            ffn(1)
            norm(5)
            norm(6)
            for j in range(17):
                if j < 16:
                    split_to(W_K2 + j + LEAD)
                    b = wait_tile(act, ("qk", j))
                    n = 2 * T if j < 8 else T
                    nc.scalar.activation(nsq[:, j % 2, 0:n], b[:, 0:n], ACT.Square).then_inc(usq_ready, 1)
                if j:
                    b = wait_tile(act, ("qkss", j - 1))
                    n = 2 * T if j - 1 < 8 else T
                    if j > 2:
                        act.wait_ge(head_ready, 12 + j - 2)
                    nc.scalar.activation(std[:, (j - 1) % 2, 0:n], b[:, 0:n], ACT.Sqrt, bias=eps[:],
                                         scale=1.0 / NA_D).then_inc(ustd_ready, 1)
            for half in range(2):
                split_to(W_V2 + 4 * half + 3 + LEAD - 1)
                for t in range(4):
                    b = wait_tile(act, ("v2", half, t))
                    nc.scalar.copy(vals[:, t, half * 512:(half + 1) * 512], b[:, :]).then_inc(v_ready, 1)
            split_to(W_OUT2 + LEAD - 1)
            attention("na", NA_H, 16, 16)
            split_to(W_FF2 + LEAD - 1)
            norm(7)
            ffn(2)

        @block.vector
        def _(dve):
            lo_next = [0]
            seq = [0]
            heads_made = [0]
            ada_made = [0]

            def step(ins):
                seq[0] += 1
                ins.then_inc(dve_seq, 1)
                dve.wait_ge(dve_seq, seq[0])

            def split_lo(w, s):
                dve.wait_ge(hi_done, w + 1)
                nc.vector.tensor_tensor(w_lo[:, s, :], w_raw[:, s, :], w_hi[:, s, :].bitcast(fp), SUB)\
                    .then_inc(split_done, 1)

            def split_to(w):
                while lo_next[0] <= min(w, N_W - 1):
                    n = lo_next[0]
                    split_lo(n, n % RING)
                    lo_next[0] += 1

            def ada_take(g, layer, first):
                dve.wait_ge(a_used, AGRP * (g + 1))
                at = PARAMS["ada_b"][0]
                mflat = mods[:].rearrange("p l m c -> p (l m) c")
                if isinstance(g, int):
                    dst, b = mflat[:, AGRP * g:AGRP * (g + 1), :], par[:, at + AGRP * g:at + AGRP * (g + 1)]
                else:
                    dst, b = mflat[:, bass.ds(AGRP * g, AGRP), :], par[:, bass.ds(AGRP * g + at, AGRP)]
                nc.vector.tensor_tensor(dst, bank[6][:, 0:2 * AGRP].rearrange("p (m c) -> p m c", c=2),
                                        b.unsqueeze(2).broadcast_to([P, AGRP, 2]), ADD).then_inc(mod_ready, 1)

            def norm(n, splits=()):
                src, c0, col, layer, which = NORMS[n]
                v = ctxT if src == "c" else xT
                m0 = 3 * KT * which
                dve.wait_ge(mod_ready, MOD_GROUPS[n])
                step(nc.vector.scalar_tensor_tensor(
                    out=gain[:], in0=mods[:, layer, m0 + KT:m0 + 2 * KT, col], scalar=1.0,
                    in1=pc("norm2" if which else "norm1", KT * layer, KT), op0=ADD, op1=MUL))
                if n == 0:
                    dve.wait_ge(s_ctx, 16)
                if n == 1:
                    dve.wait_ge(s_x, 16)
                dve.wait_ge(std_ready, n + 1)
                step(nc.vector.reciprocal(rstd[:, 0, 0:T], std[:, 0, 0:T]))
                for k in range(KT):
                    nc.vector.scalar_tensor_tensor(out=tmp[:, k, :], in0=v[:, k, :], scalar=gain[:, k:k + 1],
                                                   in1=rstd[:, 0, 0:T], op0=MUL, op1=MUL).then_inc(tmp_ready, 1)
                for k in range(KT):
                    dve.wait_ge(hhi_ready, KT * n + k + 1)
                    nc.vector.scalar_tensor_tensor(
                        out=h_lo[:, k, c0:c0 + T], in0=tmp[:, k, :], scalar=mods[:, layer, m0 + k, col:col + 1],
                        in1=h_hi[:, k, c0:c0 + T].bitcast(fp), op0=ADD, op1=SUB).then_inc(hlo_ready, 1)

            def attention(name, heads, at0, o0):
                def maximum(i):
                    b = wait_tile(dve, (name, "sc", i))
                    if name == "na":
                        h, t = i // 2, i % 2
                        if t == 0:
                            dve.wait_ge(bias_ready, h + 1)
                        m0 = 3 + 2 * t
                        ins = nc.vector.tensor_tensor(
                            b[:, T:2 * T].rearrange("p (r c) -> p r c", r=ROWS),
                            b[:, T:2 * T].rearrange("p (r c) -> p r c", r=ROWS),
                            bias[:, h % 3, :, m0 - ROWS + 1:m0 + 1][:, :, ::-1].rearrange("p c r -> p r c"), ADD)
                        step(ins)
                        if t == 1:
                            dve.sem_inc(bias_used, 1)
                    nc.vector.tensor_reduce(nmax[:, i:i + 1], b[:, :], AX.X, ALU.max, negate=True)\
                        .then_inc(nmax_ready, 1)

                def out_lo(p):
                    b = wait_tile(dve, (name, "o", p))
                    dve.wait_ge(o_hi, o0 + p + 1)
                    nc.vector.tensor_tensor(h_lo[:, p, 0:T], b[:, 0:T], h_hi[:, p, 0:T].bitcast(fp), SUB)\
                        .then_inc(o_lo, 1)

                maximum(0)
                for i in range(2 * heads):
                    if i + 1 < 2 * heads:
                        maximum(i + 1)
                    dve.wait_ge(exp_ready, at0 + i + 1)
                    step(nc.vector.reciprocal(rinv[:, i:i + 1], rsum[:, i:i + 1]))
                    nc.vector.tensor_scalar(prob[:, i % 2, :], prob[:, i % 2, :], rinv[:, i:i + 1], None, MUL)\
                        .then_inc(prob_ready, 1)
                    if i >= 5 and i % 4 == 1:
                        out_lo((i - 5) // 4)
                out_lo(heads // 2 - 1)

            def project_out(layer, w0):
                dve.wait_ge(mod_ready, 12 * layer + 6)
                for j in range(KT):
                    split_to(w0 + j + LEAD)
                    b = wait_tile(dve, ("out", layer, j))
                    nc.vector.scalar_tensor_tensor(out=xT[:, j, :], in0=b[:, 0:T],
                                                   scalar=mods[:, layer, 2 * KT + j, 0:1], in1=xT[:, j, :],
                                                   op0=MUL, op1=ADD).then_inc(x_updated, 1)

            def ffn(layer):
                w0, g0 = (W_FF0, W_FF1, W_FF2)[layer], FT * layer
                split_to(w0 + LEAD - 1)
                def turn(i, splits_on=True):
                    def lo(j, on=True):
                        if on:
                            split_lo(3 * 2 * i + (w0 + j), (w0 + j) % RING)

                    def convolve(s):
                        at = PARAMS["ff_conv"][0]
                        nc.vector.tensor_copy(taps[:, s, :], par[:, bass.ds(8 * i + (at + 4 * s), 4)])\
                            .then_inc(dve_seq, 1)
                        dve.wait_ge(dve_seq, 2 * i + (seq[0] + s + 1))
                        dve.wait_ge(ff_pad, 2 * i + (s + 1))
                        nc.vector.tensor_scalar(cv[:, s, 0, :], gpad[:, s, 0:T], taps[:, s, 0:1], None, MUL)\
                            .then_inc(ff_cv, 1)
                        for m in (1, 2):
                            dve.wait_ge(ff_cv, 6 * i + (3 * s + m))
                            nc.vector.scalar_tensor_tensor(out=cv[:, s, m, :], in0=gpad[:, s, m:m + T],
                                                           scalar=taps[:, s, m:m + 1], in1=cv[:, s, m - 1, :],
                                                           op0=MUL, op1=ADD).then_inc(ff_cv, 1)

                    def product(s):
                        b = tiles[("up", layer, s)][0]
                        half = T if layer < 2 else 0
                        dve.wait_ge(ff_act, 2 * i + (g0 + s + 1))
                        nc.vector.tensor_tensor(gate_f[:, s, :], act_f[:, s, :], bank[b][:, half:half + T], MUL)\
                            .then_inc(ff_mul, 1)

                    def low(s):
                        dve.wait_ge(ff_hi, 2 * i + (g0 + s + 1))
                        nc.vector.tensor_tensor(g_lo[:, s, :], gate_f[:, s, :], g_hi[:, s, :].bitcast(fp), SUB)\
                            .then_inc(ff_lo, 1)

                    lo(4)
                    lo(5)
                    if layer == 2:
                        convolve(0)
                    lo(6, splits_on)
                    product(0)
                    lo(7, splits_on)
                    low(0)
                    if layer == 2:
                        convolve(1)
                    lo(8, splits_on)
                    product(1)
                    lo(9, splits_on)
                    low(1)
                    if layer < 2:
                        ada_take(i + ada_in_loop(layer), None, None)

                with dve.Fori(0, FT // 2 - (layer == 2)) as i:
                    turn(i)
                if layer == 2:
                    turn(FT // 2 - 1, splits_on=False)
                if layer == 2:
                    seq[0] += FT
                lo_next[0] = w0 + 3 * FT + LEAD
                dve.wait_ge(mod_ready, 12 * (layer + 1))
                for b4 in range(4):
                    b = wait_tile(dve, ("acc", layer, b4))
                    for e in range(2):
                        j = 2 * b4 + e
                        nc.vector.scalar_tensor_tensor(out=xT[:, j, :], in0=b[:, e * T:(e + 1) * T],
                                                       scalar=mods[:, layer, 5 * KT + j, 0:1], in1=xT[:, j, :],
                                                       op0=MUL, op1=ADD).then_inc(x_updated, 1)

            dve.sem_inc(ff_mul, 2)
            dve.wait_ge(s_par, 16)
            for g in range(4):
                ada_take(g, 0, 0)
            split_to(2)
            norm(0)
            norm(1)
            for j in range(N_IN0):
                split_to(W_IN0 + j + LEAD)
                if j < 8:
                    ada_take(4 + j, 0, 0)
            split_to(W_UV)
            lrs = rstd
            dve.wait_ge(lat_ready, 3)
            dve.wait_ge(lhi_ready, 1)
            nc.vector.tensor_tensor(kr_lo, kr, kr_hi.bitcast(fp), SUB).then_inc(llo_ready, 1)
            dve.wait_ge(lstd_ready, 1)
            step(nc.vector.reciprocal(lrs[:, 0, :], std[:, 0, :]))
            dve.wait_ge(lstd_ready, 2)
            step(nc.vector.reciprocal(lrs[:, 1, 0:T], std[:, 1, 0:T]))
            for k in range(KVL_T):
                nc.vector.scalar_tensor_tensor(
                    out=tmp[:, 2 * k:2 * k + 2, :].rearrange("p a t -> p (a t)"), in0=ckv[:, k, :],
                    scalar=pc("kv_ln", k), in1=lrs[:, 0, :], op0=MUL, op1=MUL).then_inc(ltmp_ready, 1)
            for k in range(QL_T):
                nc.vector.scalar_tensor_tensor(out=tmp[:, 4 + k, :], in0=cq[:, k, :], scalar=pc("q_ln", k),
                                               in1=lrs[:, 1, 0:T], op0=MUL, op1=MUL).then_inc(ltmp_ready, 1)
            for k in range(KVL_T):
                dve.wait_ge(lhi_ready, k + 2)
                nc.vector.tensor_tensor(h_lo[:, 2 * k:2 * k + 2, T:2 * T], tmp[:, 2 * k:2 * k + 2, :],
                                        h_hi[:, 2 * k:2 * k + 2, T:2 * T].bitcast(fp), SUB).then_inc(llo_ready, 1)
            for k in range(QL_T):
                dve.wait_ge(lhi_ready, KVL_T + k + 2)
                nc.vector.tensor_tensor(h_lo[:, 4 + k, T:2 * T], tmp[:, 4 + k, :],
                                        h_hi[:, 4 + k, T:2 * T].bitcast(fp), SUB).then_inc(llo_ready, 1)
            for g in range(FN_T):
                b = wait_tile(dve, ("dft2", g))
                dve.wait_ge(o_hi, g + 1)
                nc.vector.tensor_tensor(h_lo[:, 4 + g, 0:T], b[:, 0:T], h_hi[:, 4 + g, 0:T].bitcast(fp), SUB)\
                    .then_inc(o_lo, 1)
            scale = QK ** -0.5
            for u in range(12):
                b = wait_tile(dve, ("pj", u))
                dve.wait_ge(usq_ready, u + 1)
                un = unit[0:QK, u % 2, :]
                gp = pc("q_norm" if u < 4 else "k_norm")[0:QK, :]
                nc.vector.tensor_scalar(un, b[0:QK, :], gp, None, MUL).then_inc(unit_ready, 1)
                dve.wait_ge(unit_ready, u + 1)
                b = wait_tile(dve, ("rot", u))
                for c0 in ((0, T) if u < 4 else (T,)):
                    part = unit[NOPE:QK, u % 2, c0:c0 + T]
                    nc.vector.tensor_tensor(rot1[NOPE:QK, c0:c0 + T], part, cc("cos")[NOPE:QK, :], MUL)
                    step(nc.vector.tensor_tensor(rot2[NOPE:QK, c0:c0 + T], b[NOPE:QK, c0:c0 + T],
                                                 cc("sin")[NOPE:QK, :], MUL))
                    step(nc.vector.tensor_tensor(part, rot1[NOPE:QK, c0:c0 + T], rot2[NOPE:QK, c0:c0 + T], ADD))
                dve.sem_inc(free_of(("rot", u)), 1)
                dve.wait_ge(ustd_ready, u + 1)
                step(nc.vector.reciprocal(rstd[0:QK, u % 2, :], std[0:QK, u % 2, :]))
                if u < 4:
                    nc.vector.scalar_tensor_tensor(
                        out=querT[0:QK, 2 * u:2 * u + 2, :].rearrange("p a t -> p (a t)"), in0=un, scalar=scale,
                        in1=rstd[0:QK, u % 2, :], op0=MUL, op1=MUL).then_inc(head_ready, 1)
                else:
                    nc.vector.tensor_tensor(keysT[0:QK, u - 4, :], un, rstd[0:QK, u % 2, :], MUL)\
                        .then_inc(head_ready, 1)
            split_to(W_OUT0 + LEAD - 1)
            attention("mla", MLA_H, 0, 4)
            project_out(0, W_OUT0)
            norm(2)
            ffn(0)
            norm(3)
            tap_list = [(g, k) for g in range(CG) for k in range(CONF_K)]
            taps_done = [0]

            def conv_taps(n):
                for g, k in tap_list[taps_done[0]:taps_done[0] + n]:
                    src = confp[:, g, 1 + k:1 + k + T]
                    wk = pc("conf_dw", CONF_K * g + k)
                    if k == 0:
                        ins = nc.vector.tensor_scalar(cacc[:, g, :], src, wk, pc("conf_b", g), MUL, ADD)
                    else:
                        ins = nc.vector.scalar_tensor_tensor(out=cacc[:, g, :], in0=src, scalar=wk,
                                                             in1=cacc[:, g, :], op0=MUL, op1=ADD)
                    step(ins)
                taps_done[0] = min(len(tap_list), taps_done[0] + n)

            step(nc.vector.memset(confp, 0.0))
            step(nc.vector.memset(scp, 0.0))
            for j in range(N_IN1):
                split_to(W_IN1 + j + LEAD)
                g = j // 2
                if j < 8 and j % 2:
                    b = wait_tile(dve, ("in1", j))
                    dve.wait_ge(sg_ready, g + 1)
                    nc.vector.tensor_tensor(confp[:, g, 16:16 + T], b[:, 0:T], sgate[:, g % 2, :], MUL)\
                        .then_inc(conf_ready, 1)
                    dve.wait_ge(conf_ready, g + 1)
                elif 8 <= j < 16 and j % 2:
                    g -= 4
                    b = wait_tile(dve, ("in1", j))
                    dve.wait_ge(scc_ready, g + 1)
                    nc.vector.tensor_tensor(scp[:, g, 1:1 + T], b[:, 0:T], sgate[:, g % 2, :], MUL)\
                        .then_inc(conf_ready, 1)
                    dve.wait_ge(conf_ready, 4 + g + 1)
                    for k in range(SC_K):
                        src = scp[:, g, k:k + T]
                        wk = pc("sc_dw", SC_K * g + k)
                        if k == 0:
                            step(nc.vector.tensor_scalar(sacc[:, g, :], src, wk, None, MUL))
                        else:
                            step(nc.vector.scalar_tensor_tensor(out=sacc[:, g, :], in0=src, scalar=wk,
                                                                in1=sacc[:, g, :], op0=MUL, op1=ADD))
                elif j >= 16:
                    g = j - 16
                    b = wait_tile(dve, ("in1", j))
                    nc.vector.tensor_tensor(sacc[:, g, :], b[:, 0:T], sacc[:, g, :], MUL).then_inc(sc_out, 1)
                if 2 <= j:
                    conv_taps(min(7, CONF_K * min(CG, (j + 1) // 2) - taps_done[0]))
            conv_taps(len(tap_list) - taps_done[0])
            dve.sem_inc(conf_ready, 1)
            split_to(W_OUT1 + LEAD)
            for g in range(CG):
                dve.wait_ge(o_hi, 8 + g + 1)
                nc.vector.tensor_tensor(h_lo[:, 4 + g, 0:T], sacc[:, g, :], h_hi[:, 4 + g, 0:T].bitcast(fp), SUB)\
                    .then_inc(o_lo, 1)
            for half in range(2):
                b = wait_tile(dve, ("csum", half))
                g = 2 * half
                nc.vector.scalar_tensor_tensor(
                    out=ccen[:, g:g + 2, :].rearrange("p g t -> p (g t)"), in0=b[:, :], scalar=-1.0 / P,
                    in1=cacc[:, g:g + 2, :].rearrange("p g t -> p (g t)"), op0=MUL, op1=ADD).then_inc(cen_ready, 1)
            for half in range(2):
                g = 2 * half
                dve.wait_ge(cstd_ready, half + 1)
                step(nc.vector.reciprocal(rstd[:, half, :], std[:, half, :]))
                cg = ccen[:, g:g + 2, :].rearrange("p g t -> p (g t)")
                nc.vector.tensor_tensor(cg, cg, rstd[:, half, :], MUL).then_inc(cn_ready, 1)
            for g in range(CG):
                dve.wait_ge(o_hi, 12 + g + 1)
                nc.vector.tensor_tensor(h_lo[:, g, 0:T], cacc[:, g, :], h_hi[:, g, 0:T].bitcast(fp), SUB)\
                    .then_inc(o_lo, 1)
            ada_take(23, 0, 0)
            project_out(1, W_OUT1)
            norm(4)
            ffn(1)
            norm(5)
            norm(6)
            for j in range(17):
                if j < 16:
                    split_to(W_K2 + j + LEAD)
                    b = wait_tile(dve, ("qk", j))
                    n = 2 * T if j < 8 else T
                    dst = keysT[:, j, :] if j < 8 else querT[:, j - 8, :]
                    dve.wait_ge(usq_ready, 12 + j + 1)
                    nc.vector.tensor_scalar(dst, b[:, 0:n], pc("na_k" if j < 8 else "na_q"), None, MUL)\
                        .then_inc(unit_ready, 1)
                    dve.wait_ge(unit_ready, 12 + j + 1)
                if j:
                    i = j - 1
                    n = 2 * T if i < 8 else T
                    dst = keysT[:, i, :] if i < 8 else querT[:, i - 8, :]
                    dve.wait_ge(ustd_ready, 12 + i + 1)
                    step(nc.vector.reciprocal(rstd[:, i % 2, 0:n], std[:, i % 2, 0:n]))
                    nc.vector.scalar_tensor_tensor(out=dst, in0=dst, scalar=1.0 if i < 8 else NA_D ** -0.5,
                                                   in1=rstd[:, i % 2, 0:n], op0=MUL, op1=MUL).then_inc(head_ready, 1)
            for half in range(2):
                split_to(W_V2 + 4 * half + 3 + LEAD - 1)
            ada_take(35, 0, 0)
            split_to(W_OUT2 + LEAD - 1)
            attention("na", NA_H, 16, 16)
            project_out(2, W_OUT2)
            nc.vector.memset(gpad, 0.0).then_inc(pads_ready, 1)
            norm(7)
            ffn(2)

        @block.tensor
        def _(pe):
            def split3(out, a_hi, a_lo, b_hi, b_lo, start, stop):
                nc.tensor.matmul(out, a_hi, b_hi, start=start, stop=False)
                nc.tensor.matmul(out, a_hi, b_lo, start=False, stop=False)
                return nc.tensor.matmul(out, a_lo, b_hi, start=False, stop=stop)

            def wtile(w, c0, n):
                return w_hi[:, w % RING, c0:c0 + n], w_lo[:, w % RING, c0:c0 + n]

            def split_ready(w):
                pe.wait_ge(split_done, w + 1)

            def ada_group(g):
                static = isinstance(g, int)
                if not static or g:
                    pe.wait_ge(mod_ready, g)
                for s in range(AGRP):
                    pe.wait_ge(a_loaded[s], 16 * g + 16)
                    layer = g // 12 if static else None
                    for k in range(KT):
                        ins = nc.tensor.matmul(bank[6][:, 2 * s:2 * s + 2], a_raw[:, s, k * P:(k + 1) * P],
                                               cs[:, ada_layer[0], k, :], start=(k == 0), stop=(k == KT - 1))
                    ins.then_inc(a_used, 1)

            ada_layer = [0]

            def norm(n):
                b = write_tile(pe, ("ms", n))
                for k in range(KT):
                    if k % 4 == 0:
                        pe.wait_ge(sq_ready, 2 * n + k // 4 + 1)
                    ins = nc.tensor.matmul(b[:, 0:T], ones, sq[:, k, :], start=(k == 0), stop=(k == KT - 1))
                ins.then_inc(full_of(("ms", n)), 1)

            def project(name, w, rhs, n):
                b = write_tile(pe, name)
                split_ready(w)
                for k in range(KT):
                    a = wtile(w, k * P, P)
                    ins = split3(b[:, 0:n], a[0], a[1], rhs(h_hi, k), rhs(h_lo, k), k == 0, k == KT - 1)
                ins.then_inc(w_used, 1)

            def both(h, k):
                return h[:, k, :]

            def xs(h, k):
                return h[:, k, T:2 * T]

            def mixed(h, k):
                return h[:, k, 0:T]

            def attention(name, heads, at0, ready0, rows, values):
                def scores(i):
                    h, t = i // 2, i % 2
                    b = write_tile(pe, (name, "sc", i))
                    q, k = rows(h)
                    nc.tensor.matmul(b[:, :], q[:, t * P:(t + 1) * P], k, start=True, stop=True)\
                        .then_inc(full_of((name, "sc", i)), 1)

                def turn(i):
                    b = write_tile(pe, (name, "tr", i))
                    pe.wait_ge(prob_ready, at0 + i + 1)
                    for kt in range(4):
                        ins = nc.tensor.transpose(b[:, kt * P:(kt + 1) * P], prob[:, i % 2, kt * P:(kt + 1) * P], ident)
                    ins.then_inc(full_of((name, "tr", i)), 1)

                def pv(h):
                    p, e = h // 2, h % 2
                    pe.wait_ge(pT_ready, at0 + 2 * h + 2)
                    b = write_tile(pe, (name, "o", p)) if e == 0 else bank[tiles[(name, "o", p)][0]]
                    for kt in range(4):
                        ins = nc.tensor.matmul(b[e * VH:(e + 1) * VH, 0:T], values(h, kt), probT[:, h % 2, kt, :],
                                               start=(kt == 0), stop=(kt == 3))
                    ins.then_inc(pv_done, 1)
                    if e:
                        pe.wait_ge(pv_done, at0 // 2 + h + 1)
                        pe.sem_inc(full_of((name, "o", p)), 1)

                scores(0)
                for i in range(2 * heads):
                    if i + 1 < 2 * heads:
                        scores(i + 1)
                    turn(i)
                    if i >= 2 and i % 2 == 0:
                        pv(i // 2 - 1)
                pv(heads - 1)

            def project_out(layer, w0, o_total):
                for j in range(KT):
                    if j == 0:
                        pe.wait_ge(o_lo, o_total)
                    project(("out", layer, j), w0 + j, mixed, T)

            def ffn(layer):
                w0, g0 = (W_FF0, W_FF1, W_FF2)[layer], FT * layer
                if layer == 0:
                    pe.wait_ge(const_ready, 2)
                for b4 in range(4):
                    b = write_tile(pe, ("acc", layer, b4))
                    for q4 in range(4):
                        nc.tensor.matmul(b[:, q4 * P:(q4 + 1) * P], zero_r[:, :], zero_r[:, :], start=(q4 == 0),
                                         stop=False)
                for s in range(2):
                    write_tile(pe, ("up", layer, s))
                pe.wait_ge(hlo_ready, KT * ((2, 4, 7)[layer] + 1))
                def turn(i, splits_on=True):
                    def up(s):
                        b = tiles[("up", layer, s)][0]
                        pe.wait_ge(ff_mul, 2 * i + (g0 + s + 1))
                        for e in range(2):
                            w = w0 + 2 * s + e
                            pe.wait_ge(split_done, 6 * i + (w + 1))
                            for k in range(KT):
                                a = wtile(w, k * P, P)
                                ins = split3(bank[b][:, e * T:(e + 1) * T], a[0], a[1], xs(h_hi, k), xs(h_lo, k),
                                             k == 0, k == KT - 1)
                            ins.then_inc(w_used, 1)

                    def down(s):
                        w = w0 + 4 + s
                        pe.wait_ge(split_done, 6 * i + (w + 1))
                        pe.wait_ge(ff_lo, 2 * i + (g0 + s + 1))
                        for j in range(KT):
                            b = bank[tiles[("acc", layer, j // 2)][0]]
                            a = wtile(w, j * P, P)
                            out = b[:, (j % 2) * T:(j % 2 + 1) * T]
                            ins = split3(out, a[0], a[1], g_hi[:, s, :], g_lo[:, s, :], False, False)
                        ins.then_inc(w_used, 1)

                    up(0)
                    up(1)
                    if layer < 2:
                        ada_layer[0] = layer + 1
                        ada_group(i + ada_in_loop(layer))
                    down(0)
                    down(1)

                with pe.Fori(0, FT // 2 - (layer == 2)) as i:
                    turn(i)
                if layer == 2:
                    turn(FT // 2 - 1, splits_on=False)
                for b4 in range(4):
                    name = ("acc", layer, b4)
                    for q4 in range(4):
                        ins = nc.tensor.matmul(bank[tiles[name][0]][:, q4 * P:(q4 + 1) * P], zero_r[:, :], zero_r[:, :],
                                               start=False, stop=(q4 == 3))
                    ins.then_inc(full_of(name), 1)

            pe.wait_ge(cs_ready, 1)
            for g in range(4):
                ada_group(g)
            pe.wait_ge(s_con, 16)
            norm(0)
            norm(1)
            pe.wait_ge(hlo_ready, 2 * KT)
            for j in range(N_IN0):
                if j < 3:
                    project(("in0", j), W_IN0 + j, both, 2 * T)
                else:
                    project(("in0", j), W_IN0 + j, xs, T)
                if j < 8:
                    ada_group(4 + j)
            b = write_tile(pe, "kvss")
            pe.wait_ge(lsq_ready, 1)
            lsq = sq[:, :, :].rearrange("p k t -> p (k t)")
            for k in range(KVL_T):
                ins = nc.tensor.matmul(b[:, :], ones, lsq[:, k * 512:(k + 1) * 512], start=(k == 0), stop=(k == KVL_T - 1))
            ins.then_inc(full_of("kvss"), 1)
            b = write_tile(pe, "qss")
            pe.wait_ge(lsq_ready, 2)
            for k in range(QL_T):
                ins = nc.tensor.matmul(b[:, 0:T], ones, lsq[:, 1024 + k * T:1024 + (k + 1) * T], start=(k == 0),
                                       stop=(k == QL_T - 1))
            ins.then_inc(full_of("qss"), 1)
            pe.wait_ge(lat_ready, N_IN0)
            for g in range(FN_T):
                b = write_tile(pe, ("dft1", g))
                for t in range(2):
                    ins = nc.tensor.matmul(b[:, t * T:(t + 1) * T], fu[:, g, t * P:(t + 1) * P], cc("dft_c"),
                                           start=True, stop=True)
                ins.then_inc(full_of(("dft1", g)), 1)
            for g in range(FN_T):
                b = write_tile(pe, ("dft2", g))
                pe.wait_ge(f1_ready, g + 1)
                n = 0
                for part in range(2):
                    for t in range(2):
                        ins = nc.tensor.matmul(b[:, 0:T], f1[:, g, t, part * P:(part + 1) * P],
                                               cc("dft_n", (2 * part + t) * T, (2 * part + t + 1) * T),
                                               start=(n == 0), stop=(n == 3))
                        n += 1
                ins.then_inc(full_of(("dft2", g)), 1)

            pe.wait_ge(llo_ready, 1 + KVL_T)
            split_ready(W_UV)

            def ckvn(h, k):
                return h[:, 2 * k:2 * k + 2, T:2 * T]

            for t in range(4):
                b = write_tile(pe, ("v0", t))
                for k in range(KVL_T):
                    at = (2 * k + t // 2, T + (t % 2) * P)
                    xh, xl = (h[:, at[0], at[1]:at[1] + P] for h in (h_hi, h_lo))
                    a = wtile(W_UV, k * 512, 512)
                    ins = split3(b[:, :], xh, xl, a[0], a[1], k == 0, k == KVL_T - 1)
                ins.then_inc(full_of(("v0", t)), 1)
            pe.wait_ge(llo_ready, 1 + KVL_T + QL_T)
            pe.wait_ge(cs_ready, 2)

            def unit_products(u):
                b = write_tile(pe, ("pj", u))
                if u < 4:
                    for e in range(2):
                        h = 2 * u + e
                        w = W_UQ + h // UQ_HEADS
                        split_ready(w)
                        for k in range(QL_T):
                            a = wtile(w, (h % UQ_HEADS) * QL_T * QK + k * QK, QK)
                            ins = split3(b[0:QK, e * T:(e + 1) * T], a[0], a[1], h_hi[:, 4 + k, T:2 * T],
                                         h_lo[:, 4 + k, T:2 * T], k == 0, k == QL_T - 1)
                else:
                    h = u - 4
                    w = W_UK + h // UK_HEADS
                    split_ready(w)
                    out = b[0:QK, :]
                    for k in range(KVL_T):
                        a = wtile(w, (h % UK_HEADS) * KVL_T * QK + k * QK, QK)
                        split3(out, a[0], a[1], ckvn(h_hi, k), ckvn(h_lo, k), k == 0, False)
                    nc.tensor.matmul(out, place_r[:], kr_hi, start=False, stop=False)
                    ins = nc.tensor.matmul(out, place_r[:], kr_lo, start=False, stop=True)
                ins.then_inc(full_of(("pj", u)), 1)

            def unit_sums(u):
                b = write_tile(pe, ("ss", u))
                pe.wait_ge(usq_ready, u + 1)
                nc.tensor.matmul(b[0:QK, :], ones[0:QK, 0:QK], usq[0:QK, u % 2, :], start=True, stop=True)\
                    .then_inc(full_of(("ss", u)), 1)
                b = write_tile(pe, ("rot", u))
                pe.wait_ge(unit_ready, u + 1)
                nc.tensor.matmul(b[0:QK, :], cc("swap")[0:QK, :], unit[0:QK, u % 2, :], start=True, stop=True)\
                    .then_inc(full_of(("rot", u)), 1)

            unit_products(0)
            for u in range(12):
                if u + 1 < 12:
                    unit_products(u + 1)
                unit_sums(u)
            pe.wait_ge(*tiles[("pj", 11)][1])
            pe.sem_inc(w_used, N_UQ + N_UK + 1)
            pe.wait_ge(head_ready, 12)
            pe.wait_ge(v_ready, 4)
            attention("mla", MLA_H, 0, 0, lambda h: (querT[0:QK, h, :], keysT[0:QK, h, :]),
                      lambda h, kt: vals0[:, kt, h * VH:(h + 1) * VH])
            project_out(0, W_OUT0, 8)
            norm(2)
            ffn(0)
            norm(3)
            pe.wait_ge(hlo_ready, 4 * KT)
            for j in range(N_IN1):
                project(("in1", j), W_IN1 + j, xs, T)
            ada_layer[0] = 1
            ada_group(23)
            pe.wait_ge(conf_ready, 9)
            for half in range(2):
                b = write_tile(pe, ("csum", half))
                nc.tensor.matmul(b[:, :], ones, cacc[:, 2 * half:2 * half + 2, :].rearrange("p g t -> p (g t)"),
                                 start=True, stop=True).then_inc(full_of(("csum", half)), 1)
            for half in range(2):
                b = write_tile(pe, ("cvar", half))
                pe.wait_ge(csq_ready, half + 1)
                nc.tensor.matmul(b[:, :], ones, csq[:, 2 * half:2 * half + 2, :].rearrange("p g t -> p (g t)"),
                                 start=True, stop=True).then_inc(full_of(("cvar", half)), 1)
            project_out(1, W_OUT1, 16)
            norm(4)
            ffn(1)
            norm(5)
            norm(6)
            pe.wait_ge(hlo_ready, 7 * KT)
            for j in range(17):
                if j < 16:
                    project(("qk", j), W_K2 + j, both if j < 8 else xs, 2 * T if j < 8 else T)
                if j:
                    i = j - 1
                    n = 2 * T if i < 8 else T
                    b = write_tile(pe, ("qkss", i))
                    pe.wait_ge(usq_ready, 12 + i + 1)
                    nc.tensor.matmul(b[:, 0:n], cc("ones64"), nsq[:, i % 2, 0:n], start=True, stop=True)\
                        .then_inc(full_of(("qkss", i)), 1)
            for half in range(2):
                banks = [write_tile(pe, ("v2", half, t)) for t in range(4)]
                for q4 in range(4):
                    w = W_V2 + 4 * half + q4
                    split_ready(w)
                    for e in range(2):
                        k = 2 * q4 + e
                        a = wtile(w, e * 512, 512)
                        for t in range(4):
                            ins = split3(banks[t][:, :], h_hi[:, k, t * P:(t + 1) * P], h_lo[:, k, t * P:(t + 1) * P],
                                         a[0], a[1], k == 0, k == KT - 1)
                            if k == KT - 1 and t < 3:
                                ins.then_inc(full_of(("v2", half, t)), 1)
                    ins.then_inc(w_used, 1)
            ada_layer[0] = 2
            ada_group(35)
            pe.wait_ge(v_ready, 12)
            pe.wait_ge(head_ready, 28)
            attention("na", NA_H, 16, 0,
                      lambda h: (querT[(h % 2) * NA_D:(h % 2 + 1) * NA_D, h // 2, :],
                                 keysT[(h % 2) * NA_D:(h % 2 + 1) * NA_D, h // 2, :]),
                      lambda h, kt: vals[:, kt, h * NA_D:(h + 1) * NA_D])
            project_out(2, W_OUT2, 24)
            norm(7)
            ffn(2)


def pack_weights(i):
    w = np.zeros((N_W, P, BLK), np.float32)

    def across(at, m, tiles=None):
        n = m.shape[1] // P
        w[at:at + n] = m.reshape(KT, P, n, P).transpose(2, 1, 0, 3).reshape(n, P, BLK)

    def ffn(at, w1, w3, w2):
        b = w[at:at + 3 * FT].reshape(FT // 2, 6, P, BLK)
        for e, m in enumerate((w1, w3)):
            up = m.reshape(KT, P, FT // 2, 2, P).transpose(2, 3, 1, 0, 4).reshape(FT // 2, 2, P, BLK)
            b[:, e], b[:, 2 + e] = up[:, 0], up[:, 1]
        down = w2.reshape(FT // 2, 2, P, BLK)
        b[:, 4], b[:, 5] = down[:, 0], down[:, 1]

    a = i["a_w_in"][0]
    q, kv, kr, fn = np.split(a, [QL_T * P, (QL_T + KVL_T) * P, (QL_T + KVL_T) * P + ROPE_D], axis=1)
    across(W_IN0, np.concatenate([kv, np.pad(kr, ((0, 0), (0, P - ROPE_D))), q, fn], axis=1))
    uq = i["a_w_uq"][0].reshape(QL_T, P, MLA_H, QK).transpose(2, 1, 0, 3)
    for h in range(MLA_H):
        c = (h % UQ_HEADS) * QL_T * QK
        w[W_UQ + h // UQ_HEADS, :, c:c + QL_T * QK] = uq[h].reshape(P, QL_T * QK)
    uk = np.pad(i["a_w_uk"][0], ((0, 0), (0, 0), (0, ROPE_D))).reshape(KVL_T, P, MLA_H, QK).transpose(2, 1, 0, 3)
    for h in range(MLA_H):
        c = (h % UK_HEADS) * KVL_T * QK
        w[W_UK + h // UK_HEADS, :, c:c + KVL_T * QK] = uk[h].reshape(P, KVL_T * QK)
    w[W_UV] = i["a_w_uv"][0].reshape(KVL_T, P, 512).transpose(1, 0, 2).reshape(P, BLK)
    across(W_OUT0, i["a_w_out"][0])
    ffn(W_FF0, i["ffn_w1"][0], i["ffn_w3"][0], i["ffn_w2"][0])
    a, gate, sb_, scc, sx = np.split(i["b_w_in"][0], 5, axis=1)

    def woven(u, v):
        return np.stack([u.reshape(D, 4, P), v.reshape(D, 4, P)], axis=2).reshape(D, 8 * P)

    across(W_IN1, np.concatenate([woven(gate, a), woven(scc, sx), sb_], axis=1))
    across(W_OUT1, i["b_w_out"][0])
    ffn(W_FF1, i["ffn_w1"][1], i["ffn_w3"][1], i["ffn_w2"][1])
    q, k, v = np.split(i["l0_na_w_qkv_2"], 3, axis=1)
    across(W_K2, k)
    across(W_Q2, q)
    w[W_V2:W_V2 + 8] = v.reshape(4, 2, P, 2, 512).transpose(3, 0, 2, 1, 4).reshape(8, P, BLK)
    across(W_OUT2, i["l0_na_w_o_2"])
    up = i["l0_ffn_w_up_2"]
    ffn(W_FF2, up[:, :F_FF], up[:, F_FF:], i["l0_ffn_w_down_2"])
    return w


def pack_ada(i):
    m = np.stack([i["ada_w"][0], i["ada_w"][1], i["l0_w_mod_2"]])
    return np.ascontiguousarray(m.reshape(LAYERS, KT, P, MODS, P).transpose(0, 3, 2, 1, 4).reshape(N_A, P, BLK))


def by_partition(v):
    return np.moveaxis(v.reshape(*v.shape[:-1], -1, P), -1, 0).reshape(P, -1)


def pack_params(i):
    t = np.zeros((P, N_PARAMS), np.float32)

    def put(name, a):
        c0, c1 = PARAMS[name]
        assert a.shape[1] == c1 - c0, name
        t[:a.shape[0], c0:c1] = a

    pairs = [(i["c"][0], i["c_ctx"]), (i["c"][0], i["c_ctx"]), (i["c_2"][0], i["c_ctx_2"])]
    c = np.stack([np.stack([u.reshape(KT, P), v.reshape(KT, P)], axis=-1) for u, v in pairs])
    put("c", c.transpose(2, 0, 1, 3).reshape(P, -1))
    put("ada_b", by_partition(np.stack([i["ada_b"][0], i["ada_b"][1], i["l0_b_mod_2"]])))
    put("norm1", by_partition(np.stack([i["norm1_g"][0], i["norm1_g"][1], i["l0_norm1_2"]])))
    put("norm2", by_partition(np.stack([i["norm2_g"][0], i["norm2_g"][1], i["l0_norm2_2"]])))
    put("q_ln", by_partition(i["a_q_ln_g"][0]))
    put("kv_ln", by_partition(i["a_kv_ln_g"][0]))
    put("q_norm", i["a_q_norm_g"][0][:, None])
    put("k_norm", i["a_k_norm_g"][0][:, None])
    put("conf_dw", i["b_conf_dw"][0].reshape(CONF_K, CG, P).transpose(2, 1, 0).reshape(P, -1))
    put("conf_b", by_partition(i["b_conf_dw_b"][0]))
    put("ln_g", by_partition(i["b_conf_ln_g"][0]))
    put("ln_b", by_partition(i["b_conf_ln_b"][0]))
    put("sc_dw", i["b_sc_dw"][0].reshape(SC_K, CG, P).transpose(2, 1, 0).reshape(P, -1))
    put("na_q", np.tile(i["l0_na_q_gain_2"], 2)[:, None])
    put("na_k", np.tile(i["l0_na_k_gain_2"], 2)[:, None])
    conv = np.concatenate([i["l0_ffn_conv_w_2"], i["l0_ffn_conv_b_2"][None]])
    put("ff_conv", conv.reshape(4, FT, P).transpose(2, 1, 0).reshape(P, -1))
    return t


def feature_major(x):
    return np.ascontiguousarray(x[0].reshape(T, KT, P).transpose(2, 1, 0))


def pack_rpb(rpb):
    rows = rpb[:, WIN // 2 - ROWS:WIN // 2 - 1 + ROWS, :]
    side = (TOEP - rpb.shape[2]) // 2
    t = np.pad(rows[:, ::-1], ((0, 0), (0, 0), (side, side))).transpose(0, 2, 1)
    return np.pad(t.reshape(-1), (0, 64))


def kernel(**inputs):
    import concourse.bacc as bacc
    from concourse.bass_utils import run_bass_kernel_spmd as run

    i = {k: np.asarray(v) for k, v in inputs.items()}
    arrays = {
        "weights": pack_weights(i), "ada": pack_ada(i), "xt": feature_major(i["x"]),
        "ctx1": feature_major(i["ctx"]), "ctx2": feature_major(i["ctx_2"]), "params": pack_params(i),
        "consts": constant_table(), "rpb": pack_rpb(i["l0_na_rpb_2"])}
    nc = bacc.Bacc("TRN2", target_bir_lowering=False, num_devices=1)
    args = [nc.dram_tensor(n, a.shape, mybir.dt.from_np(a.dtype), kind="ExternalInput").ap()
            for n, a in arrays.items()]
    out = nc.dram_tensor("out_t", (P, KT, T), mybir.dt.float32, kind="ExternalOutput").ap()
    program(nc, *args, out)
    got = run(nc, [arrays], core_ids=[0]).results[0]["out_t"]
    return got.transpose(2, 1, 0).reshape(1, T, D)
```

```python
import math
from contextlib import ExitStack

import numpy as np

import concourse.bass as bass
from concourse import mybir

P = 128
D = 1024
KT = D // P
T = 256
F_FF = 2816
FT = F_FF // P
EPS = 1e-6
LAYERS = 3
MODS = 6 * KT

MLA_H, NOPE, ROPE_D, QK, VH = 8, 64, 32, 96, 64
QL_T, KVL_T, FN_T = 3, 2, 4
CONF_K, SC_K, CG = 31, 3, 4
NA_H, NA_D, GRID_W, WIN = 16, 64, 64, 16
ROWS = T // GRID_W
TOEP = 2 * GRID_W - 1
DRS = 2 * ROWS - 1
MASKED = -1e30

BLK = KT * P
RING = 6
AGRP = 4
LEAD = 4

W_IN0, N_IN0 = 0, 10
W_UQ, N_UQ = 10, 3
W_UK, W_UV, W_OUT0 = 13, 14, 15
W_FF0 = W_OUT0 + KT
W_IN1, N_IN1 = W_FF0 + 3 * FT, 20
W_OUT1 = W_IN1 + N_IN1
W_FF1 = W_OUT1 + KT
W_K2 = W_FF1 + 3 * FT
W_Q2 = W_K2 + KT
W_V2 = W_Q2 + KT
W_OUT2 = W_V2 + KT
W_FF2 = W_OUT2 + KT
N_W = W_FF2 + 3 * FT
N_A = LAYERS * MODS
assert N_A % AGRP == 0 and FT % 2 == 0


def columns(sizes):
    out, at = {}, 0
    for name, n in sizes:
        out[name] = (at, at + n)
        at += n
    return out, at


PARAMS, N_PARAMS = columns([
    ("c", LAYERS * KT * 2), ("ada_b", LAYERS * MODS), ("norm1", LAYERS * KT), ("norm2", LAYERS * KT),
    ("q_ln", QL_T), ("kv_ln", KVL_T), ("q_norm", 1), ("k_norm", 1), ("k_nope", 1),
    ("conf_dw", CG * CONF_K), ("conf_b", CG), ("ln_g", CG), ("ln_b", CG), ("sc_dw", CG * SC_K),
    ("na_q", 1), ("na_k", 1), ("ff_conv", FT * 4)])
CONSTS, N_CONSTS = columns([
    ("ident", P), ("ones", P), ("of_pair", 2), ("of_rope", MLA_H), ("of_query", 1), ("of_cond", 2), ("cos", T),
    ("sin", T), ("dft_c", 2 * P), ("dft_n", 2 * 2 * T), ("mask", GRID_W)])


STATS, N_STAT = columns(
    [(("norm", n), 2) for n in range(8)] + [("kv", 4), ("ql", 2), ("mq", 2 * MLA_H), ("mk", 4 * MLA_H), ("conf", 2 * CG)]
    + [(("qk", j), 8 if j < 8 else 4) for j in range(16)])
STAT_ORDER = ([("norm", 0), ("norm", 1), "kv", "ql", "mq", "mk", ("norm", 2), ("norm", 3), "conf", ("norm", 4),
               ("norm", 5), ("norm", 6)] + [("qk", j) for j in range(16)] + [("norm", 7)])


def constant_table():
    t = np.zeros((P, N_CONSTS), np.float32)

    def put(name, a):
        c0, _ = CONSTS[name]
        t[:a.shape[0], c0:c0 + a.shape[1]] = a

    put("ident", np.eye(P))
    put("ones", np.ones((P, P)))
    row = np.arange(P)[:, None]
    put("of_pair", (row // NA_D == np.arange(2)).astype(np.float32))
    put("of_rope", np.repeat((row >= NOPE) & (row < QK), MLA_H, axis=1).astype(np.float32))
    put("of_query", (row < QK).astype(np.float32))
    put("of_cond", (row % 32 == np.arange(2)).astype(np.float32))
    per_axis = ROPE_D // 4
    inv = np.float32(10000.0) ** (-np.arange(per_axis, dtype=np.float32) / np.float32(per_axis))
    n = np.arange(T)
    row, col = (n // GRID_W).astype(np.float32), (n % GRID_W).astype(np.float32)
    ang = np.concatenate([row[:, None] * inv, col[:, None] * inv], axis=1).astype(np.float32)
    cos, sin = np.zeros((P, T), np.float32), np.zeros((P, T), np.float32)
    cos[NOPE:QK] = np.concatenate([np.cos(ang), np.cos(ang)], axis=1).T
    sin[QK:] = np.concatenate([-np.sin(ang), np.sin(ang)], axis=1).T
    put("cos", cos)
    put("sin", sin)
    c = np.arange(P)
    w = 2 * np.pi * np.outer(c, c) / P
    put("dft_c", np.concatenate([np.cos(w), np.sin(w)], axis=1))
    w = 2 * np.pi * (np.outer(n, n) % T) / T
    norm = 1.0 / math.sqrt(T * P)
    both = np.stack([np.cos(w) * norm, -np.sin(w) * norm])
    put("dft_n", both.reshape(2, 2, P, T).transpose(2, 0, 1, 3).reshape(P, 4 * T))
    q = np.arange(P) % GRID_W
    k = np.arange(GRID_W)
    first = np.clip(q - WIN // 2, 0, GRID_W - WIN)[:, None]
    put("mask", np.where((k >= first) & (k < first + WIN), 0.0, MASKED))
    return t


def program(nc, weights, ada, xt_in, ctx1_in, ctx2_in, params_in, consts_in, rpb_in, out_t, upto=9):
    fp, fr = mybir.dt.float32, mybir.dt.float32r
    ALU, ACT, AX = mybir.AluOpType, mybir.ActivationFunctionType, mybir.AxisListType
    MUL, ADD, SUB = ALU.mult, ALU.add, ALU.subtract

    ctx = ExitStack()
    with ctx:
        def sb(name, shape, dt=fp):
            return ctx.enter_context(nc.sbuf_tensor(name, shape, dt))

        def sem(name):
            return ctx.enter_context(nc.semaphore(name))

        w_raw = sb("w_raw", [P, RING, BLK])
        w_hi = sb("w_hi", [P, RING, BLK], fr)
        w_lo = sb("w_lo", [P, RING, BLK], fr)
        a_raw = sb("a_raw", [P, AGRP, BLK])
        xT = sb("xT", [P, KT, T])
        h_hi = sb("h_hi", [P, KT, 2 * T], fr)
        h_lo = sb("h_lo", [P, KT, 2 * T], fr)
        par = sb("par", [P, N_PARAMS])
        con = sb("con", [P, N_CONSTS])
        cs = sb("cs", [P, LAYERS, KT, 2])
        mods = sb("mods", [P, LAYERS, MODS, 2])
        gain = sb("gain", [P, KT])
        eps = sb("eps", [P, 1])
        zero_r = sb("zero_r", [P, P], fr)
        stat = sb("stat", [P, N_STAT])
        eps_q = sb("eps_q", [P, 1])
        ada_s = sb("ada_s", [P, 4 * P])
        big = sb("big", [P, 24 * 256])
        ctxT = big[:, 0:2048].rearrange("p (k t) -> p k t", k=KT)
        sq = big[:, 2048:4096].rearrange("p (k t) -> p k t", k=KT)
        tmp = big[:, 4096:6144].rearrange("p (k t) -> p k t", k=KT)
        keysT = big[:, 0:4096].rearrange("p (h t) -> p h t", h=8)
        querT = big[:, 4096:6144].rearrange("p (h t) -> p h t", h=8)
        vals = sb("vals", [P, 4, D])
        work = sb("work", [P, 12 * 256])
        prob = work[:, 0:1024].rearrange("p (b t) -> p b t", b=2)
        probT = work[:, 1024:3072].rearrange("p (b k t) -> p b k t", b=2, k=4)
        nmax = sb("nmax", [P, 32])
        rsum = sb("rsum", [P, 32])
        rinv = sb("rinv", [P, 32])
        act_f = work[:, 0:512].rearrange("p (b t) -> p b t", b=2)
        gate_f = work[:, 512:1024].rearrange("p (b t) -> p b t", b=2)
        cv = work[:, 1024:2560].rearrange("p (b m t) -> p b m t", b=2, m=3)
        g_hi = sb("g_hi", [P, 2, T], fr)
        g_lo = sb("g_lo", [P, 2, T], fr)
        bank = [ctx.enter_context(nc.psum_tensor(f"bank{i}", [P, 2 * T], fp)) for i in range(8)]

        def pc(name, j=0, n=1):
            c0, _ = PARAMS[name]
            return par[:, c0 + j:c0 + j + n]

        def cc(name, lo=0, hi=None):
            c0, c1 = CONSTS[name]
            return con[:, c0 + lo:(c1 if hi is None else c0 + hi)]

        ident, ones = cc("ident"), cc("ones")

        cq = work[:, 0:768].rearrange("p (k t) -> p k t", k=3)
        ckv = work[:, 768:1792].rearrange("p (k t) -> p k t", k=2)
        fu = vals[:, 0, :].rearrange("p (g t) -> p g t", g=4)
        rope_k = vals[:, 1, 0:512]
        kr_sq = vals[:, 1, 512:1024]
        f1 = big[:, 0:2048].rearrange("p (g u c) -> p g u c", g=4, u=2)
        usq = vals[:, 2:4, 0:512]
        rot1 = work[:, 2048:2560]
        rot2 = work[:, 2560:3072]
        vals0 = vals[:, :, 512:1024]
        sgate = work[:, 0:512].rearrange("p (b t) -> p b t", b=2)
        confp = vals[:, 0:2, :].rearrange("p a b -> p (a b)")[:, 0:CG * 288].rearrange("p (g t) -> p g t", g=CG)
        cacc = vals[:, 2, :].rearrange("p (g t) -> p g t", g=CG)
        ccen = vals[:, 3, :].rearrange("p (g t) -> p g t", g=CG)
        csq = work[:, 512:1536].rearrange("p (g t) -> p g t", g=CG)
        scp = big[:, 2048:2048 + CG * 264].rearrange("p (g t) -> p g t", g=CG)
        sacc = big[:, 4096:4096 + CG * T].rearrange("p (g t) -> p g t", g=CG)
        bias = sb("bias", [P, 3, GRID_W, DRS])
        nsq = work[:, 0:1024].rearrange("p (b t) -> p b t", b=2)
        gpad = vals[:, 0, 0:2 * (T + 2)].rearrange("p (b t) -> p b t", b=2)
        taps = sb("taps", [P, 2, 4])

        s_par, s_con, s_x, s_ctx = sem("params_loaded"), sem("consts_loaded"), sem("x_loaded"), sem("ctx_loaded")
        w_loaded = [sem(f"w_loaded{i}") for i in range(RING)]
        a_loaded = [sem(f"a_loaded{i}") for i in range(AGRP)]
        hi_done, split_done, w_used = sem("w_hi_done"), sem("w_split_done"), sem("w_used")
        a_used = sem("ada_block_used")
        full = [sem(f"bank{i}_full") for i in range(8)]
        free = [sem(f"bank{i}_free") for i in range(8)]
        cs_ready, mod_ready, gain_ready = sem("cond_ready"), sem("mods_ready"), sem("gain_ready")
        const_ready, pads_ready = sem("const_ready"), sem("pads_ready")
        sq_ready, root_ready, inv_ready = sem("norm_sq"), sem("root_ready"), sem("root_inverted")
        ada_copied, ada_turned, ada_cleared = sem("ada_copied"), sem("ada_turned"), sem("ada_cleared")
        krsq_ready, kr_taken, rope_ready = sem("rope_sq"), sem("rope_taken"), sem("rope_ready")
        tmp_ready, hhi_ready, hlo_ready = sem("norm_scaled"), sem("h_hi_ready"), sem("h_lo_ready")
        x_updated = sem("x_updated")
        lat_ready, lsq_ready, ltmp_ready = sem("latents_ready"), sem("latent_sq"), sem("latent_scaled")
        lhi_ready, llo_ready = sem("latent_hi"), sem("latent_lo")
        f1_ready, o_hi, o_lo = sem("dft1_ready"), sem("mix_hi"), sem("mix_lo")
        v_ready = sem("values_ready")
        usq_ready, unit_ready, head_ready = sem("unit_sq"), sem("unit_gained"), sem("head_ready")
        nmax_ready, exp_ready, prob_ready, pT_ready, pv_done = (
            sem("nmax_ready"), sem("exp_ready"), sem("prob_ready"), sem("probT_ready"), sem("pv_done"))
        sg_ready, conf_ready, cen_ready, csq_ready = (
            sem("sigmoid_ready"), sem("conv_ready"), sem("centred"), sem("centred_sq"))
        cn_ready, conf_out, scc_ready, sc_out = sem("conf_normed"), sem("conf_silu"), sem("scc_ready"), sem("short_out")
        b_loaded = [sem(f"bias_loaded{i}") for i in range(3)]
        bias_ready, bias_used = sem("bias_masked"), sem("bias_used")
        ff_act, ff_mul, ff_hi, ff_lo = sem("ff_activated"), sem("ff_product"), sem("ff_hi"), sem("ff_lo")
        ff_pad, ff_cv = sem("ff_padded"), sem("ff_convolved")
        dve_seq, act_seq = sem("dve_step"), sem("act_step")
        stored = sem("stored")

        tiles, last_taken, made_count, free_count = {}, [None] * 8, [0] * 8, [0] * 8

        def place_tile(name, b, taken=None, made=None):
            if made is None:
                made_count[b] += 1
                made = (full[b], made_count[b])
            if taken is None:
                free_count[b] += 1
                taken = (free[b], free_count[b])
            tiles[name] = (b, made, last_taken[b])
            last_taken[b] = taken

        def used(w):
            return (w_used, w + 1)

        def place_stat(name, b):
            place_tile(("sum", name), b, (root_ready, STAT_ORDER.index(name) + 1))

        def place_norm(n):
            place_stat(("norm", n), 7)
            place_tile(("inv", n), 5, (tmp_ready, KT * (n + 1)))

        place_norm(0)
        place_norm(1)
        for j in range(N_IN0):
            place_tile(("in0", j), j % 4, (kr_taken, 1) if j == 2 else (lat_ready, j + (j < 2)), used(W_IN0 + j))
        place_stat("kv", 7)
        place_stat("ql", 5)
        for g in range(FN_T):
            place_tile(("dft1", g), g, (f1_ready, g + 1))
        place_tile(("inv", "kv"), 4, (ltmp_ready, KVL_T))
        place_tile(("inv", "ql"), 7, (ltmp_ready, KVL_T + QL_T))
        for g in range(FN_T):
            place_tile(("dft2", g), 2 + g % 2, (o_lo, g + 1))
        for u in range(8):
            place_tile(("pj", u), u % 2, (unit_ready, u + 1), None if u < 7 else used(W_UK))
        place_stat("mq", 5)
        place_stat("mk", 7)
        for t in range(4):
            place_tile(("v0", t), t, (v_ready, t + 1), None if t < 3 else used(W_UV))
        for h in range(MLA_H):
            place_tile(("inv", "mk", h), 4 + h % 2, (head_ready, h + 1))

        def place_attention(name, heads, at0, o0):
            for i in range(2 * heads):
                place_tile((name, "sc", i), i % 2, (exp_ready, at0 + i + 1))
                place_tile((name, "tr", i), 2 + i % 2, (pT_ready, at0 + i + 1))
            for p in range(heads // 2):
                place_tile((name, "o", p), 4 + p % 2, (o_lo, o0 + p + 1))

        def place_ffn(layer):
            for j in range(KT):
                place_tile(("out", layer, j), j % 4, (x_updated, 2 * KT * layer + j + 1),
                           used((W_OUT0, W_OUT1, W_OUT2)[layer] + j))
            place_norm((2, 4, 7)[layer])
            for b in range(4):
                place_tile(("acc", layer, b), b, (x_updated, KT * (2 * layer + 1) + 2 * b + 2))
            for s in range(2):
                place_tile(("up", layer, s), 4 + s, (ff_mul, FT * (layer + 1) + s + 1), used(-1))

        place_attention("mla", MLA_H, 0, 4)
        place_ffn(0)
        place_norm(3)
        for j in range(N_IN1):
            g = j // 2
            taken = ((sc_out, j - 15) if j >= 16 else (conf_ready, g + 1) if j % 2
                     else (sg_ready, g + 1) if j < 8 else (scc_ready, g - 3))
            place_tile(("in1", j), j % 4, taken, used(W_IN1 + j))
        for half in range(2):
            place_tile(("csum", half), 4 + half, (cen_ready, half + 1))
        place_stat("conf", 7)
        for half in range(2):
            place_tile(("inv", "conf", half), 4 + half, (cn_ready, half + 1))
        place_ffn(1)
        place_norm(5)
        place_norm(6)
        for j in range(16):
            place_tile(("qk", j), j % 3, (unit_ready, 8 + j + 1), used(W_K2 + j))
            place_stat(("qk", j), 3 + 4 * (j % 2))
            place_tile(("inv", "qk", j), 4 + j % 2, (head_ready, MLA_H + j + 1))
        for half in range(2):
            for t in range(4):
                place_tile(("v2", half, t), t, (v_ready, 4 + 4 * half + t + 1),
                           used(W_V2 + 4 * half + 3) if t == 3 else None)
        place_attention("na", NA_H, 16, 16)
        place_ffn(2)

        def write_tile(pe, name):
            b, _, before = tiles[name]
            if before:
                pe.wait_ge(*before)
            return bank[b]

        def wait_tile(eng, name):
            b, made, _ = tiles[name]
            eng.wait_ge(*made)
            return bank[b]

        def full_of(name):
            return full[tiles[name][0]]

        def free_of(name):
            return free[tiles[name][0]]

        NORMS = [("c", 0, 1, 0, 0), ("x", T, 0, 0, 0), ("x", T, 0, 0, 1), ("x", T, 0, 1, 0),
                 ("x", T, 0, 1, 1), ("c", 0, 1, 2, 0), ("x", T, 0, 2, 0), ("x", T, 0, 2, 1)]
        UPDATES = [0, 0, 1, 2, 3, 4, 4, 5]
        MOD_GROUPS = [4, 4, 10, 16, 22, 28, 28, 34]

        def ada_in_loop(layer):
            return (12, 24, None)[layer]

        block = ctx.enter_context(nc.Block())

        @block.sync
        def _(sp):
            def block_of(stream, n):
                return stream[n] if isinstance(n, int) else stream[bass.ds(n, 1), :, :].rearrange("o p n -> (o p) n")

            def load_w(w, s):
                if not isinstance(w, int) or w >= RING:
                    sp.wait_ge(split_done, w - (RING - 1))
                sp.dma_start(w_raw[:, s, :], block_of(weights, w)).then_inc(w_loaded[s], 16)

            def load_ada(g):
                for s in range(AGRP):
                    if not isinstance(g, int) or g:
                        sp.wait_ge(a_used, AGRP * g + (s + 1 - AGRP))
                    sp.dma_start(a_raw[:, s, :], block_of(ada, AGRP * g + s)).then_inc(a_loaded[s], 16)

            w_next = [0]

            def load_to(w):
                while w_next[0] < min(w, N_W):
                    load_w(w_next[0], w_next[0] % RING)
                    w_next[0] += 1

            sp.dma_start(par[:], params_in).then_inc(s_par, 16)
            load_ada(0)
            sp.dma_start(ctxT, ctx1_in).then_inc(s_ctx, 16)
            sp.dma_start(xT[:], xt_in).then_inc(s_x, 16)
            sp.dma_start(con[:], consts_in).then_inc(s_con, 16)
            for g in range(1, 4):
                load_ada(g)
            load_to(RING)
            load_ada(4)
            for j in range(7):
                load_to(RING + j + 1)
                load_ada(5 + j)
            load_ada(12)
            for layer, w0 in enumerate((W_FF0, W_FF1, W_FF2)):
                ahead = LEAD + RING
                load_to(w0 + ahead)
                with sp.Fori(0, FT // 2 - (2 if layer == 2 else 0)) as i:
                    for j in range(6):
                        if j == 4 and layer < 2:
                            load_ada(i + (ada_in_loop(layer) + 1))
                        load_w(6 * i + (w0 + ahead + j), (w0 + ahead + j) % RING)
                w_next[0] = w0 + ahead + 3 * FT - (12 if layer == 2 else 0)
                if layer == 0:
                    load_to(W_OUT1 + 4)
                    load_ada(24)
            load_to(N_W)
            sp.wait_ge(x_updated, 6 * KT)
            sp.dma_start(out_t, xT[:]).then_inc(stored, 16)
            sp.wait_ge(stored, 16)

        @block.gpsimd
        def _(pool):
            nc.gpsimd.memset(eps[:], EPS).then_inc(const_ready, 1)
            nc.gpsimd.memset(eps_q[:], QK * EPS).then_inc(const_ready, 1)
            nc.gpsimd.memset(zero_r[:].bitcast(fp), 0.0).then_inc(const_ready, 1)
            def load_bias(h):
                if h >= 3:
                    pool.wait_ge(bias_used, h - 2)
                src = bass.AP(rpb_in.tensor, h * TOEP * DRS + (GRID_W - 1) * DRS,
                              [[1, 2], [-DRS, GRID_W], [1, GRID_W * DRS]])
                pool.dma_start(bias[:, h % 3, :, :].rearrange("p c d -> p (c d)"), src).then_inc(b_loaded[h % 3], 16)

            pool.wait_ge(s_con, 16)
            for h in range(2):
                load_bias(h)
            for h in range(NA_H):
                if h + 2 < NA_H:
                    load_bias(h + 2)
                pool.wait_ge(b_loaded[h % 3], 16 * (h // 3 + 1))
                nc.gpsimd.tensor_tensor(bias[:, h % 3, :, :], bias[:, h % 3, :, :],
                                        cc("mask").unsqueeze(2).broadcast_to([P, GRID_W, DRS]), ADD)\
                    .then_inc(bias_ready, 1)

        @block.scalar
        def _(act):
            hi_next = [0]
            steps = [0]

            def split_hi(w, s, turn):
                act.wait_ge(w_loaded[s], 16 * turn)
                if not isinstance(w, int) or w >= RING:
                    act.wait_ge(w_used, w - (RING - 1))
                nc.scalar.copy(w_hi[:, s, :], w_raw[:, s, :]).then_inc(hi_done, 1)

            def split_to(w):
                while hi_next[0] <= min(w, N_W - 1):
                    n = hi_next[0]
                    split_hi(n, n % RING, n // RING + 1)
                    hi_next[0] += 1

            def root(name, width, bias=eps):
                b = wait_tile(act, ("sum", name))
                c0, c1 = STATS[name]
                nc.scalar.activation(stat[:, c0:c1], b[:, 0:c1 - c0], ACT.Sqrt, bias=bias[:], scale=1.0 / width)\
                    .then_inc(root_ready, 1)

            def ada_copy(g):
                act.wait_ge(a_used, AGRP * g + AGRP)
                nc.scalar.copy(ada_s[:], bank[6][:, :]).then_inc(ada_copied, 1)

            def norm(n):
                src, c0, col, layer, which = NORMS[n]
                if n == 0:
                    act.wait_ge(s_ctx, 16)
                if n == 1:
                    act.wait_ge(s_x, 16)
                if n == 5:
                    act.wait_ge(s_ctx, 32)
                v = ctxT if src == "c" else xT
                for half in range(2):
                    k0 = half * 4
                    if src == "x" and UPDATES[n]:
                        act.wait_ge(x_updated, KT * (UPDATES[n] - 1) + k0 + 4)
                    nc.scalar.activation(sq[:, k0:k0 + 4, :], v[:, k0:k0 + 4, :], ACT.Square).then_inc(sq_ready, 1)
                act.wait_ge(const_ready, 3)
                root(("norm", n), D)
                for k in range(KT):
                    act.wait_ge(tmp_ready, KT * n + k + 1)
                    sh = mods[:, layer, 3 * KT * which + k, col:col + 1]
                    nc.scalar.activation(h_hi[:, k, c0:c0 + T], tmp[:, k, :], ACT.Identity, bias=sh)\
                        .then_inc(hhi_ready, 1)

            def attention(name, heads, at0, o0, query_scale):
                def turned(i):
                    b = wait_tile(act, (name, "tr", i))
                    h = i // 2
                    if h >= 2:
                        act.wait_ge(pv_done, at0 // 2 + h - 1)
                    nc.scalar.copy(probT[:, h % 2, :, (i % 2) * P:(i % 2 + 1) * P],
                                   b[:, :].rearrange("p (k q) -> p k q", k=4)).then_inc(pT_ready, 1)

                def out_hi(p):
                    b = wait_tile(act, (name, "o", p))
                    nc.scalar.copy(h_hi[:, p, 0:T], b[:, 0:T]).then_inc(o_hi, 1)

                for i in range(2 * heads):
                    b = wait_tile(act, (name, "sc", i))
                    act.wait_ge(nmax_ready, at0 + i + 1)
                    nc.scalar.activation(prob[:, i % 2, :], b[:, :], ACT.Exp, bias=nmax[:, i:i + 1],
                                         scale=query_scale(i), accum_out=rsum[:, i:i + 1]).then_inc(exp_ready, 1)
                    if i:
                        turned(i - 1)
                    if i >= 5 and i % 4 == 1:
                        out_hi((i - 5) // 4)
                turned(2 * heads - 1)
                out_hi(heads // 2 - 1)

            def ffn(layer):
                w0, g0 = (W_FF0, W_FF1, W_FF2)[layer], FT * layer
                split_to(w0 + LEAD - 1)
                def turn(i, splits_on=True):
                    def hi(j, on=True):
                        if on:
                            split_hi(3 * 2 * i + (w0 + j), (w0 + j) % RING, i + ((w0 + j) // RING + 1))

                    def activate(s):
                        b = tiles[("up", layer, s)][0]
                        act.wait_ge(w_used, 6 * i + (w0 + 2 * s + 2))
                        if layer < 2:
                            nc.scalar.activation(act_f[:, s, :], bank[b][:, 0:T], ACT.Silu).then_inc(ff_act, 1)
                        else:
                            act.wait_ge(pads_ready, 1)
                            nc.scalar.copy(gpad[:, s, 1:T + 1], bank[b][:, T:2 * T]).then_inc(ff_pad, 1)

                    def gelu(s):
                        act.wait_ge(ff_cv, 6 * i + 3 * (s + 1))
                        nc.scalar.activation(act_f[:, s, :], cv[:, s, 2, :], ACT.Gelu, bias=taps[:, s, 3:4])\
                            .then_inc(ff_act, 1)

                    def high(s):
                        act.wait_ge(ff_mul, 2 * i + (g0 + s + 3))
                        nc.scalar.copy(g_hi[:, s, :], gate_f[:, s, :]).then_inc(ff_hi, 1)

                    hi(4)
                    hi(5)
                    activate(0)
                    hi(6, splits_on)
                    if layer == 2:
                        gelu(0)
                    hi(7, splits_on)
                    high(0)
                    if layer < 2:
                        ada_copy(i + ada_in_loop(layer))
                    activate(1)
                    hi(8, splits_on)
                    if layer == 2:
                        gelu(1)
                    hi(9, splits_on)
                    high(1)

                with act.Fori(0, FT // 2 - (layer == 2)) as i:
                    turn(i)
                if layer == 2:
                    turn(FT // 2 - 1, splits_on=False)
                hi_next[0] = w0 + 3 * FT + LEAD

            act.wait_ge(s_par, 16)
            nc.scalar.activation(cs[:].rearrange("p l k c -> p (l k c)"), pc("c", 0, LAYERS * KT * 2), ACT.Silu)\
                .then_inc(cs_ready, 1)
            for g in range(4):
                ada_copy(g)
            split_to(2)
            norm(0)
            norm(1)
            for j in range(N_IN0):
                split_to(W_IN0 + j + LEAD)
                b = wait_tile(act, ("in0", j))
                if j == 2:
                    nc.scalar.activation(kr_sq, b[:, :], ACT.Square).then_inc(krsq_ready, 1)
                else:
                    dst, n = ((ckv[:, j, :], 2 * T) if j < 2 else (cq[:, j - 3, :], T) if j < 6
                              else (fu[:, j - 6, :], T))
                    nc.scalar.copy(dst, b[:, 0:n]).then_inc(lat_ready, 1)
                if j < 8:
                    ada_copy(4 + j)
            split_to(W_UV)
            lsq = sq[:, :, :].rearrange("p k t -> p (k t)")
            act.wait_ge(lat_ready, 5)
            nc.scalar.activation(lsq[:, 0:1024], ckv.rearrange("p k t -> p (k t)"), ACT.Square).then_inc(lsq_ready, 1)
            nc.scalar.activation(lsq[:, 1024:1792], cq.rearrange("p k t -> p (k t)"), ACT.Square).then_inc(lsq_ready, 1)
            root("kv", KVL_T * P)
            root("ql", QL_T * P)
            for g in range(FN_T):
                b = wait_tile(act, ("dft1", g))
                nc.scalar.copy(f1[:, g, :, :].rearrange("p u c -> p (u c)"), b[:, :]).then_inc(f1_ready, 1)
            for k in range(KVL_T):
                act.wait_ge(ltmp_ready, k + 1)
                nc.scalar.copy(h_hi[:, 2 * k:2 * k + 2, T:2 * T],
                               tmp[:, 2 * k:2 * k + 2, :]).then_inc(lhi_ready, 1)
            for k in range(QL_T):
                act.wait_ge(ltmp_ready, KVL_T + k + 1)
                nc.scalar.copy(h_hi[:, 4 + k, T:2 * T], tmp[:, 4 + k, :]).then_inc(lhi_ready, 1)
            for g in range(FN_T):
                b = wait_tile(act, ("dft2", g))
                nc.scalar.copy(h_hi[:, 4 + g, 0:T], b[:, 0:T]).then_inc(o_hi, 1)
            for u in range(8):
                b = wait_tile(act, ("pj", u))
                nc.scalar.activation(usq[:, u % 2, :], b[:, :], ACT.Square).then_inc(usq_ready, 1)
            root("mq", 1, eps_q)
            root("mk", QK)
            for t in range(4):
                b = wait_tile(act, ("v0", t))
                nc.scalar.copy(vals0[:, t, :], b[:, :]).then_inc(v_ready, 1)
            split_to(W_OUT0 + LEAD - 1)
            mq0 = STATS["mq"][0]
            attention("mla", MLA_H, 0, 4, lambda i: stat[:, mq0 + i:mq0 + i + 1])
            act.dma_start(ctxT, ctx2_in).then_inc(s_ctx, 16)
            split_to(W_FF0 + LEAD - 1)
            norm(2)
            ffn(0)
            norm(3)
            for j in range(N_IN1):
                split_to(W_IN1 + j + LEAD)
                if j < 8 and j % 2 == 0:
                    b = wait_tile(act, ("in1", j))
                    if j >= 4:
                        act.wait_ge(conf_ready, j // 2 - 1)
                    nc.scalar.activation(sgate[:, j // 2 % 2, :], b[:, 0:T], ACT.Sigmoid).then_inc(sg_ready, 1)
                elif 8 <= j < 16 and j % 2 == 0:
                    b = wait_tile(act, ("in1", j))
                    g = (j - 8) // 2
                    act.wait_ge(conf_ready, 4 if g < 2 else 4 + g - 1)
                    nc.scalar.copy(sgate[:, g % 2, :], b[:, 0:T]).then_inc(scc_ready, 1)
                elif j >= 16:
                    g = j - 16
                    act.wait_ge(sc_out, g + 1)
                    nc.scalar.copy(h_hi[:, 4 + g, 0:T], sacc[:, g, :]).then_inc(o_hi, 1)
            split_to(W_OUT1 + LEAD)
            ada_copy(23)
            for half in range(2):
                g = 2 * half
                act.wait_ge(cen_ready, half + 1)
                nc.scalar.activation(csq[:, g:g + 2, :], ccen[:, g:g + 2, :], ACT.Square).then_inc(csq_ready, 1)
            root("conf", P)
            for g in range(CG):
                act.wait_ge(cn_ready, g // 2 + 1)
                nc.scalar.activation(cacc[:, g, :], ccen[:, g, :], ACT.Silu, bias=pc("ln_b", g), scale=pc("ln_g", g))\
                    .then_inc(conf_out, 1)
            for g in range(CG):
                act.wait_ge(conf_out, g + 1)
                nc.scalar.copy(h_hi[:, g, 0:T], cacc[:, g, :]).then_inc(o_hi, 1)
            split_to(W_FF1 + LEAD - 1)
            norm(4)
            ffn(1)
            norm(5)
            norm(6)
            for j in range(17):
                if j < 16:
                    split_to(W_K2 + j + LEAD)
                    b = wait_tile(act, ("qk", j))
                    n = 2 * T if j < 8 else T
                    nc.scalar.activation(nsq[:, j % 2, 0:n], b[:, 0:n], ACT.Square).then_inc(usq_ready, 1)
                if j:
                    root(("qk", j - 1), NA_D)
            for half in range(2):
                split_to(W_V2 + 4 * half + 3 + LEAD - 1)
                for t in range(4):
                    b = wait_tile(act, ("v2", half, t))
                    nc.scalar.copy(vals[:, t, half * 512:(half + 1) * 512], b[:, :]).then_inc(v_ready, 1)
            split_to(W_OUT2 + LEAD - 1)
            ada_copy(35)
            attention("na", NA_H, 16, 16, lambda i: 1.0)
            split_to(W_FF2 + LEAD - 1)
            norm(7)
            ffn(2)

        @block.vector
        def _(dve):
            lo_next = [0]
            seq = [0]
            heads_made = [0]
            ada_made = [0]

            def step(ins):
                seq[0] += 1
                ins.then_inc(dve_seq, 1)
                dve.wait_ge(dve_seq, seq[0])

            def split_lo(w, s):
                dve.wait_ge(hi_done, w + 1)
                nc.vector.tensor_tensor(w_lo[:, s, :], w_raw[:, s, :], w_hi[:, s, :].bitcast(fp), SUB)\
                    .then_inc(split_done, 1)

            def split_to(w):
                while lo_next[0] <= min(w, N_W - 1):
                    n = lo_next[0]
                    split_lo(n, n % RING)
                    lo_next[0] += 1

            def ada_take(g, layer, first):
                dve.wait_ge(ada_turned, g + 1)
                at = PARAMS["ada_b"][0]
                mflat = mods[:].rearrange("p l m c -> p (l m) c")
                if isinstance(g, int):
                    dst, b = mflat[:, AGRP * g:AGRP * (g + 1), :], par[:, at + AGRP * g:at + AGRP * (g + 1)]
                else:
                    dst, b = mflat[:, bass.ds(AGRP * g, AGRP), :], par[:, bass.ds(AGRP * g + at, AGRP)]
                nc.vector.tensor_tensor(dst, bank[6][:, 0:2 * AGRP].rearrange("p (m c) -> p m c", c=2),
                                        b.unsqueeze(2).broadcast_to([P, AGRP, 2]), ADD).then_inc(mod_ready, 1)

            def invert(name):
                c0, c1 = STATS[name]
                dve.wait_ge(root_ready, STAT_ORDER.index(name) + 1)
                nc.vector.reciprocal(stat[:, c0:c1], stat[:, c0:c1]).then_inc(inv_ready, 1)

            def norm(n):
                src, c0, col, layer, which = NORMS[n]
                v = ctxT if src == "c" else xT
                m0 = 3 * KT * which
                dve.wait_ge(mod_ready, MOD_GROUPS[n])
                step(nc.vector.scalar_tensor_tensor(
                    out=gain[:], in0=mods[:, layer, m0 + KT:m0 + 2 * KT, col], scalar=1.0,
                    in1=pc("norm2" if which else "norm1", KT * layer, KT), op0=ADD, op1=MUL))
                if n == 0:
                    dve.wait_ge(s_ctx, 16)
                if n == 1:
                    dve.wait_ge(s_x, 16)
                invert(("norm", n))
                inv = wait_tile(dve, ("inv", n))
                for k in range(KT):
                    nc.vector.scalar_tensor_tensor(out=tmp[:, k, :], in0=v[:, k, :], scalar=gain[:, k:k + 1],
                                                   in1=inv[:, 0:T], op0=MUL, op1=MUL).then_inc(tmp_ready, 1)
                for k in range(KT):
                    dve.wait_ge(hhi_ready, KT * n + k + 1)
                    nc.vector.scalar_tensor_tensor(
                        out=h_lo[:, k, c0:c0 + T], in0=tmp[:, k, :], scalar=mods[:, layer, m0 + k, col:col + 1],
                        in1=h_hi[:, k, c0:c0 + T].bitcast(fp), op0=ADD, op1=SUB).then_inc(hlo_ready, 1)

            def attention(name, heads, at0, o0):
                def maximum(i):
                    b = wait_tile(dve, (name, "sc", i))
                    if name == "na":
                        h, t = i // 2, i % 2
                        if t == 0:
                            dve.wait_ge(bias_ready, h + 1)
                        m0 = 3 + 2 * t
                        ins = nc.vector.tensor_tensor(
                            b[:, T:2 * T].rearrange("p (r c) -> p r c", r=ROWS),
                            b[:, T:2 * T].rearrange("p (r c) -> p r c", r=ROWS),
                            bias[:, h % 3, :, m0 - ROWS + 1:m0 + 1][:, :, ::-1].rearrange("p c r -> p r c"), ADD)
                        step(ins)
                        if t == 1:
                            dve.sem_inc(bias_used, 1)
                        nc.vector.tensor_reduce(nmax[:, i:i + 1], b[:, :], AX.X, ALU.max, negate=True)\
                            .then_inc(nmax_ready, 1)
                    else:
                        step(nc.vector.tensor_reduce(nmax[:, i:i + 1], b[:, :], AX.X, ALU.max, negate=True))
                        c = STATS["mq"][0] + i
                        nc.vector.tensor_tensor(nmax[:, i:i + 1], nmax[:, i:i + 1], stat[:, c:c + 1], MUL)\
                            .then_inc(nmax_ready, 1)

                def out_lo(p):
                    b = wait_tile(dve, (name, "o", p))
                    dve.wait_ge(o_hi, o0 + p + 1)
                    nc.vector.tensor_tensor(h_lo[:, p, 0:T], b[:, 0:T], h_hi[:, p, 0:T].bitcast(fp), SUB)\
                        .then_inc(o_lo, 1)

                maximum(0)
                for i in range(2 * heads):
                    if i + 1 < 2 * heads:
                        maximum(i + 1)
                    dve.wait_ge(exp_ready, at0 + i + 1)
                    step(nc.vector.reciprocal(rinv[:, i:i + 1], rsum[:, i:i + 1]))
                    nc.vector.tensor_scalar(prob[:, i % 2, :], prob[:, i % 2, :], rinv[:, i:i + 1], None, MUL)\
                        .then_inc(prob_ready, 1)
                    if i >= 5 and i % 4 == 1:
                        out_lo((i - 5) // 4)
                out_lo(heads // 2 - 1)

            def project_out(layer, w0):
                dve.wait_ge(mod_ready, 12 * layer + 6)
                for j in range(KT):
                    split_to(w0 + j + LEAD)
                    b = wait_tile(dve, ("out", layer, j))
                    nc.vector.scalar_tensor_tensor(out=xT[:, j, :], in0=b[:, 0:T],
                                                   scalar=mods[:, layer, 2 * KT + j, 0:1], in1=xT[:, j, :],
                                                   op0=MUL, op1=ADD).then_inc(x_updated, 1)

            def ffn(layer):
                w0, g0 = (W_FF0, W_FF1, W_FF2)[layer], FT * layer
                split_to(w0 + LEAD - 1)
                def turn(i, splits_on=True):
                    def lo(j, on=True):
                        if on:
                            split_lo(3 * 2 * i + (w0 + j), (w0 + j) % RING)

                    def convolve(s):
                        at = PARAMS["ff_conv"][0]
                        nc.vector.tensor_copy(taps[:, s, :], par[:, bass.ds(8 * i + (at + 4 * s), 4)])\
                            .then_inc(dve_seq, 1)
                        dve.wait_ge(dve_seq, 2 * i + (seq[0] + s + 1))
                        dve.wait_ge(ff_pad, 2 * i + (s + 1))
                        nc.vector.tensor_scalar(cv[:, s, 0, :], gpad[:, s, 0:T], taps[:, s, 0:1], None, MUL)\
                            .then_inc(ff_cv, 1)
                        for m in (1, 2):
                            dve.wait_ge(ff_cv, 6 * i + (3 * s + m))
                            nc.vector.scalar_tensor_tensor(out=cv[:, s, m, :], in0=gpad[:, s, m:m + T],
                                                           scalar=taps[:, s, m:m + 1], in1=cv[:, s, m - 1, :],
                                                           op0=MUL, op1=ADD).then_inc(ff_cv, 1)

                    def product(s):
                        b = tiles[("up", layer, s)][0]
                        half = T if layer < 2 else 0
                        dve.wait_ge(ff_act, 2 * i + (g0 + s + 1))
                        nc.vector.tensor_tensor(gate_f[:, s, :], act_f[:, s, :], bank[b][:, half:half + T], MUL)\
                            .then_inc(ff_mul, 1)

                    def low(s):
                        dve.wait_ge(ff_hi, 2 * i + (g0 + s + 1))
                        nc.vector.tensor_tensor(g_lo[:, s, :], gate_f[:, s, :], g_hi[:, s, :].bitcast(fp), SUB)\
                            .then_inc(ff_lo, 1)

                    lo(4)
                    lo(5)
                    if layer == 2:
                        convolve(0)
                    lo(6, splits_on)
                    product(0)
                    lo(7, splits_on)
                    low(0)
                    if layer == 2:
                        convolve(1)
                    lo(8, splits_on)
                    product(1)
                    lo(9, splits_on)
                    low(1)
                    if layer < 2:
                        ada_take(i + ada_in_loop(layer), None, None)

                with dve.Fori(0, FT // 2 - (layer == 2)) as i:
                    turn(i)
                if layer == 2:
                    turn(FT // 2 - 1, splits_on=False)
                if layer == 2:
                    seq[0] += FT
                lo_next[0] = w0 + 3 * FT + LEAD
                dve.wait_ge(mod_ready, 12 * (layer + 1))
                for b4 in range(4):
                    b = wait_tile(dve, ("acc", layer, b4))
                    for e in range(2):
                        j = 2 * b4 + e
                        nc.vector.scalar_tensor_tensor(out=xT[:, j, :], in0=b[:, e * T:(e + 1) * T],
                                                       scalar=mods[:, layer, 5 * KT + j, 0:1], in1=xT[:, j, :],
                                                       op0=MUL, op1=ADD).then_inc(x_updated, 1)

            nc.vector.memset(bank[6][:, :], 0.0).then_inc(ada_cleared, 1)
            dve.sem_inc(ff_mul, 2)
            dve.wait_ge(s_par, 16)
            for g in range(4):
                ada_take(g, 0, 0)
            split_to(2)
            norm(0)
            norm(1)
            def rotate(dst, b, gains, n):
                shape = lambda a: a.rearrange("p (e t) -> p e t", t=T)
                table = lambda name, lo: cc(name)[lo:lo + ROPE_D, :].unsqueeze(1).broadcast_to([ROPE_D, n // T, T])
                r1, r2 = rot1[NOPE:QK, 0:n], rot2[NOPE:QK, 0:n]
                yield nc.vector.scalar_tensor_tensor(out=shape(r2), in0=shape(b), scalar=gains, in1=table("sin", QK),
                                                     op0=MUL, op1=MUL)
                step(nc.vector.tensor_tensor(shape(r1), shape(dst), table("cos", NOPE), MUL))
                yield nc.vector.tensor_tensor(dst, r1, r2, ADD)

            for j in range(N_IN0):
                split_to(W_IN0 + j + LEAD)
                if j == 2:
                    b = wait_tile(dve, ("in0", j))
                    dve.wait_ge(krsq_ready, 1)
                    dve.wait_ge(s_con, 16)
                    step(nc.vector.tensor_scalar(rope_k[NOPE:QK, :], b[NOPE:QK, :], pc("k_norm")[NOPE:QK, :], None, MUL))
                    ops = rotate(rope_k[NOPE:QK, T:2 * T], b[QK:P, T:2 * T], pc("k_norm")[QK:P, :], T)
                    next(ops).then_inc(kr_taken, 1)
                    dve.wait_ge(kr_taken, 1)
                    step(next(ops))
                if 1 <= j < 9:
                    ada_take(3 + j, 0, 0)
            split_to(W_UV)
            invert("kv")
            invert("ql")
            inv = wait_tile(dve, ("inv", "kv"))
            for k in range(KVL_T):
                nc.vector.scalar_tensor_tensor(
                    out=tmp[:, 2 * k:2 * k + 2, :].rearrange("p a t -> p (a t)"), in0=ckv[:, k, :],
                    scalar=pc("kv_ln", k), in1=inv[:, :], op0=MUL, op1=MUL).then_inc(ltmp_ready, 1)
            inv = wait_tile(dve, ("inv", "ql"))
            for k in range(QL_T):
                nc.vector.scalar_tensor_tensor(out=tmp[:, 4 + k, :], in0=cq[:, k, :], scalar=pc("q_ln", k),
                                               in1=inv[:, 0:T], op0=MUL, op1=MUL).then_inc(ltmp_ready, 1)
            for k in range(KVL_T):
                dve.wait_ge(lhi_ready, k + 1)
                nc.vector.tensor_tensor(h_lo[:, 2 * k:2 * k + 2, T:2 * T], tmp[:, 2 * k:2 * k + 2, :],
                                        h_hi[:, 2 * k:2 * k + 2, T:2 * T].bitcast(fp), SUB).then_inc(llo_ready, 1)
            for k in range(QL_T):
                dve.wait_ge(lhi_ready, KVL_T + k + 1)
                nc.vector.tensor_tensor(h_lo[:, 4 + k, T:2 * T], tmp[:, 4 + k, :],
                                        h_hi[:, 4 + k, T:2 * T].bitcast(fp), SUB).then_inc(llo_ready, 1)
            for g in range(FN_T):
                b = wait_tile(dve, ("dft2", g))
                dve.wait_ge(o_hi, g + 1)
                nc.vector.tensor_tensor(h_lo[:, 4 + g, 0:T], b[:, 0:T], h_hi[:, 4 + g, 0:T].bitcast(fp), SUB)\
                    .then_inc(o_lo, 1)
            for u in range(4):
                b = wait_tile(dve, ("pj", u))
                dve.wait_ge(usq_ready, u + 1)
                q = querT[:, 2 * u:2 * u + 2, :].rearrange("p a t -> p (a t)")
                step(nc.vector.tensor_scalar(q[0:QK, :], b[0:QK, :], pc("q_norm")[0:QK, :], None, MUL))
                ops = rotate(q[NOPE:QK, :], b[QK:P, :], pc("q_norm")[QK:P, :], 2 * T)
                next(ops).then_inc(unit_ready, 1)
                dve.wait_ge(unit_ready, u + 1)
                step(next(ops))
            for u in range(4, 8):
                b = wait_tile(dve, ("pj", u))
                dve.wait_ge(usq_ready, u + 1)
                for e in range(2):
                    rows = slice(e * NOPE, (e + 1) * NOPE)
                    ins = nc.vector.tensor_scalar(keysT[0:NOPE, 2 * (u - 4) + e, :], b[rows, :], pc("k_nope")[rows, :],
                                                  None, MUL)
                ins.then_inc(unit_ready, 1)
            invert("mq")
            invert("mk")
            dve.wait_ge(unit_ready, 8)
            for h in range(MLA_H):
                inv = wait_tile(dve, ("inv", "mk", h))
                nc.vector.tensor_tensor(keysT[0:NOPE, h, :], keysT[0:NOPE, h, :], inv[0:NOPE, :], MUL)
                nc.vector.tensor_tensor(keysT[NOPE:QK, h, :], rope_k[NOPE:QK, :], inv[NOPE:QK, :], MUL)\
                    .then_inc(head_ready, 1)
            split_to(W_OUT0 + LEAD - 1)
            attention("mla", MLA_H, 0, 4)
            project_out(0, W_OUT0)
            norm(2)
            ffn(0)
            norm(3)
            tap_list = [(g, k) for g in range(CG) for k in range(CONF_K)]
            taps_done = [0]

            def conv_taps(n):
                for g, k in tap_list[taps_done[0]:taps_done[0] + n]:
                    src = confp[:, g, 1 + k:1 + k + T]
                    wk = pc("conf_dw", CONF_K * g + k)
                    if k == 0:
                        ins = nc.vector.tensor_scalar(cacc[:, g, :], src, wk, pc("conf_b", g), MUL, ADD)
                    else:
                        ins = nc.vector.scalar_tensor_tensor(out=cacc[:, g, :], in0=src, scalar=wk,
                                                             in1=cacc[:, g, :], op0=MUL, op1=ADD)
                    step(ins)
                taps_done[0] = min(len(tap_list), taps_done[0] + n)

            step(nc.vector.memset(confp, 0.0))
            step(nc.vector.memset(scp, 0.0))
            for j in range(N_IN1):
                split_to(W_IN1 + j + LEAD)
                g = j // 2
                if j < 8 and j % 2:
                    b = wait_tile(dve, ("in1", j))
                    dve.wait_ge(sg_ready, g + 1)
                    nc.vector.tensor_tensor(confp[:, g, 16:16 + T], b[:, 0:T], sgate[:, g % 2, :], MUL)\
                        .then_inc(conf_ready, 1)
                    dve.wait_ge(conf_ready, g + 1)
                elif 8 <= j < 16 and j % 2:
                    g -= 4
                    b = wait_tile(dve, ("in1", j))
                    dve.wait_ge(scc_ready, g + 1)
                    nc.vector.tensor_tensor(scp[:, g, 1:1 + T], b[:, 0:T], sgate[:, g % 2, :], MUL)\
                        .then_inc(conf_ready, 1)
                    dve.wait_ge(conf_ready, 4 + g + 1)
                    for k in range(SC_K):
                        src = scp[:, g, k:k + T]
                        wk = pc("sc_dw", SC_K * g + k)
                        if k == 0:
                            step(nc.vector.tensor_scalar(sacc[:, g, :], src, wk, None, MUL))
                        else:
                            step(nc.vector.scalar_tensor_tensor(out=sacc[:, g, :], in0=src, scalar=wk,
                                                                in1=sacc[:, g, :], op0=MUL, op1=ADD))
                elif j >= 16:
                    g = j - 16
                    b = wait_tile(dve, ("in1", j))
                    nc.vector.tensor_tensor(sacc[:, g, :], b[:, 0:T], sacc[:, g, :], MUL).then_inc(sc_out, 1)
                if 2 <= j:
                    conv_taps(min(7, CONF_K * min(CG, (j + 1) // 2) - taps_done[0]))
            conv_taps(len(tap_list) - taps_done[0])
            dve.sem_inc(conf_ready, 1)
            split_to(W_OUT1 + LEAD)
            for g in range(CG):
                dve.wait_ge(o_hi, 8 + g + 1)
                nc.vector.tensor_tensor(h_lo[:, 4 + g, 0:T], sacc[:, g, :], h_hi[:, 4 + g, 0:T].bitcast(fp), SUB)\
                    .then_inc(o_lo, 1)
            for half in range(2):
                b = wait_tile(dve, ("csum", half))
                g = 2 * half
                nc.vector.scalar_tensor_tensor(
                    out=ccen[:, g:g + 2, :].rearrange("p g t -> p (g t)"), in0=b[:, :], scalar=-1.0 / P,
                    in1=cacc[:, g:g + 2, :].rearrange("p g t -> p (g t)"), op0=MUL, op1=ADD).then_inc(cen_ready, 1)
            invert("conf")
            for half in range(2):
                g = 2 * half
                inv = wait_tile(dve, ("inv", "conf", half))
                cg = ccen[:, g:g + 2, :].rearrange("p g t -> p (g t)")
                nc.vector.tensor_tensor(cg, cg, inv[:, :], MUL).then_inc(cn_ready, 1)
            for g in range(CG):
                dve.wait_ge(o_hi, 12 + g + 1)
                nc.vector.tensor_tensor(h_lo[:, g, 0:T], cacc[:, g, :], h_hi[:, g, 0:T].bitcast(fp), SUB)\
                    .then_inc(o_lo, 1)
            ada_take(23, 0, 0)
            project_out(1, W_OUT1)
            norm(4)
            ffn(1)
            norm(5)
            norm(6)
            for j in range(17):
                if j < 16:
                    split_to(W_K2 + j + LEAD)
                    b = wait_tile(dve, ("qk", j))
                    n = 2 * T if j < 8 else T
                    dst = keysT[:, j, :] if j < 8 else querT[:, j - 8, :]
                    dve.wait_ge(usq_ready, 8 + j + 1)
                    nc.vector.tensor_scalar(dst, b[:, 0:n], pc("na_k" if j < 8 else "na_q"), None, MUL)\
                        .then_inc(unit_ready, 1)
                    dve.wait_ge(unit_ready, 8 + j + 1)
                if j:
                    i = j - 1
                    n = 2 * T if i < 8 else T
                    dst = keysT[:, i, :] if i < 8 else querT[:, i - 8, :]
                    invert(("qk", i))
                    inv = wait_tile(dve, ("inv", "qk", i))
                    nc.vector.scalar_tensor_tensor(out=dst, in0=dst, scalar=1.0 if i < 8 else NA_D ** -0.5,
                                                   in1=inv[:, 0:n], op0=MUL, op1=MUL).then_inc(head_ready, 1)
            for half in range(2):
                split_to(W_V2 + 4 * half + 3 + LEAD - 1)
            ada_take(35, 0, 0)
            split_to(W_OUT2 + LEAD - 1)
            attention("na", NA_H, 16, 16)
            project_out(2, W_OUT2)
            nc.vector.memset(gpad, 0.0).then_inc(pads_ready, 1)
            norm(7)
            ffn(2)

        @block.tensor
        def _(pe):
            def split3(out, a_hi, a_lo, b_hi, b_lo, start, stop):
                nc.tensor.matmul(out, a_hi, b_hi, start=start, stop=False)
                nc.tensor.matmul(out, a_hi, b_lo, start=False, stop=False)
                return nc.tensor.matmul(out, a_lo, b_hi, start=False, stop=stop)

            def wtile(w, c0, n):
                return w_hi[:, w % RING, c0:c0 + n], w_lo[:, w % RING, c0:c0 + n]

            def split_ready(w):
                pe.wait_ge(split_done, w + 1)

            def ada_rows(g):
                if not isinstance(g, int) or g:
                    pe.wait_ge(mod_ready, g)
                else:
                    pe.wait_ge(ada_cleared, 1)
                for k in range(KT):
                    s, part = k // 2, k % 4
                    if k % 2 == 0:
                        pe.wait_ge(a_loaded[s], 16 * g + 16)
                    ins = nc.tensor.matmul(bank[6][32 * part:32 * part + 2, :], cs[:, ada_layer[0], k, :],
                                           a_raw[:, s, (k % 2) * 512:(k % 2 + 1) * 512], start=(k < 4), stop=(k >= 4),
                                           tile_position=(0, 32 * part))
                    if k % 2:
                        ins.then_inc(a_used, 1)

            def ada_columns(g):
                pe.wait_ge(ada_copied, g + 1)
                for m in range(AGRP):
                    ins = nc.tensor.matmul(bank[6][:, 2 * m:2 * m + 2], ada_s[:, m * P:(m + 1) * P], cc("of_cond"),
                                           start=True, stop=True)
                ins.then_inc(ada_turned, 1)

            ada_layer = [0]

            def sums(name, tiles_of, select):
                b = write_tile(pe, ("sum", name))
                n = select.shape[1]
                for t, parts in enumerate(tiles_of):
                    for k, part in enumerate(parts):
                        ins = nc.tensor.matmul(b[:, t * n:(t + 1) * n], part, select, start=(k == 0),
                                               stop=(k == len(parts) - 1))
                ins.then_inc(full_of(("sum", name)), 1)

            def spread(name, cols, m=P):
                b = write_tile(pe, name)
                for t, c in enumerate(cols):
                    ins = nc.tensor.matmul(b[0:m, t * P:(t + 1) * P], c, ident, start=True, stop=True)
                ins.then_inc(full_of(name), 1)

            def column(c, m=P):
                return stat[:, c:c + 1].broadcast_to([P, m])

            def norm(n):
                b = write_tile(pe, ("sum", ("norm", n)))
                for t in range(2):
                    for k in range(KT):
                        if t == 0 and k % 4 == 0:
                            pe.wait_ge(sq_ready, 2 * n + k // 4 + 1)
                        ins = nc.tensor.matmul(b[:, t:t + 1], sq[:, k, t * P:(t + 1) * P], ones[:, 0:1],
                                               start=(k == 0), stop=(k == KT - 1))
                ins.then_inc(full_of(("sum", ("norm", n))), 1)
                pe.wait_ge(inv_ready, STAT_ORDER.index(("norm", n)) + 1)
                c0 = STATS["norm", n][0]
                spread(("inv", n), [column(c0), column(c0 + 1)])

            def project(name, w, rhs, n):
                b = write_tile(pe, name)
                split_ready(w)
                for k in range(KT):
                    a = wtile(w, k * P, P)
                    ins = split3(b[:, 0:n], a[0], a[1], rhs(h_hi, k), rhs(h_lo, k), k == 0, k == KT - 1)
                ins.then_inc(w_used, 1)

            def both(h, k):
                return h[:, k, :]

            def xs(h, k):
                return h[:, k, T:2 * T]

            def mixed(h, k):
                return h[:, k, 0:T]

            def attention(name, heads, at0, ready0, rows, values):
                def scores(i):
                    h, t = i // 2, i % 2
                    b = write_tile(pe, (name, "sc", i))
                    q, k = rows(h)
                    nc.tensor.matmul(b[:, :], q[:, t * P:(t + 1) * P], k, start=True, stop=True)\
                        .then_inc(full_of((name, "sc", i)), 1)

                def turn(i):
                    b = write_tile(pe, (name, "tr", i))
                    pe.wait_ge(prob_ready, at0 + i + 1)
                    for kt in range(4):
                        ins = nc.tensor.transpose(b[:, kt * P:(kt + 1) * P], prob[:, i % 2, kt * P:(kt + 1) * P], ident)
                    ins.then_inc(full_of((name, "tr", i)), 1)

                def pv(h):
                    p, e = h // 2, h % 2
                    pe.wait_ge(pT_ready, at0 + 2 * h + 2)
                    b = write_tile(pe, (name, "o", p)) if e == 0 else bank[tiles[(name, "o", p)][0]]
                    for kt in range(4):
                        ins = nc.tensor.matmul(b[e * VH:(e + 1) * VH, 0:T], values(h, kt), probT[:, h % 2, kt, :],
                                               start=(kt == 0), stop=(kt == 3))
                    ins.then_inc(pv_done, 1)
                    if e:
                        pe.wait_ge(pv_done, at0 // 2 + h + 1)
                        pe.sem_inc(full_of((name, "o", p)), 1)

                scores(0)
                for i in range(2 * heads):
                    if i + 1 < 2 * heads:
                        scores(i + 1)
                    turn(i)
                    if i >= 2 and i % 2 == 0:
                        pv(i // 2 - 1)
                pv(heads - 1)

            def project_out(layer, w0, o_total):
                for j in range(KT):
                    if j == 0:
                        pe.wait_ge(o_lo, o_total)
                    project(("out", layer, j), w0 + j, mixed, T)

            def ffn(layer):
                w0, g0 = (W_FF0, W_FF1, W_FF2)[layer], FT * layer
                if layer == 0:
                    pe.wait_ge(const_ready, 3)
                for b4 in range(4):
                    b = write_tile(pe, ("acc", layer, b4))
                    for q4 in range(4):
                        nc.tensor.matmul(b[:, q4 * P:(q4 + 1) * P], zero_r[:, :], zero_r[:, :], start=(q4 == 0),
                                         stop=False)
                for s in range(2):
                    write_tile(pe, ("up", layer, s))
                pe.wait_ge(hlo_ready, KT * ((2, 4, 7)[layer] + 1))
                def turn(i, splits_on=True):
                    def up(s):
                        b = tiles[("up", layer, s)][0]
                        pe.wait_ge(ff_mul, 2 * i + (g0 + s + 1))
                        for e in range(2):
                            w = w0 + 2 * s + e
                            pe.wait_ge(split_done, 6 * i + (w + 1))
                            for k in range(KT):
                                a = wtile(w, k * P, P)
                                ins = split3(bank[b][:, e * T:(e + 1) * T], a[0], a[1], xs(h_hi, k), xs(h_lo, k),
                                             k == 0, k == KT - 1)
                            ins.then_inc(w_used, 1)

                    def down(s):
                        w = w0 + 4 + s
                        pe.wait_ge(split_done, 6 * i + (w + 1))
                        pe.wait_ge(ff_lo, 2 * i + (g0 + s + 1))
                        for j in range(KT):
                            b = bank[tiles[("acc", layer, j // 2)][0]]
                            a = wtile(w, j * P, P)
                            out = b[:, (j % 2) * T:(j % 2 + 1) * T]
                            ins = split3(out, a[0], a[1], g_hi[:, s, :], g_lo[:, s, :], False, False)
                        ins.then_inc(w_used, 1)

                    up(0)
                    if layer < 2:
                        ada_layer[0] = layer + 1
                        ada_rows(i + ada_in_loop(layer))
                    up(1)
                    if layer < 2:
                        ada_columns(i + ada_in_loop(layer))
                    down(0)
                    down(1)

                with pe.Fori(0, FT // 2 - (layer == 2)) as i:
                    turn(i)
                if layer == 2:
                    turn(FT // 2 - 1, splits_on=False)
                for b4 in range(4):
                    name = ("acc", layer, b4)
                    for q4 in range(4):
                        ins = nc.tensor.matmul(bank[tiles[name][0]][:, q4 * P:(q4 + 1) * P], zero_r[:, :], zero_r[:, :],
                                               start=False, stop=(q4 == 3))
                    ins.then_inc(full_of(name), 1)

            pe.wait_ge(cs_ready, 1)
            pe.wait_ge(s_con, 16)
            for g in range(4):
                ada_rows(g)
                ada_columns(g)
            norm(0)
            norm(1)
            pe.wait_ge(hlo_ready, 2 * KT)
            for j in range(N_IN0):
                if j < 3:
                    project(("in0", j), W_IN0 + j, both, 2 * T)
                else:
                    project(("in0", j), W_IN0 + j, xs, T)
                if 1 <= j < 9:
                    ada_columns(3 + j)
                if j < 8:
                    ada_rows(4 + j)
            lsq = sq[:, :, :].rearrange("p k t -> p (k t)")
            pe.wait_ge(lsq_ready, 1)
            sums("kv", [[lsq[:, k * 512 + t * P:k * 512 + (t + 1) * P] for k in range(KVL_T)] for t in range(4)],
                 ones[:, 0:1])
            pe.wait_ge(lsq_ready, 2)
            sums("ql", [[lsq[:, 1024 + k * T + t * P:1024 + k * T + (t + 1) * P] for k in range(QL_T)]
                        for t in range(2)], ones[:, 0:1])
            pe.wait_ge(lat_ready, N_IN0 - 1)
            for g in range(FN_T):
                b = write_tile(pe, ("dft1", g))
                for t in range(2):
                    ins = nc.tensor.matmul(b[:, t * T:(t + 1) * T], fu[:, g, t * P:(t + 1) * P], cc("dft_c"),
                                           start=True, stop=True)
                ins.then_inc(full_of(("dft1", g)), 1)
            pe.wait_ge(inv_ready, STAT_ORDER.index("ql") + 1)
            c0 = STATS["kv"][0]
            spread(("inv", "kv"), [column(c0 + t) for t in range(4)])
            c0 = STATS["ql"][0]
            spread(("inv", "ql"), [column(c0 + t) for t in range(2)])
            for g in range(FN_T):
                b = write_tile(pe, ("dft2", g))
                pe.wait_ge(f1_ready, g + 1)
                n = 0
                for part in range(2):
                    for t in range(2):
                        ins = nc.tensor.matmul(b[:, 0:T], f1[:, g, t, part * P:(part + 1) * P],
                                               cc("dft_n", (2 * part + t) * T, (2 * part + t + 1) * T),
                                               start=(n == 0), stop=(n == 3))
                        n += 1
                ins.then_inc(full_of(("dft2", g)), 1)
            def ckvn(h, k):
                return h[:, 2 * k:2 * k + 2, T:2 * T]

            def unit_products(u):
                b = write_tile(pe, ("pj", u))
                if u < 4:
                    pe.wait_ge(llo_ready, KVL_T + QL_T)
                    for e in range(2):
                        for k in range(QL_T):
                            n = QL_T * (2 * u + e) + k
                            split_ready(W_UQ + n // KT)
                            a = wtile(W_UQ + n // KT, (n % KT) * P, P)
                            ins = split3(b[:, e * T:(e + 1) * T], a[0], a[1], h_hi[:, 4 + k, T:2 * T],
                                         h_lo[:, 4 + k, T:2 * T], k == 0, k == QL_T - 1)
                else:
                    split_ready(W_UK)
                    for k in range(KVL_T):
                        a = wtile(W_UK, ((u - 4) * KVL_T + k) * P, P)
                        ins = split3(b[:, :], a[0], a[1], ckvn(h_hi, k), ckvn(h_lo, k), k == 0, k == KVL_T - 1)
                if u < 7:
                    ins.then_inc(full_of(("pj", u)), 1)
                else:
                    ins.then_inc(w_used, 1)

            def unit_sums(u):
                pe.wait_ge(usq_ready, u + 1)
                if u < 4:
                    b = write_tile(pe, ("sum", "mq")) if u == 0 else bank[tiles["sum", "mq"][0]]
                    for e in range(2):
                        for t in range(2):
                            c = 2 * (2 * u + e) + t
                            ins = nc.tensor.matmul(b[:, c:c + 1], usq[:, u % 2, e * T + t * P:e * T + (t + 1) * P],
                                                   cc("of_query"), start=True, stop=True)
                    if u == 3:
                        ins.then_inc(full_of(("sum", "mq")), 1)
                        pe.wait_ge(full_of(("sum", "mq")), tiles["sum", "mq"][1][1])
                        pe.sem_inc(w_used, N_UQ)
                else:
                    b = bank[tiles["sum", "mk"][0]]
                    if u == 4:
                        write_tile(pe, ("sum", "mk"))
                        pe.wait_ge(krsq_ready, 1)
                        for t in range(4):
                            nc.tensor.matmul(b[:, t * MLA_H:(t + 1) * MLA_H], kr_sq[:, t * P:(t + 1) * P], cc("of_rope"),
                                             start=(t == 0), stop=False)
                    for t in range(4):
                        c = t * MLA_H + 2 * (u - 4)
                        ins = nc.tensor.matmul(b[:, c:c + 2], usq[:, u % 2, t * P:(t + 1) * P], cc("of_pair"),
                                               start=False, stop=(u == 7 and t == 3))
                    if u == 7:
                        ins.then_inc(full_of(("sum", "mk")), 1)

            unit_products(0)
            for u in range(8):
                if u == 3:
                    unit_sums(3)
                    unit_products(4)
                    continue
                if u + 1 < 8:
                    unit_products(u + 1)
                unit_sums(u)
            split_ready(W_UV)
            for t in range(4):
                b = write_tile(pe, ("v0", t))
                for k in range(KVL_T):
                    at = (2 * k + t // 2, T + (t % 2) * P)
                    xh, xl = (h[:, at[0], at[1]:at[1] + P] for h in (h_hi, h_lo))
                    a = wtile(W_UV, k * 512, 512)
                    ins = split3(b[:, :], xh, xl, a[0], a[1], k == 0, k == KVL_T - 1)
                ins.then_inc(full_of(("v0", t)) if t < 3 else w_used, 1)
            pe.wait_ge(inv_ready, STAT_ORDER.index("mk") + 1)
            c0 = STATS["mk"][0]
            for h in range(MLA_H):
                spread(("inv", "mk", h), [column(c0 + t * MLA_H + h, QK) for t in range(4)], QK)
            pe.wait_ge(head_ready, MLA_H)
            pe.wait_ge(v_ready, 4)
            attention("mla", MLA_H, 0, 0, lambda h: (querT[0:QK, h, :], keysT[0:QK, h, :]),
                      lambda h, kt: vals0[:, kt, h * VH:(h + 1) * VH])
            project_out(0, W_OUT0, 8)
            norm(2)
            ffn(0)
            norm(3)
            pe.wait_ge(hlo_ready, 4 * KT)
            for j in range(N_IN1):
                project(("in1", j), W_IN1 + j, xs, T)
            ada_layer[0] = 1
            ada_rows(23)
            ada_columns(23)
            pe.wait_ge(conf_ready, 9)
            for half in range(2):
                b = write_tile(pe, ("csum", half))
                nc.tensor.matmul(b[:, :], ones, cacc[:, 2 * half:2 * half + 2, :].rearrange("p g t -> p (g t)"),
                                 start=True, stop=True).then_inc(full_of(("csum", half)), 1)
            pe.wait_ge(csq_ready, 2)
            sums("conf", [[csq[:, g, t * P:(t + 1) * P]] for g in range(CG) for t in range(2)], ones[:, 0:1])
            pe.wait_ge(inv_ready, STAT_ORDER.index("conf") + 1)
            c0 = STATS["conf"][0]
            for half in range(2):
                spread(("inv", "conf", half), [column(c0 + 4 * half + t) for t in range(4)])
            project_out(1, W_OUT1, 16)
            norm(4)
            ffn(1)
            norm(5)
            norm(6)
            pe.wait_ge(hlo_ready, 7 * KT)
            def spread_qk(i):
                pe.wait_ge(inv_ready, STAT_ORDER.index(("qk", i)) + 1)
                c0 = STATS["qk", i][0]
                b = write_tile(pe, ("inv", "qk", i))
                for t in range(4 if i < 8 else 2):
                    for e in range(2):
                        ins = nc.tensor.matmul(b[e * NA_D:(e + 1) * NA_D, t * P:(t + 1) * P],
                                               column(c0 + 2 * t + e, NA_D), ident, start=True, stop=True)
                ins.then_inc(full_of(("inv", "qk", i)), 1)

            for j in range(17):
                if j < 16:
                    project(("qk", j), W_K2 + j, both if j < 8 else xs, 2 * T if j < 8 else T)
                if j:
                    i = j - 1
                    pe.wait_ge(usq_ready, 8 + i + 1)
                    sums(("qk", i), [[nsq[:, i % 2, t * P:(t + 1) * P]] for t in range(4 if i < 8 else 2)], cc("of_pair"))
                if j > 1:
                    spread_qk(j - 2)
            spread_qk(15)
            for half in range(2):
                banks = [write_tile(pe, ("v2", half, t)) for t in range(4)]
                for q4 in range(4):
                    w = W_V2 + 4 * half + q4
                    split_ready(w)
                    for e in range(2):
                        k = 2 * q4 + e
                        a = wtile(w, e * 512, 512)
                        for t in range(4):
                            ins = split3(banks[t][:, :], h_hi[:, k, t * P:(t + 1) * P], h_lo[:, k, t * P:(t + 1) * P],
                                         a[0], a[1], k == 0, k == KT - 1)
                            if k == KT - 1 and t < 3:
                                ins.then_inc(full_of(("v2", half, t)), 1)
                    ins.then_inc(w_used, 1)
            ada_layer[0] = 2
            ada_rows(35)
            ada_columns(35)
            pe.wait_ge(v_ready, 12)
            pe.wait_ge(head_ready, MLA_H + 16)
            attention("na", NA_H, 16, 0,
                      lambda h: (querT[(h % 2) * NA_D:(h % 2 + 1) * NA_D, h // 2, :],
                                 keysT[(h % 2) * NA_D:(h % 2 + 1) * NA_D, h // 2, :]),
                      lambda h, kt: vals[:, kt, h * NA_D:(h + 1) * NA_D])
            project_out(2, W_OUT2, 24)
            norm(7)
            ffn(2)


def pack_weights(i):
    w = np.zeros((N_W, P, BLK), np.float32)

    def across(at, m, tiles=None):
        n = m.shape[1] // P
        w[at:at + n] = m.reshape(KT, P, n, P).transpose(2, 1, 0, 3).reshape(n, P, BLK)

    def ffn(at, w1, w3, w2):
        b = w[at:at + 3 * FT].reshape(FT // 2, 6, P, BLK)
        for e, m in enumerate((w1, w3)):
            up = m.reshape(KT, P, FT // 2, 2, P).transpose(2, 3, 1, 0, 4).reshape(FT // 2, 2, P, BLK)
            b[:, e], b[:, 2 + e] = up[:, 0], up[:, 1]
        down = w2.reshape(FT // 2, 2, P, BLK)
        b[:, 4], b[:, 5] = down[:, 0], down[:, 1]

    a = i["a_w_in"][0]
    q, kv, kr, fn = np.split(a, [QL_T * P, (QL_T + KVL_T) * P, (QL_T + KVL_T) * P + ROPE_D], axis=1)
    swapped = np.r_[QK - ROPE_D // 2:QK, NOPE:QK - ROPE_D // 2]
    across(W_IN0, np.concatenate([kv, np.zeros((D, NOPE), np.float32), kr, kr[:, swapped - NOPE], q, fn], axis=1))
    uq = i["a_w_uq"][0].reshape(QL_T, P, MLA_H, QK)
    uq = np.concatenate([uq, uq[..., swapped]], axis=-1).transpose(2, 0, 1, 3)
    w[W_UQ:W_UQ + N_UQ] = uq.reshape(N_UQ, KT, P, P).transpose(0, 2, 1, 3).reshape(N_UQ, P, BLK)
    uk = i["a_w_uk"][0].reshape(KVL_T, P, MLA_H // 2, P)
    w[W_UK] = uk.transpose(1, 2, 0, 3).reshape(P, BLK)
    w[W_UV] = i["a_w_uv"][0].reshape(KVL_T, P, 512).transpose(1, 0, 2).reshape(P, BLK)
    across(W_OUT0, i["a_w_out"][0])
    ffn(W_FF0, i["ffn_w1"][0], i["ffn_w3"][0], i["ffn_w2"][0])
    a, gate, sb_, scc, sx = np.split(i["b_w_in"][0], 5, axis=1)

    def woven(u, v):
        return np.stack([u.reshape(D, 4, P), v.reshape(D, 4, P)], axis=2).reshape(D, 8 * P)

    across(W_IN1, np.concatenate([woven(gate, a), woven(scc, sx), sb_], axis=1))
    across(W_OUT1, i["b_w_out"][0])
    ffn(W_FF1, i["ffn_w1"][1], i["ffn_w3"][1], i["ffn_w2"][1])
    q, k, v = np.split(i["l0_na_w_qkv_2"], 3, axis=1)
    across(W_K2, k)
    across(W_Q2, q)
    w[W_V2:W_V2 + 8] = v.reshape(4, 2, P, 2, 512).transpose(3, 0, 2, 1, 4).reshape(8, P, BLK)
    across(W_OUT2, i["l0_na_w_o_2"])
    up = i["l0_ffn_w_up_2"]
    ffn(W_FF2, up[:, :F_FF], up[:, F_FF:], i["l0_ffn_w_down_2"])
    return w


def pack_ada(i):
    m = np.stack([i["ada_w"][0], i["ada_w"][1], i["l0_w_mod_2"]])
    m = m.reshape(LAYERS, AGRP, 2, P, MODS // AGRP, AGRP * P)
    return np.ascontiguousarray(m.transpose(0, 4, 1, 3, 2, 5).reshape(N_A, P, BLK))


def by_partition(v):
    return np.moveaxis(v.reshape(*v.shape[:-1], -1, P), -1, 0).reshape(P, -1)


def pack_params(i):
    t = np.zeros((P, N_PARAMS), np.float32)

    def put(name, a):
        c0, c1 = PARAMS[name]
        assert a.shape[1] == c1 - c0, name
        t[:a.shape[0], c0:c1] = a

    pairs = [(i["c"][0], i["c_ctx"]), (i["c"][0], i["c_ctx"]), (i["c_2"][0], i["c_ctx_2"])]
    c = np.stack([np.stack([u.reshape(KT, P), v.reshape(KT, P)], axis=-1) for u, v in pairs])
    put("c", c.transpose(2, 0, 1, 3).reshape(P, -1))
    put("ada_b", by_partition(np.stack([i["ada_b"][0], i["ada_b"][1], i["l0_b_mod_2"]])))
    put("norm1", by_partition(np.stack([i["norm1_g"][0], i["norm1_g"][1], i["l0_norm1_2"]])))
    put("norm2", by_partition(np.stack([i["norm2_g"][0], i["norm2_g"][1], i["l0_norm2_2"]])))
    put("q_ln", by_partition(i["a_q_ln_g"][0]))
    put("kv_ln", by_partition(i["a_kv_ln_g"][0]))
    swapped = np.r_[0:QK, QK - ROPE_D // 2:QK, NOPE:QK - ROPE_D // 2]
    put("q_norm", i["a_q_norm_g"][0][swapped][:, None])
    put("k_norm", i["a_k_norm_g"][0][swapped][:, None])
    put("k_nope", np.tile(i["a_k_norm_g"][0][:NOPE], 2)[:, None])
    put("conf_dw", i["b_conf_dw"][0].reshape(CONF_K, CG, P).transpose(2, 1, 0).reshape(P, -1))
    put("conf_b", by_partition(i["b_conf_dw_b"][0]))
    put("ln_g", by_partition(i["b_conf_ln_g"][0]))
    put("ln_b", by_partition(i["b_conf_ln_b"][0]))
    put("sc_dw", i["b_sc_dw"][0].reshape(SC_K, CG, P).transpose(2, 1, 0).reshape(P, -1))
    put("na_q", np.tile(i["l0_na_q_gain_2"], 2)[:, None])
    put("na_k", np.tile(i["l0_na_k_gain_2"], 2)[:, None])
    conv = np.concatenate([i["l0_ffn_conv_w_2"], i["l0_ffn_conv_b_2"][None]])
    put("ff_conv", conv.reshape(4, FT, P).transpose(2, 1, 0).reshape(P, -1))
    return t


def feature_major(x):
    return np.ascontiguousarray(x[0].reshape(T, KT, P).transpose(2, 1, 0))


def pack_rpb(rpb):
    rows = rpb[:, WIN // 2 - ROWS:WIN // 2 - 1 + ROWS, :]
    side = (TOEP - rpb.shape[2]) // 2
    t = np.pad(rows[:, ::-1], ((0, 0), (0, 0), (side, side))).transpose(0, 2, 1)
    return np.pad(t.reshape(-1), (0, 64))


def kernel(**inputs):
    import concourse.bacc as bacc
    from concourse.bass_utils import run_bass_kernel_spmd as run

    i = {k: np.asarray(v) for k, v in inputs.items()}
    arrays = {
        "weights": pack_weights(i), "ada": pack_ada(i), "xt": feature_major(i["x"]),
        "ctx1": feature_major(i["ctx"]), "ctx2": feature_major(i["ctx_2"]), "params": pack_params(i),
        "consts": constant_table(), "rpb": pack_rpb(i["l0_na_rpb_2"])}
    nc = bacc.Bacc("TRN2", target_bir_lowering=False, num_devices=1)
    args = [nc.dram_tensor(n, a.shape, mybir.dt.from_np(a.dtype), kind="ExternalInput").ap()
            for n, a in arrays.items()]
    out = nc.dram_tensor("out_t", (P, KT, T), mybir.dt.float32, kind="ExternalOutput").ap()
    program(nc, *args, out)
    got = run(nc, [arrays], core_ids=[0]).results[0]["out_t"]
    return got.transpose(2, 1, 0).reshape(1, T, D)
```

```python
import math
from contextlib import ExitStack

import numpy as np

import concourse.bass as bass
from concourse import mybir

P = 128
D = 1024
KT = D // P
T = 256
F_FF = 2816
FT = F_FF // P
EPS = 1e-6
LAYERS = 3
MODS = 6 * KT

MLA_H, NOPE, ROPE_D, QK, VH = 8, 64, 32, 96, 64
QL_T, KVL_T, FN_T = 3, 2, 4
CONF_K, SC_K, CG = 31, 3, 4
NA_H, NA_D, GRID_W, WIN = 16, 64, 64, 16
ROWS = T // GRID_W
TOEP = 2 * GRID_W - 1
DRS = 2 * ROWS - 1
MASKED = -1e30

BLK = KT * P
RING = 6
AGRP = 4
LEAD = 4
PROBS = 3
POOL_CONV = (0, 2)
TAP_RING = 6
BIASES = 4

W_IN0, N_IN0 = 0, 10
W_UQ, N_UQ = 10, 3
W_UK, W_UV, W_OUT0 = 13, 14, 15
W_FF0 = W_OUT0 + KT
W_IN1, N_IN1 = W_FF0 + 3 * FT, 20
W_OUT1 = W_IN1 + N_IN1
W_FF1 = W_OUT1 + KT
W_K2 = W_FF1 + 3 * FT
W_Q2 = W_K2 + KT
W_V2 = W_Q2 + KT
W_OUT2 = W_V2 + KT
W_FF2 = W_OUT2 + KT
N_W = W_FF2 + 3 * FT
N_A = LAYERS * MODS
ADA_IN0 = {4: 4, 6: 5, 8: 6}
ADA_LATENT = (7, 8)
ADA_UNITS = {2 * n: 9 + n for n in range(4)}
ADA_MLA = {n: 13 + n for n in range(7)}
ADA_IN1 = {2 * n + 3: 20 + n for n in range(8)}
ADA_NA = {2 * n: 28 + n for n in range(8)}
assert N_A % AGRP == 0 and FT % 2 == 0


POOL_TAPS = [(g, k) for g in POOL_CONV for k in range(CONF_K)]


def added_to(m):
    return m - m // CONF_K


def columns(sizes):
    out, at = {}, 0
    for name, n in sizes:
        out[name] = (at, at + n)
        at += n
    return out, at


PARAMS, N_PARAMS = columns([
    ("c", LAYERS * KT * 2), ("ada_b", LAYERS * MODS), ("norm1", LAYERS * KT), ("norm2", LAYERS * KT),
    ("q_ln", QL_T), ("kv_ln", KVL_T), ("q_norm", 1), ("k_norm", 1), ("k_nope", 1),
    ("conf_dw", CG * CONF_K), ("conf_b", CG), ("ln_g", CG), ("ln_b", CG), ("sc_dw", CG * SC_K),
    ("na_q", 1), ("na_k", 1), ("ff_conv", FT * 4)])
CONSTS, N_CONSTS = columns([
    ("ident", P), ("ones", 1), ("of_pair", 2), ("of_rope", MLA_H), ("of_query", 1), ("of_cond", 2), ("cos", T),
    ("sin", T), ("dft_c", 2 * P), ("dft_n", 2 * 2 * T), ("mask", GRID_W)])


STATS, N_STAT = columns(
    [(("norm", n), 2) for n in range(8)] + [("kv", 4), ("ql", 2), ("mq", 2 * MLA_H), ("mk", 4 * MLA_H), ("conf", 2 * CG)]
    + [(("qk", j), 8 if j < 8 else 4) for j in range(16)])
SQ_ORDER = (0, 1, 5, 2, 3, 4, 6, 7)
STAT_ORDER = ([("norm", 0), ("norm", 1), "kv", "ql", "mq", "mk", ("norm", 5), ("norm", 2), ("norm", 3), "conf",
               ("norm", 4), ("norm", 6)] + [("qk", j) for j in range(16)] + [("norm", 7)])


def constant_table():
    t = np.zeros((P, N_CONSTS), np.float32)

    def put(name, a):
        c0, _ = CONSTS[name]
        t[:a.shape[0], c0:c0 + a.shape[1]] = a

    put("ident", np.eye(P))
    put("ones", np.ones((P, 1)))
    row = np.arange(P)[:, None]
    put("of_pair", (row // NA_D == np.arange(2)).astype(np.float32))
    put("of_rope", np.repeat((row >= NOPE) & (row < QK), MLA_H, axis=1).astype(np.float32))
    put("of_query", (row < QK).astype(np.float32))
    put("of_cond", (row % 32 == np.arange(2)).astype(np.float32))
    per_axis = ROPE_D // 4
    inv = np.float32(10000.0) ** (-np.arange(per_axis, dtype=np.float32) / np.float32(per_axis))
    n = np.arange(T)
    row, col = (n // GRID_W).astype(np.float32), (n % GRID_W).astype(np.float32)
    ang = np.concatenate([row[:, None] * inv, col[:, None] * inv], axis=1).astype(np.float32)
    cos, sin = np.zeros((P, T), np.float32), np.zeros((P, T), np.float32)
    cos[NOPE:QK] = np.concatenate([np.cos(ang), np.cos(ang)], axis=1).T
    sin[QK:] = np.concatenate([-np.sin(ang), np.sin(ang)], axis=1).T
    put("cos", cos)
    put("sin", sin)
    c = np.arange(P)
    w = 2 * np.pi * np.outer(c, c) / P
    put("dft_c", np.concatenate([np.cos(w), np.sin(w)], axis=1))
    w = 2 * np.pi * (np.outer(n, n) % T) / T
    norm = 1.0 / math.sqrt(T * P)
    both = np.stack([np.cos(w) * norm, -np.sin(w) * norm])
    put("dft_n", both.reshape(2, 2, P, T).transpose(2, 0, 1, 3).reshape(P, 4 * T))
    q = np.arange(P) % GRID_W
    k = np.arange(GRID_W)
    first = np.clip(q - WIN // 2, 0, GRID_W - WIN)[:, None]
    put("mask", np.where((k >= first) & (k < first + WIN), 0.0, MASKED))
    return t


def program(nc, weights, ada, xt_in, ctx1_in, ctx2_in, params_in, consts_in, rpb_in, out_t):
    fp, fr = mybir.dt.float32, mybir.dt.float32r
    ALU, ACT, AX = mybir.AluOpType, mybir.ActivationFunctionType, mybir.AxisListType
    MUL, ADD, SUB = ALU.mult, ALU.add, ALU.subtract

    ctx = ExitStack()
    with ctx:
        def sb(name, shape, dt=fp):
            return ctx.enter_context(nc.sbuf_tensor(name, shape, dt))

        def sem(name):
            return ctx.enter_context(nc.semaphore(name))

        w_raw = sb("w_raw", [P, RING, BLK])
        w_hi = sb("w_hi", [P, RING, BLK], fr)
        w_lo = sb("w_lo", [P, RING, BLK], fr)
        a_raw = sb("a_raw", [P, AGRP, BLK])
        xT = sb("xT", [P, KT, T])
        h_hi = sb("h_hi", [P, KT, 2 * T], fr)
        h_lo = sb("h_lo", [P, KT, 2 * T], fr)
        par = sb("par", [P, N_PARAMS])
        con = sb("con", [P, N_CONSTS])
        cs = sb("cs", [P, LAYERS, KT, 2])
        mods = sb("mods", [P, LAYERS, MODS, 2])
        gain = sb("gain", [P, KT])
        eps = sb("eps", [P, 1])
        zero_r = sb("zero_r", [P, P], fr)
        stat = sb("stat", [P, N_STAT])
        eps_q = sb("eps_q", [P, 1])
        warmed = sb("warmed", [P, 1])
        ada_s = sb("ada_s", [P, 4 * P])
        big = sb("big", [P, 24 * 256])
        ctxT = big[:, 0:2048].rearrange("p (k t) -> p k t", k=KT)
        sq = big[:, 2048:4096].rearrange("p (k t) -> p k t", k=KT)
        tmp = big[:, 4096:6144].rearrange("p (k t) -> p k t", k=KT)
        keysT = big[:, 0:4096].rearrange("p (h t) -> p h t", h=8)
        querT = big[:, 4096:6144].rearrange("p (h t) -> p h t", h=8)
        vals = sb("vals", [P, 4, D])
        work = sb("work", [P, (PROBS + 4) * 512])
        prob = work[:, 0:PROBS * 512].rearrange("p (b t) -> p b t", b=PROBS)
        probT = work[:, PROBS * 512:].rearrange("p (b e k t) -> p b e k t", b=2, e=2, k=4)
        nmax = sb("nmax", [P, 32])
        rsum = sb("rsum", [P, 32])
        rinv = sb("rinv", [P, 32])
        act_f = work[:, 0:512].rearrange("p (b t) -> p b t", b=2)
        gate_f = work[:, 512:1024].rearrange("p (b t) -> p b t", b=2)
        cv = work[:, 1024:2560].rearrange("p (b m t) -> p b m t", b=2, m=3)
        g_hi = sb("g_hi", [P, 2, T], fr)
        g_lo = sb("g_lo", [P, 2, T], fr)
        bank = [ctx.enter_context(nc.psum_tensor(f"bank{i}", [P, 2 * T], fp)) for i in range(8)]

        def pc(name, j=0, n=1):
            c0, _ = PARAMS[name]
            return par[:, c0 + j:c0 + j + n]

        def cc(name, lo=0, hi=None):
            c0, c1 = CONSTS[name]
            return con[:, c0 + lo:(c1 if hi is None else c0 + hi)]

        ident, ones = cc("ident"), cc("ones")

        cq = work[:, 0:768].rearrange("p (k t) -> p k t", k=3)
        ckv = work[:, 768:1792].rearrange("p (k t) -> p k t", k=2)
        fu = vals[:, 0, :].rearrange("p (g t) -> p g t", g=4)
        rope_k = vals[:, 1, 0:512]
        kr_sq = vals[:, 1, 512:1024]
        f1 = big[:, 0:2048].rearrange("p (g u c) -> p g u c", g=4, u=2)
        usq = vals[:, 2:4, 0:512]
        rot1 = work[:, 2048:2560]
        rot2 = work[:, 2560:3072]
        vals0 = vals[:, :, 512:1024]
        sgate = work[:, 0:512].rearrange("p (b t) -> p b t", b=2)
        confp = vals[:, 0:2, :].rearrange("p a b -> p (a b)")[:, 0:CG * 288].rearrange("p (g t) -> p g t", g=CG)
        cacc = vals[:, 2, :].rearrange("p (g t) -> p g t", g=CG)
        ccen = vals[:, 3, :].rearrange("p (g t) -> p g t", g=CG)
        tap = work[:, 1536:1536 + TAP_RING * T].rearrange("p (b t) -> p b t", b=TAP_RING)
        csq = work[:, 512:1536].rearrange("p (g t) -> p g t", g=CG)
        scp = big[:, 2048:2048 + CG * 264].rearrange("p (g t) -> p g t", g=CG)
        sacc = big[:, 4096:4096 + CG * T].rearrange("p (g t) -> p g t", g=CG)
        bias = sb("bias", [P, BIASES, GRID_W, DRS])
        nsq = work[:, 0:1024].rearrange("p (b t) -> p b t", b=2)
        gpad = vals[:, 0, 0:2 * (T + 2)].rearrange("p (b t) -> p b t", b=2)
        taps = sb("taps", [P, 2, 4])

        s_par, s_con, s_x, s_ctx = sem("params_loaded"), sem("consts_loaded"), sem("x_loaded"), sem("ctx_loaded")
        w_loaded = [sem(f"w_loaded{i}") for i in range(RING)]
        a_loaded = [sem(f"a_loaded{i}") for i in range(AGRP)]
        hi_done, split_done, w_used = sem("w_hi_done"), sem("w_split_done"), sem("w_used")
        a_used = sem("ada_block_used")
        full = [sem(f"bank{i}_full") for i in range(8)]
        cs_ready, mod_ready, gain_ready = sem("cond_ready"), sem("mods_ready"), sem("gain_ready")
        const_ready, pads_ready = sem("const_ready"), sem("pads_ready")
        added, pool_taps = sem("squares_added"), sem("pool_taps")
        taps_made, rope_placed = sem("tap_products"), sem("rope_placed")
        sq_ready, root_ready, inv_ready = sem("norm_sq"), sem("root_ready"), sem("root_inverted")
        ada_copied, ada_turned, ada_cleared = sem("ada_copied"), sem("ada_turned"), sem("ada_cleared")
        krsq_ready, kr_taken, rope_ready = sem("rope_sq"), sem("rope_taken"), sem("rope_ready")
        tmp_ready, hhi_ready, hlo_ready = sem("norm_scaled"), sem("h_hi_ready"), sem("h_lo_ready")
        x_updated = sem("x_updated")
        lat_ready, lsq_ready, ltmp_ready = sem("latents_ready"), sem("latent_sq"), sem("latent_scaled")
        lhi_ready, llo_ready = sem("latent_hi"), sem("latent_lo")
        f1_ready, o_hi, o_lo = sem("dft1_ready"), sem("mix_hi"), sem("mix_lo")
        v_ready = sem("values_ready")
        usq_ready, unit_ready, head_ready = sem("unit_sq"), sem("unit_gained"), sem("head_ready")
        nmax_ready, exp_ready, prob_ready, pT_ready, pv_done = (
            sem("nmax_ready"), sem("exp_ready"), sem("prob_ready"), sem("probT_ready"), sem("pv_done"))
        sg_ready, conf_ready, cen_ready, csq_ready = (
            sem("sigmoid_ready"), sem("conv_ready"), sem("centred"), sem("centred_sq"))
        cn_ready, conf_out, scc_ready, sc_out = sem("conf_normed"), sem("conf_silu"), sem("scc_ready"), sem("short_out")
        b_loaded = [sem(f"bias_loaded{i}") for i in range(BIASES)]
        bias_ready, bias_used = sem("bias_masked"), sem("bias_used")
        ff_act, ff_mul, ff_hi, ff_lo = sem("ff_activated"), sem("ff_product"), sem("ff_hi"), sem("ff_lo")
        ff_pad, ff_cv = sem("ff_padded"), sem("ff_convolved")
        dve_seq, act_seq = sem("dve_step"), sem("act_step")
        stored = sem("stored")

        tiles, last_taken, made_count = {}, [None] * 8, [0] * 8

        def place_tile(name, b, taken, made=None):
            if made is None:
                made_count[b] += 1
                made = (full[b], made_count[b])
            tiles[name] = (b, made, last_taken[b])
            last_taken[b] = taken

        def used(w):
            return (w_used, w + 1)

        def place_stat(name, b):
            place_tile(("sum", name), b, (root_ready, STAT_ORDER.index(name) + 1))

        def place_norm(n):
            place_stat(("norm", n), 7)
            place_tile(("inv", n), 4 if n == 1 else 5, (tmp_ready, KT * (n + 1)))

        place_norm(0)
        place_norm(1)
        for j in range(N_IN0):
            place_tile(("in0", j), j % 4, (kr_taken, 1) if j == 9 else (lat_ready, j + 1), used(W_IN0 + j))
        place_stat("kv", 7)
        place_stat("ql", 5)
        for g in range(FN_T):
            place_tile(("dft1", g), g, (f1_ready, g + 1))
        place_tile(("inv", "kv"), 4, (ltmp_ready, KVL_T))
        place_tile(("inv", "ql"), 7, (ltmp_ready, KVL_T + QL_T))
        for g in range(FN_T):
            place_tile(("dft2", g), 2 + g % 2, (o_lo, g + 1))
        for u in range(8):
            place_tile(("pj", u), u % 2, (unit_ready, u + 1), None if u < 7 else used(W_UK))
        place_stat("mq", 5)
        place_stat("mk", 7)
        for t in range(4):
            place_tile(("v0", t), t, (v_ready, t + 1), None if t < 3 else used(W_UV))
        for h in range(MLA_H):
            place_tile(("inv", "mk", h), 4 + h % 2, (head_ready, h + 1))

        def place_attention(name, heads, at0, o0):
            for n in range(2 * heads):
                place_tile((name, "sc", n), (0, 1, 7)[n % 3], (exp_ready, at0 + n + 1))
                place_tile((name, "tr", n), 2 + n % 2, (pT_ready, at0 + n + 1))
            for p in range(heads // 2):
                place_tile((name, "o", p), 4 + p % 2, (o_lo, o0 + p + 1), (pv_done, at0 + 4 * (p + 1)))

        def place_ffn(layer):
            if layer == 0:
                last_taken[6] = (mod_ready, ADA_IN1[3])
                place_stat(("norm", 5), 6)
            for j in range(KT):
                place_tile(("out", layer, j), j % 4, (x_updated, 2 * KT * layer + j + 1),
                           used((W_OUT0, W_OUT1, W_OUT2)[layer] + j))
            place_norm((2, 4, 7)[layer])
            if layer == 1:
                last_taken[6] = (mod_ready, ADA_NA[0])
                place_tile(("inv", 5), 6, (tmp_ready, KT * 6))
            for b in range(4):
                place_tile(("acc", layer, b), b, (x_updated, KT * (2 * layer + 1) + 2 * b + 2))
            for s in range(2):
                place_tile(("up", layer, s), 4 + s, (ff_mul, FT * (layer + 1) + s + 1), used(-1))

        place_attention("mla", MLA_H, 0, 4)
        place_ffn(0)
        place_norm(3)
        for j in range(N_IN1):
            g = j // 2
            taken = ((sc_out, j - 15) if j >= 16 else (conf_ready, g + 1) if j % 2
                     else (sg_ready, g + 1) if j < 8 else (scc_ready, g - 3))
            place_tile(("in1", j), j % 4, taken, used(W_IN1 + j))
        for half in range(2):
            place_tile(("csum", half), 4 + half, (cen_ready, half + 1))
        place_stat("conf", 7)
        for half in range(2):
            place_tile(("inv", "conf", half), 4 + half, (cn_ready, half + 1))
        place_ffn(1)
        place_norm(6)
        for j in range(16):
            place_tile(("qk", j), j % 3, (unit_ready, 8 + j + 1), used(W_K2 + j))
            place_stat(("qk", j), 3 + 4 * (j % 2))
            place_tile(("inv", "qk", j), 4 + j % 2, (head_ready, MLA_H + j + 1))
        for half in range(2):
            for t in range(4):
                place_tile(("v2", half, t), t, (v_ready, 4 + 4 * half + t + 1),
                           used(W_V2 + 4 * half + 3) if t == 3 else None)
        place_attention("na", NA_H, 16, 16)
        place_ffn(2)
        last_taken[6] = (mod_ready, N_A // AGRP)
        for s in range(2):
            place_tile(("gate", s), 6 + s, (ff_pad, FT), used(-1))

        def write_tile(pe, name):
            b, _, before = tiles[name]
            if before:
                pe.wait_ge(*before)
            return bank[b]

        def wait_tile(eng, name):
            b, made, _ = tiles[name]
            eng.wait_ge(*made)
            return bank[b]

        def row_of(n):
            return 4 * (n // 4) + 2 * (n % 2) + n // 2 % 2

        def full_of(name):
            return full[tiles[name][0]]

        NORMS = [("x", T, 0, 0, 0), ("c", 0, 1, 0, 0), ("x", T, 0, 0, 1), ("x", T, 0, 1, 0),
                 ("x", T, 0, 1, 1), ("c", 0, 1, 2, 0), ("x", T, 0, 2, 0), ("x", T, 0, 2, 1)]
        UPDATES = [0, 0, 1, 2, 3, 4, 4, 5]
        POOLED = [7, 7, 7, 4, 7, 7, 4, 7]

        def sq_of(n):
            return tmp if n in (1, 5) else sq

        MOD_GROUPS = [4, 4, 10, 16, 22, 28, 28, 34]

        block = ctx.enter_context(nc.Block())

        @block.sync
        def _(sp):
            def block_of(stream, n):
                return stream[n] if isinstance(n, int) else stream[bass.ds(n, 1), :, :].rearrange("o p n -> (o p) n")

            def load_w(w, s):
                if not isinstance(w, int) or w >= RING:
                    sp.wait_ge(split_done, w - (RING - 1))
                sp.dma_start(w_raw[:, s, :], block_of(weights, w)).then_inc(w_loaded[s], 16)

            def load_ada(g):
                for s in range(AGRP):
                    if not isinstance(g, int) or g:
                        sp.wait_ge(a_used, AGRP * g + (s + 1 - AGRP))
                    sp.dma_start(a_raw[:, s, :], block_of(ada, AGRP * g + s)).then_inc(a_loaded[s], 16)

            w_next = [0]

            def load_to(w):
                while w_next[0] < min(w, N_W):
                    load_w(w_next[0], w_next[0] % RING)
                    w_next[0] += 1

            sp.dma_start(par[:], params_in).then_inc(s_par, 16)
            load_ada(0)
            sp.dma_start(xT[:], xt_in).then_inc(s_x, 16)
            sp.dma_start(ctxT, ctx1_in).then_inc(s_ctx, 16)
            sp.dma_start(con[:], consts_in).then_inc(s_con, 16)
            for g in range(1, 4):
                load_ada(g)
            load_to(RING)
            load_ada(4)
            for j, g in ADA_IN0.items():
                load_to(W_IN0 + j + 1 + RING)
                load_ada(g + 1)
            load_to(W_UV + RING + 1)
            for g in (*ADA_LATENT, *ADA_UNITS.values()):
                load_ada(g + 1)
            for j, g in ADA_MLA.items():
                load_to(W_OUT0 + min(j, LEAD) + RING)
                load_ada(g + 1)
            for layer, w0 in enumerate((W_FF0, W_FF1, W_FF2)):
                ahead = LEAD + RING
                load_to(w0 + ahead)
                with sp.Fori(0, FT // 2 - (2 if layer == 2 else 0)) as i:
                    for j in range(6):
                        load_w(6 * i + (w0 + ahead + j), (w0 + ahead + j) % RING)
                w_next[0] = w0 + ahead + 3 * FT - (12 if layer == 2 else 0)
                if layer == 0:
                    for j, g in ADA_IN1.items():
                        load_to(W_IN1 + j + 1 + RING)
                        load_ada(g + 1)
                if layer == 1:
                    for j, g in ADA_NA.items():
                        load_to(W_OUT2 + min(j, LEAD) + RING)
                        if g + 1 < N_A // AGRP:
                            load_ada(g + 1)
            load_to(N_W)
            for half in range(2):
                tiles_of = slice(4 * half, 4 * half + 4)
                sp.wait_ge(x_updated, 5 * KT + 4 * half + 4)
                sp.dma_start(out_t[:, tiles_of, :], xT[:, tiles_of, :]).then_inc(stored, 16)
            sp.wait_ge(stored, 32)

        @block.gpsimd
        def _(pool):
            nc.gpsimd.memset(eps[:], EPS).then_inc(const_ready, 1)
            nc.gpsimd.memset(eps_q[:], QK * EPS).then_inc(const_ready, 1)
            nc.gpsimd.memset(zero_r[:].bitcast(fp), 0.0).then_inc(const_ready, 1)
            def load_bias(h):
                if h >= BIASES:
                    pool.wait_ge(bias_used, h - (BIASES - 1))
                src = bass.AP(rpb_in.tensor, h * TOEP * DRS + (GRID_W - 1) * DRS,
                              [[1, 2], [-DRS, GRID_W], [1, GRID_W * DRS]])
                pool.dma_start(bias[:, h % BIASES, :, :].rearrange("p c d -> p (c d)"), src)\
                    .then_inc(b_loaded[h % BIASES], 16)

            def add_squares(n):
                v, at = sq_of(n), KT * SQ_ORDER.index(n)
                for k in range(1, POOLED[n]):
                    pool.wait_ge(sq_ready, at + k + 1)
                    nc.gpsimd.tensor_tensor(v[:, 0, :], v[:, 0, :], v[:, k, :], ADD).then_inc(added, 1)
                    pooled[0] += 1
                    if k + 1 < POOLED[n]:
                        pool.wait_ge(added, pooled[0])

            def mask_bias(h):
                pool.wait_ge(b_loaded[h % BIASES], 16 * (h // BIASES + 1))
                nc.gpsimd.tensor_tensor(bias[:, h % BIASES, :, :], bias[:, h % BIASES, :, :],
                                        cc("mask").unsqueeze(2).broadcast_to([P, GRID_W, DRS]), ADD)\
                    .then_inc(bias_ready, 1)

            pooled = [0]
            add_squares(0)
            add_squares(1)
            pool.wait_ge(s_con, 16)
            for h in range(BIASES):
                load_bias(h)
            for h in range(BIASES):
                mask_bias(h)
            pool.wait_ge(rope_ready, 1)
            pool.wait_ge(o_lo, FN_T)
            pool.wait_ge(bias_ready, BIASES)
            for h in range(MLA_H):
                nc.gpsimd.tensor_copy(keysT[NOPE:QK, h, :], rope_k[NOPE:QK, :]).then_inc(rope_placed, 1)
            pool.wait_ge(rope_placed, MLA_H)
            for n in SQ_ORDER[2:5]:
                add_squares(n)
            for m, (g, k) in enumerate(POOL_TAPS):
                if k == 0:
                    continue
                pool.wait_ge(taps_made, m + 1)
                if k > 1:
                    pool.wait_ge(pool_taps, added_to(m - 1))
                nc.gpsimd.tensor_tensor(cacc[:, g, :], cacc[:, g, :], tap[:, m % TAP_RING, :], ADD)\
                    .then_inc(pool_taps, 1)
            for n in SQ_ORDER[5:7]:
                add_squares(n)
            for h in range(2, NA_H):
                if h + 2 < NA_H and h + 2 >= BIASES:
                    load_bias(h + 2)
                if h >= BIASES:
                    mask_bias(h)
            add_squares(7)

        @block.scalar
        def _(act):
            hi_next = [0]
            steps = [0]

            def split_hi(w, s, turn):
                act.wait_ge(w_loaded[s], 16 * turn)
                if not isinstance(w, int) or w >= RING:
                    act.wait_ge(w_used, w - (RING - 1))
                nc.scalar.copy(w_hi[:, s, :], w_raw[:, s, :]).then_inc(hi_done, 1)

            def split_to(w):
                while hi_next[0] <= min(w, N_W - 1):
                    n = hi_next[0]
                    split_hi(n, n % RING, n // RING + 1)
                    hi_next[0] += 1

            def warm(func):
                act.wait_ge(const_ready, 3)
                nc.scalar.activation(warmed[:], eps[:], func).then_inc(act_seq, 1)
                steps[0] += 1
                act.wait_ge(act_seq, steps[0])

            def root(name, width, bias=eps):
                b = wait_tile(act, ("sum", name))
                c0, c1 = STATS[name]
                nc.scalar.activation(stat[:, c0:c1], b[:, 0:c1 - c0], ACT.Sqrt, bias=bias[:], scale=1.0 / width)\
                    .then_inc(root_ready, 1)

            def ada_copy(g):
                act.wait_ge(a_used, AGRP * g + AGRP)
                nc.scalar.copy(ada_s[:], bank[6][:, :]).then_inc(ada_copied, 1)

            def square(n, k):
                src, upd = NORMS[n][0], UPDATES[n]
                if k == 0 and n < 2:
                    act.wait_ge((s_x, s_ctx)[n], 16)
                if k == 0 and n == 5:
                    act.wait_ge(s_ctx, 32)
                if src == "x" and upd:
                    act.wait_ge(x_updated, KT * (upd - 1) + k + 1)
                v = ctxT if src == "c" else xT
                nc.scalar.activation(sq_of(n)[:, k, :], v[:, k, :], ACT.Square).then_inc(sq_ready, 1)

            def norm_root(n):
                act.wait_ge(const_ready, 3)
                root(("norm", n), D)

            def norm(n):
                src, c0, col, layer, which = NORMS[n]
                for k in range(KT):
                    act.wait_ge(tmp_ready, KT * n + k + 1)
                    sh = mods[:, layer, 3 * KT * which + k, col:col + 1]
                    nc.scalar.activation(h_hi[:, k, c0:c0 + T], tmp[:, k, :], ACT.Identity, bias=sh)\
                        .then_inc(hhi_ready, 1)

            def project_out(w0, n):
                if n == 2:
                    for k in range(KT):
                        square(5, k)
                for j in range(KT):
                    split_to(w0 + max(j + LEAD, 5))
                    if j == 5 and n == 2:
                        norm_root(5)
                    if j:
                        square(n, j - 1)
                warm(ACT.Sqrt)
                square(n, KT - 1)
                norm_root(n)
                norm(n)

            def attention(name, heads, at0, o0, query_scale, ada_at, w_next):
                def turned(n):
                    b = wait_tile(act, (name, "tr", n))
                    j, e = n // 2, n % 2
                    if j >= 2:
                        act.wait_ge(pv_done, at0 + 2 * (j - 1))
                    nc.scalar.copy(probT[:, j % 2, e, :, :], b[:, :].rearrange("p (k q) -> p k q", k=4))\
                        .then_inc(pT_ready, 1)

                def out_hi(p):
                    b = wait_tile(act, (name, "o", p))
                    nc.scalar.copy(h_hi[:, p, 0:T], b[:, 0:T]).then_inc(o_hi, 1)

                for j in range(heads):
                    for n in (2 * j, 2 * j + 1):
                        if n >= 2:
                            turned(n - 2)
                        b = wait_tile(act, (name, "sc", n))
                        act.wait_ge(nmax_ready, at0 + n + 1)
                        if n >= PROBS:
                            act.wait_ge(full_of((name, "tr", n - PROBS)), tiles[name, "tr", n - PROBS][1][1])
                        nc.scalar.activation(prob[:, n % PROBS, :], b[:, :], ACT.Exp, bias=nmax[:, n:n + 1],
                                             scale=query_scale(n), accum_out=rsum[:, n:n + 1]).then_inc(exp_ready, 1)
                    if j - 1 in ada_at:
                        ada_copy(ada_at[j - 1])
                    if 1 <= j <= LEAD:
                        split_to(w_next + j - 1)
                    if j >= 3 and j % 2:
                        out_hi((j - 3) // 2)
                for n in (2 * heads - 2, 2 * heads - 1):
                    turned(n)
                out_hi(heads // 2 - 1)

            def ffn(layer):
                w0, g0 = (W_FF0, W_FF1, W_FF2)[layer], FT * layer
                split_to(w0 + LEAD - 1)
                def turn(i, splits_on=True):
                    def hi(j, on=True):
                        if on:
                            split_hi(3 * 2 * i + (w0 + j), (w0 + j) % RING, i + ((w0 + j) // RING + 1))

                    def activate(s):
                        b = tiles[("up", layer, s)][0]
                        if layer < 2:
                            act.wait_ge(w_used, 6 * i + (w0 + 2 * s + 2))
                            nc.scalar.activation(act_f[:, s, :], bank[b][:, 0:T], ACT.Silu).then_inc(ff_act, 1)
                        else:
                            b = tiles["gate", s][0]
                            act.wait_ge(w_used, 6 * i + (w0 + 2 * s + 1))
                            act.wait_ge(pads_ready, 1)
                            nc.scalar.copy(gpad[:, s, 1:T + 1], bank[b][:, 0:T]).then_inc(ff_pad, 1)

                    def gelu(s):
                        act.wait_ge(ff_cv, 6 * i + 3 * (s + 1))
                        nc.scalar.activation(act_f[:, s, :], cv[:, s, 2, :], ACT.Gelu, bias=taps[:, s, 3:4])\
                            .then_inc(ff_act, 1)

                    def high(s):
                        act.wait_ge(ff_mul, 2 * i + (g0 + s + 3))
                        nc.scalar.copy(g_hi[:, s, :], gate_f[:, s, :]).then_inc(ff_hi, 1)

                    hi(4)
                    hi(5)
                    activate(0)
                    if layer == 2:
                        gelu(0)
                    hi(6, splits_on)
                    high(0)
                    hi(7, splits_on)
                    activate(1)
                    if layer == 2:
                        gelu(1)
                    high(1)
                    hi(8, splits_on)
                    hi(9, splits_on)

                warm(ACT.Silu if layer < 2 else ACT.Gelu)
                with act.Fori(0, FT // 2 - (layer == 2)) as i:
                    turn(i)
                if layer == 2:
                    turn(FT // 2 - 1, splits_on=False)
                hi_next[0] = w0 + 3 * FT + LEAD

            act.wait_ge(s_par, 16)
            nc.scalar.activation(cs[:].rearrange("p l k c -> p (l k c)"), pc("c", 0, LAYERS * KT * 2), ACT.Silu)\
                .then_inc(cs_ready, 1)
            ada_copy(0)
            for n in range(2):
                for k in range(KT):
                    square(n, k)
            for g in range(1, 4):
                ada_copy(g)
                if g < 3:
                    norm_root(g - 1)
            split_to(0)
            norm(0)
            split_to(4)
            norm(1)
            for j in range(N_IN0):
                split_to(W_IN0 + j + LEAD)
                if j - 1 in ADA_IN0:
                    ada_copy(ADA_IN0[j - 1])
                b = wait_tile(act, ("in0", j))
                if j == 9:
                    nc.scalar.activation(kr_sq, b[:, :], ACT.Square).then_inc(krsq_ready, 1)
                else:
                    dst, n = ((cq[:, j, :], T) if j < 3 else (fu[:, j - 3, :], T) if j < 7 else (ckv[:, j - 7, :], 2 * T))
                    nc.scalar.copy(dst, b[:, 0:n]).then_inc(lat_ready, 1)
            split_to(W_UV)
            lsq = sq[:, :, :].rearrange("p k t -> p (k t)")
            warm(ACT.Sqrt)
            act.wait_ge(lat_ready, N_IN0 - 1)
            nc.scalar.activation(lsq[:, 0:1024], ckv.rearrange("p k t -> p (k t)"), ACT.Square).then_inc(lsq_ready, 1)
            nc.scalar.activation(lsq[:, 1024:1792], cq.rearrange("p k t -> p (k t)"), ACT.Square).then_inc(lsq_ready, 1)
            root("kv", KVL_T * P)
            root("ql", QL_T * P)
            ada_copy(ADA_LATENT[0])
            for g in range(FN_T):
                b = wait_tile(act, ("dft1", g))
                nc.scalar.copy(f1[:, g, :, :].rearrange("p u c -> p (u c)"), b[:, :]).then_inc(f1_ready, 1)
            for k in range(KVL_T):
                act.wait_ge(ltmp_ready, k + 1)
                nc.scalar.copy(h_hi[:, 2 * k:2 * k + 2, T:2 * T],
                               tmp[:, 2 * k:2 * k + 2, :]).then_inc(lhi_ready, 1)
            for k in range(QL_T):
                act.wait_ge(ltmp_ready, KVL_T + k + 1)
                nc.scalar.copy(h_hi[:, 4 + k, T:2 * T], tmp[:, 4 + k, :]).then_inc(lhi_ready, 1)
            ada_copy(ADA_LATENT[1])
            for g in range(FN_T):
                b = wait_tile(act, ("dft2", g))
                nc.scalar.copy(h_hi[:, 4 + g, 0:T], b[:, 0:T]).then_inc(o_hi, 1)
            for u in range(8):
                b = wait_tile(act, ("pj", u))
                nc.scalar.activation(usq[:, u % 2, :], b[:, :], ACT.Square).then_inc(usq_ready, 1)
                if u - 1 in ADA_UNITS:
                    ada_copy(ADA_UNITS[u - 1])
            root("mq", 1, eps_q)
            root("mk", QK)
            for t in range(4):
                b = wait_tile(act, ("v0", t))
                nc.scalar.copy(vals0[:, t, :], b[:, :]).then_inc(v_ready, 1)
            warm(ACT.Exp)
            mq0 = STATS["mq"][0]
            attention("mla", MLA_H, 0, 4, lambda n: stat[:, mq0 + row_of(n):mq0 + row_of(n) + 1], ADA_MLA, W_OUT0)
            act.dma_start(ctxT, ctx2_in).then_inc(s_ctx, 16)
            project_out(W_OUT0, 2)
            ffn(0)
            warm(ACT.Sqrt)
            for k in range(KT):
                square(3, k)
            norm_root(3)
            norm(3)
            warm(ACT.Sigmoid)
            made = [0]

            def tap_products(n):
                for m in range(made[0], made[0] + n):
                    g, k = POOL_TAPS[m]
                    src, wk = confp[:, g, 1 + k:1 + k + T], pc("conf_dw", CONF_K * g + k)
                    if k == 0:
                        act.wait_ge(conf_ready, g + 1)
                        ins = nc.scalar.activation(cacc[:, g, :], src, ACT.Identity, bias=pc("conf_b", g), scale=wk)
                    else:
                        if m >= TAP_RING:
                            act.wait_ge(pool_taps, added_to(m - TAP_RING))
                        ins = nc.scalar.activation(tap[:, m % TAP_RING, :], src, ACT.Copy, scale=wk)
                    ins.then_inc(taps_made, 1)
                made[0] += n

            for j in range(N_IN1):
                split_to(W_IN1 + max(j + LEAD, 5))
                if j - 1 in ADA_IN1:
                    ada_copy(ADA_IN1[j - 1])
                if j >= 2:
                    tap_products(min(5, CONF_K * (1 + (j > 6)) - made[0]))
                if j < 8 and j % 2 == 0:
                    b = wait_tile(act, ("in1", j))
                    if j >= 4:
                        act.wait_ge(conf_ready, j // 2 - 1)
                    nc.scalar.activation(sgate[:, j // 2 % 2, :], b[:, 0:T], ACT.Sigmoid).then_inc(sg_ready, 1)
                elif 8 <= j < 16 and j % 2 == 0:
                    b = wait_tile(act, ("in1", j))
                    g = (j - 8) // 2
                    act.wait_ge(conf_ready, 4 if g < 2 else 4 + g - 1)
                    nc.scalar.copy(sgate[:, g % 2, :], b[:, 0:T]).then_inc(scc_ready, 1)
                elif j >= 16:
                    g = j - 16
                    act.wait_ge(sc_out, g + 1)
                    nc.scalar.copy(h_hi[:, 4 + g, 0:T], sacc[:, g, :]).then_inc(o_hi, 1)
                if j == 16:
                    for half in range(2):
                        g = 2 * half
                        act.wait_ge(cen_ready, half + 1)
                        nc.scalar.activation(csq[:, g:g + 2, :], ccen[:, g:g + 2, :], ACT.Square)\
                            .then_inc(csq_ready, 1)
                if j == 18:
                    root("conf", P)
                    warm(ACT.Silu)
            for g in range(CG):
                act.wait_ge(cn_ready, g // 2 + 1)
                nc.scalar.activation(cacc[:, g, :], ccen[:, g, :], ACT.Silu, bias=pc("ln_b", g), scale=pc("ln_g", g))\
                    .then_inc(conf_out, 1)
                act.wait_ge(conf_out, g + 1)
                nc.scalar.copy(h_hi[:, g, 0:T], cacc[:, g, :]).then_inc(o_hi, 1)
            project_out(W_OUT1, 4)
            norm(5)
            ffn(1)
            warm(ACT.Sqrt)
            for k in range(KT):
                square(6, k)
            norm_root(6)
            norm(6)
            for j in range(17):
                if j < 16:
                    split_to(W_K2 + j + LEAD)
                    b = wait_tile(act, ("qk", j))
                    n = 2 * T if j < 8 else T
                    nc.scalar.activation(nsq[:, j % 2, 0:n], b[:, 0:n], ACT.Square).then_inc(usq_ready, 1)
                if j:
                    root(("qk", j - 1), NA_D)
            for half in range(2):
                split_to(W_V2 + 4 * half + 3 + LEAD - 1)
                for t in range(4):
                    b = wait_tile(act, ("v2", half, t))
                    nc.scalar.copy(vals[:, t, half * 512:(half + 1) * 512], b[:, :]).then_inc(v_ready, 1)
            warm(ACT.Exp)
            attention("na", NA_H, 16, 16, lambda n: 1.0, ADA_NA, W_OUT2)
            project_out(W_OUT2, 7)
            ffn(2)

        @block.vector
        def _(dve):
            lo_next = [0]
            seq = [0]

            def step(ins):
                seq[0] += 1
                ins.then_inc(dve_seq, 1)
                dve.wait_ge(dve_seq, seq[0])

            def split_lo(w, s):
                dve.wait_ge(hi_done, w + 1)
                nc.vector.tensor_tensor(w_lo[:, s, :], w_raw[:, s, :], w_hi[:, s, :].bitcast(fp), SUB)\
                    .then_inc(split_done, 1)

            def split_to(w):
                while lo_next[0] <= min(w, N_W - 1):
                    n = lo_next[0]
                    split_lo(n, n % RING)
                    lo_next[0] += 1

            def ada_take(g):
                dve.wait_ge(ada_turned, g + 1)
                at = PARAMS["ada_b"][0]
                mflat = mods[:].rearrange("p l m c -> p (l m) c")
                dst, b = mflat[:, AGRP * g:AGRP * (g + 1), :], par[:, at + AGRP * g:at + AGRP * (g + 1)]
                nc.vector.tensor_tensor(dst, bank[6][:, 0:2 * AGRP].rearrange("p (m c) -> p m c", c=2),
                                        b.unsqueeze(2).broadcast_to([P, AGRP, 2]), ADD).then_inc(mod_ready, 1)

            def invert(name):
                c0, c1 = STATS[name]
                dve.wait_ge(root_ready, STAT_ORDER.index(name) + 1)
                nc.vector.reciprocal(stat[:, c0:c1], stat[:, c0:c1]).then_inc(inv_ready, 1)

            def norm(n):
                src, c0, col, layer, which = NORMS[n]
                v = ctxT if src == "c" else xT
                m0 = 3 * KT * which
                if n == 0:
                    dve.wait_ge(s_x, 16)
                if n == 1:
                    dve.wait_ge(s_ctx, 16)
                if n == 5:
                    dve.wait_ge(s_ctx, 32)
                if n not in (0, 1, 5):
                    invert(("norm", n))
                dve.wait_ge(mod_ready, MOD_GROUPS[n])
                step(nc.vector.scalar_tensor_tensor(
                    out=gain[:], in0=mods[:, layer, m0 + KT:m0 + 2 * KT, col], scalar=1.0,
                    in1=pc("norm2" if which else "norm1", KT * layer, KT), op0=ADD, op1=MUL))
                inv = wait_tile(dve, ("inv", n))

                def scale(k):
                    nc.vector.scalar_tensor_tensor(out=tmp[:, k, :], in0=v[:, k, :], scalar=gain[:, k:k + 1],
                                                   in1=inv[:, 0:T], op0=MUL, op1=MUL).then_inc(tmp_ready, 1)

                scale(0)
                scale(1)
                for k in range(KT):
                    if k + 2 < KT:
                        scale(k + 2)
                    dve.wait_ge(hhi_ready, KT * n + k + 1)
                    nc.vector.scalar_tensor_tensor(
                        out=h_lo[:, k, c0:c0 + T], in0=tmp[:, k, :], scalar=mods[:, layer, m0 + k, col:col + 1],
                        in1=h_hi[:, k, c0:c0 + T].bitcast(fp), op0=ADD, op1=SUB).then_inc(hlo_ready, 1)

            def attention(name, heads, at0, o0, ada_at, w_next):
                def maximum(n):
                    b = wait_tile(dve, (name, "sc", n))
                    if name == "na":
                        h, t = 2 * (n // 4) + n % 2, n // 2 % 2
                        if t == 0:
                            dve.wait_ge(bias_ready, h + 1)
                        m0 = 3 + 2 * t
                        ins = nc.vector.tensor_tensor(
                            b[:, T:2 * T].rearrange("p (r c) -> p r c", r=ROWS),
                            b[:, T:2 * T].rearrange("p (r c) -> p r c", r=ROWS),
                            bias[:, h % BIASES, :, m0 - ROWS + 1:m0 + 1][:, :, ::-1].rearrange("p c r -> p r c"), ADD)
                        step(ins)
                        if t == 1:
                            dve.sem_inc(bias_used, 1)
                        nc.vector.tensor_reduce(nmax[:, n:n + 1], b[:, :], AX.X, ALU.max, negate=True)\
                            .then_inc(nmax_ready, 1)
                    else:
                        step(nc.vector.tensor_reduce(nmax[:, n:n + 1], b[:, :], AX.X, ALU.max, negate=True))
                        c = STATS["mq"][0] + row_of(n)
                        nc.vector.tensor_tensor(nmax[:, n:n + 1], nmax[:, n:n + 1], stat[:, c:c + 1], MUL)\
                            .then_inc(nmax_ready, 1)

                def out_lo(p):
                    b = wait_tile(dve, (name, "o", p))
                    dve.wait_ge(o_hi, o0 + p + 1)
                    nc.vector.tensor_tensor(h_lo[:, p, 0:T], b[:, 0:T], h_hi[:, p, 0:T].bitcast(fp), SUB)\
                        .then_inc(o_lo, 1)

                for j in range(heads):
                    for n in (2 * j, 2 * j + 1):
                        maximum(n)
                    for n in (2 * j, 2 * j + 1):
                        dve.wait_ge(exp_ready, at0 + n + 1)
                        step(nc.vector.reciprocal(rinv[:, n:n + 1], rsum[:, n:n + 1]))
                        nc.vector.tensor_scalar(prob[:, n % PROBS, :], prob[:, n % PROBS, :], rinv[:, n:n + 1], None, MUL)\
                            .then_inc(prob_ready, 1)
                    if j - 1 in ada_at:
                        ada_take(ada_at[j - 1])
                    if 1 <= j <= LEAD:
                        split_to(w_next + j - 1)
                    if j >= 3 and j % 2:
                        out_lo((j - 3) // 2)
                out_lo(heads // 2 - 1)

            def project_out(layer, w0):
                dve.wait_ge(mod_ready, 12 * layer + 6)
                for j in range(KT):
                    split_to(w0 + max(j + LEAD, 5))
                    if layer == 0 and j == 6:
                        invert(("norm", 5))
                    b = wait_tile(dve, ("out", layer, j))
                    nc.vector.scalar_tensor_tensor(out=xT[:, j, :], in0=b[:, 0:T],
                                                   scalar=mods[:, layer, 2 * KT + j, 0:1], in1=xT[:, j, :],
                                                   op0=MUL, op1=ADD).then_inc(x_updated, 1)

            def ffn(layer):
                w0, g0 = (W_FF0, W_FF1, W_FF2)[layer], FT * layer
                split_to(w0 + LEAD - 1)
                def turn(i, splits_on=True):
                    def lo(j, on=True):
                        if on:
                            split_lo(3 * 2 * i + (w0 + j), (w0 + j) % RING)

                    def convolve(s):
                        at = PARAMS["ff_conv"][0]
                        nc.vector.tensor_copy(taps[:, s, :], par[:, bass.ds(8 * i + (at + 4 * s), 4)])\
                            .then_inc(dve_seq, 1)
                        dve.wait_ge(dve_seq, 2 * i + (seq[0] + s + 1))
                        dve.wait_ge(ff_pad, 2 * i + (s + 1))
                        nc.vector.tensor_scalar(cv[:, s, 0, :], gpad[:, s, 0:T], taps[:, s, 0:1], None, MUL)\
                            .then_inc(ff_cv, 1)
                        for m in (1, 2):
                            dve.wait_ge(ff_cv, 6 * i + (3 * s + m))
                            nc.vector.scalar_tensor_tensor(out=cv[:, s, m, :], in0=gpad[:, s, m:m + T],
                                                           scalar=taps[:, s, m:m + 1], in1=cv[:, s, m - 1, :],
                                                           op0=MUL, op1=ADD).then_inc(ff_cv, 1)

                    def product(s):
                        b = tiles[("up", layer, s)][0]
                        half = T if layer < 2 else 0
                        if layer == 2:
                            dve.wait_ge(w_used, 6 * i + (w0 + 2 * s + 2))
                        dve.wait_ge(ff_act, 2 * i + (g0 + s + 1))
                        nc.vector.tensor_tensor(gate_f[:, s, :], act_f[:, s, :], bank[b][:, half:half + T], MUL)\
                            .then_inc(ff_mul, 1)

                    def low(s):
                        dve.wait_ge(ff_hi, 2 * i + (g0 + s + 1))
                        nc.vector.tensor_tensor(g_lo[:, s, :], gate_f[:, s, :], g_hi[:, s, :].bitcast(fp), SUB)\
                            .then_inc(ff_lo, 1)

                    lo(4)
                    lo(5)
                    if layer == 2:
                        convolve(0)
                    product(0)
                    lo(6, splits_on)
                    low(0)
                    if layer == 2:
                        convolve(1)
                    lo(7, splits_on)
                    product(1)
                    low(1)
                    lo(8, splits_on)
                    lo(9, splits_on)

                with dve.Fori(0, FT // 2 - (layer == 2)) as i:
                    turn(i)
                if layer == 2:
                    turn(FT // 2 - 1, splits_on=False)
                if layer == 2:
                    seq[0] += FT
                lo_next[0] = w0 + 3 * FT + LEAD
                dve.wait_ge(mod_ready, 12 * (layer + 1))
                for b4 in range(4):
                    b = wait_tile(dve, ("acc", layer, b4))
                    for e in range(2):
                        j = 2 * b4 + e
                        nc.vector.scalar_tensor_tensor(out=xT[:, j, :], in0=b[:, e * T:(e + 1) * T],
                                                       scalar=mods[:, layer, 5 * KT + j, 0:1], in1=xT[:, j, :],
                                                       op0=MUL, op1=ADD).then_inc(x_updated, 1)

            nc.vector.memset(bank[6][:, :], 0.0).then_inc(ada_cleared, 1)
            dve.sem_inc(ff_mul, 2)
            dve.wait_ge(s_par, 16)
            ada_take(0)
            for g in range(1, 4):
                ada_take(g)
                if g < 3:
                    invert(("norm", g - 1))
            split_to(0)
            norm(0)
            split_to(4)
            norm(1)

            def rotate(dst, b, gains, n):
                shape = lambda a: a.rearrange("p (e t) -> p e t", t=T)
                table = lambda name, lo: cc(name)[lo:lo + ROPE_D, :].unsqueeze(1).broadcast_to([ROPE_D, n // T, T])
                r1, r2 = rot1[NOPE:QK, 0:n], rot2[NOPE:QK, 0:n]
                yield nc.vector.scalar_tensor_tensor(out=shape(r2), in0=shape(b), scalar=gains, in1=table("sin", QK),
                                                     op0=MUL, op1=MUL)
                step(nc.vector.tensor_tensor(shape(r1), shape(dst), table("cos", NOPE), MUL))
                yield nc.vector.tensor_tensor(dst, r1, r2, ADD)

            for j in range(N_IN0):
                split_to(W_IN0 + j + LEAD)
                if j == 9:
                    b = wait_tile(dve, ("in0", j))
                    dve.wait_ge(krsq_ready, 1)
                    dve.wait_ge(s_con, 16)
                    step(nc.vector.tensor_scalar(rope_k[NOPE:QK, :], b[NOPE:QK, :], pc("k_norm")[NOPE:QK, :], None, MUL))
                    ops = rotate(rope_k[NOPE:QK, T:2 * T], b[QK:P, T:2 * T], pc("k_norm")[QK:P, :], T)
                    next(ops).then_inc(kr_taken, 1)
                    dve.wait_ge(kr_taken, 1)
                    next(ops).then_inc(rope_ready, 1)
                if j - 1 in ADA_IN0:
                    ada_take(ADA_IN0[j - 1])
            split_to(W_UV)
            invert("kv")
            invert("ql")
            ada_take(ADA_LATENT[0])
            inv = wait_tile(dve, ("inv", "kv"))
            for k in range(KVL_T):
                nc.vector.scalar_tensor_tensor(
                    out=tmp[:, 2 * k:2 * k + 2, :].rearrange("p a t -> p (a t)"), in0=ckv[:, k, :],
                    scalar=pc("kv_ln", k), in1=inv[:, :], op0=MUL, op1=MUL).then_inc(ltmp_ready, 1)
            inv = wait_tile(dve, ("inv", "ql"))
            for k in range(QL_T):
                nc.vector.scalar_tensor_tensor(out=tmp[:, 4 + k, :], in0=cq[:, k, :], scalar=pc("q_ln", k),
                                               in1=inv[:, 0:T], op0=MUL, op1=MUL).then_inc(ltmp_ready, 1)
            for k in range(KVL_T):
                dve.wait_ge(lhi_ready, k + 1)
                nc.vector.tensor_tensor(h_lo[:, 2 * k:2 * k + 2, T:2 * T], tmp[:, 2 * k:2 * k + 2, :],
                                        h_hi[:, 2 * k:2 * k + 2, T:2 * T].bitcast(fp), SUB).then_inc(llo_ready, 1)
            for k in range(QL_T):
                dve.wait_ge(lhi_ready, KVL_T + k + 1)
                nc.vector.tensor_tensor(h_lo[:, 4 + k, T:2 * T], tmp[:, 4 + k, :],
                                        h_hi[:, 4 + k, T:2 * T].bitcast(fp), SUB).then_inc(llo_ready, 1)
            for g in range(FN_T):
                b = wait_tile(dve, ("dft2", g))
                dve.wait_ge(o_hi, g + 1)
                nc.vector.tensor_tensor(h_lo[:, 4 + g, 0:T], b[:, 0:T], h_hi[:, 4 + g, 0:T].bitcast(fp), SUB)\
                    .then_inc(o_lo, 1)
            ada_take(ADA_LATENT[1])
            for u in range(4):
                b = wait_tile(dve, ("pj", u))
                dve.wait_ge(usq_ready, u + 1)
                q = querT[:, 2 * u:2 * u + 2, :].rearrange("p a t -> p (a t)")
                step(nc.vector.tensor_scalar(q[0:QK, :], b[0:QK, :], pc("q_norm")[0:QK, :], None, MUL))
                ops = rotate(q[NOPE:QK, :], b[QK:P, :], pc("q_norm")[QK:P, :], 2 * T)
                next(ops).then_inc(unit_ready, 1)
                dve.wait_ge(unit_ready, u + 1)
                step(next(ops))
                if u - 1 in ADA_UNITS:
                    ada_take(ADA_UNITS[u - 1])
            for u in range(4, 8):
                b = wait_tile(dve, ("pj", u))
                dve.wait_ge(usq_ready, u + 1)
                for e in range(2):
                    rows = slice(e * NOPE, (e + 1) * NOPE)
                    ins = nc.vector.tensor_scalar(keysT[0:NOPE, 2 * (u - 4) + e, :], b[rows, :], pc("k_nope")[rows, :],
                                                  None, MUL)
                ins.then_inc(unit_ready, 1)
                if u - 1 in ADA_UNITS:
                    ada_take(ADA_UNITS[u - 1])
            invert("mq")
            invert("mk")
            dve.wait_ge(unit_ready, 8)
            for h in range(MLA_H):
                inv = wait_tile(dve, ("inv", "mk", h))
                dve.wait_ge(rope_placed, h + 1)
                nc.vector.tensor_tensor(keysT[0:QK, h, :], keysT[0:QK, h, :], inv[0:QK, :], MUL).then_inc(head_ready, 1)
            attention("mla", MLA_H, 0, 4, ADA_MLA, W_OUT0)
            project_out(0, W_OUT0)
            norm(2)
            ffn(0)
            norm(3)
            tap_list = [(g, k) for g in range(CG) if g not in POOL_CONV for k in range(CONF_K)]
            taps_done = [0]

            def conv_taps(n):
                for g, k in tap_list[taps_done[0]:taps_done[0] + n]:
                    src = confp[:, g, 1 + k:1 + k + T]
                    wk = pc("conf_dw", CONF_K * g + k)
                    if k == 0:
                        ins = nc.vector.tensor_scalar(cacc[:, g, :], src, wk, pc("conf_b", g), MUL, ADD)
                    else:
                        ins = nc.vector.scalar_tensor_tensor(out=cacc[:, g, :], in0=src, scalar=wk,
                                                             in1=cacc[:, g, :], op0=MUL, op1=ADD)
                    step(ins)
                taps_done[0] = min(len(tap_list), taps_done[0] + n)

            def short_low(g):
                dve.wait_ge(o_hi, 8 + g + 1)
                nc.vector.tensor_tensor(h_lo[:, 4 + g, 0:T], sacc[:, g, :], h_hi[:, 4 + g, 0:T].bitcast(fp), SUB)\
                    .then_inc(o_lo, 1)

            step(nc.vector.memset(confp, 0.0))
            step(nc.vector.memset(scp, 0.0))
            for j in range(N_IN1):
                split_to(W_IN1 + max(j + LEAD, 5))
                g = j // 2
                if j < 8 and j % 2:
                    b = wait_tile(dve, ("in1", j))
                    dve.wait_ge(sg_ready, g + 1)
                    nc.vector.tensor_tensor(confp[:, g, 16:16 + T], b[:, 0:T], sgate[:, g % 2, :], MUL)\
                        .then_inc(conf_ready, 1)
                    dve.wait_ge(conf_ready, g + 1)
                elif 8 <= j < 16 and j % 2:
                    g -= 4
                    b = wait_tile(dve, ("in1", j))
                    dve.wait_ge(scc_ready, g + 1)
                    nc.vector.tensor_tensor(scp[:, g, 1:1 + T], b[:, 0:T], sgate[:, g % 2, :], MUL)\
                        .then_inc(conf_ready, 1)
                    dve.wait_ge(conf_ready, 4 + g + 1)
                    for k in range(SC_K):
                        src = scp[:, g, k:k + T]
                        wk = pc("sc_dw", SC_K * g + k)
                        if k == 0:
                            step(nc.vector.tensor_scalar(sacc[:, g, :], src, wk, None, MUL))
                        else:
                            step(nc.vector.scalar_tensor_tensor(out=sacc[:, g, :], in0=src, scalar=wk,
                                                                in1=sacc[:, g, :], op0=MUL, op1=ADD))
                elif j >= 16:
                    g = j - 16
                    b = wait_tile(dve, ("in1", j))
                    nc.vector.tensor_tensor(sacc[:, g, :], b[:, 0:T], sacc[:, g, :], MUL).then_inc(sc_out, 1)
                    if g:
                        short_low(g - 1)
                if 2 <= j:
                    conv_taps(min(5, CONF_K * (min(CG, (j + 1) // 2) // 2) - taps_done[0]))
                if j - 1 in ADA_IN1:
                    ada_take(ADA_IN1[j - 1])
                if j == 15:
                    conv_taps(len(tap_list) - taps_done[0])
                    dve.sem_inc(conf_ready, 1)
                if j == 16:
                    for half in range(2):
                        b = wait_tile(dve, ("csum", half))
                        g = 2 * half
                        nc.vector.scalar_tensor_tensor(
                            out=ccen[:, g:g + 2, :].rearrange("p g t -> p (g t)"), in0=b[:, :], scalar=-1.0 / P,
                            in1=cacc[:, g:g + 2, :].rearrange("p g t -> p (g t)"), op0=MUL, op1=ADD).then_inc(cen_ready, 1)
                if j == 18:
                    invert("conf")
            short_low(CG - 1)
            for half in range(2):
                g = 2 * half
                inv = wait_tile(dve, ("inv", "conf", half))
                cg = ccen[:, g:g + 2, :].rearrange("p g t -> p (g t)")
                nc.vector.tensor_tensor(cg, cg, inv[:, :], MUL).then_inc(cn_ready, 1)
            for g in range(CG):
                dve.wait_ge(o_hi, 12 + g + 1)
                nc.vector.tensor_tensor(h_lo[:, g, 0:T], cacc[:, g, :], h_hi[:, g, 0:T].bitcast(fp), SUB)\
                    .then_inc(o_lo, 1)
            project_out(1, W_OUT1)
            norm(4)
            norm(5)
            ffn(1)
            norm(6)
            for j in range(17):
                if j < 16:
                    split_to(W_K2 + j + LEAD)
                    b = wait_tile(dve, ("qk", j))
                    n = 2 * T if j < 8 else T
                    dst = keysT[:, j, :] if j < 8 else querT[:, j - 8, :]
                    dve.wait_ge(usq_ready, 8 + j + 1)
                    nc.vector.tensor_scalar(dst, b[:, 0:n], pc("na_k" if j < 8 else "na_q"), None, MUL)\
                        .then_inc(unit_ready, 1)
                    dve.wait_ge(unit_ready, 8 + j + 1)
                if j:
                    i = j - 1
                    n = 2 * T if i < 8 else T
                    dst = keysT[:, i, :] if i < 8 else querT[:, i - 8, :]
                    invert(("qk", i))
                    inv = wait_tile(dve, ("inv", "qk", i))
                    nc.vector.scalar_tensor_tensor(out=dst, in0=dst, scalar=1.0 if i < 8 else NA_D ** -0.5,
                                                   in1=inv[:, 0:n], op0=MUL, op1=MUL).then_inc(head_ready, 1)
            for half in range(2):
                split_to(W_V2 + 4 * half + 3 + LEAD - 1)
            attention("na", NA_H, 16, 16, ADA_NA, W_OUT2)
            project_out(2, W_OUT2)
            nc.vector.memset(gpad, 0.0).then_inc(pads_ready, 1)
            norm(7)
            ffn(2)

        @block.tensor
        def _(pe):
            def split3(out, a_hi, a_lo, b_hi, b_lo, start, stop):
                nc.tensor.matmul(out, a_hi, b_hi, start=start, stop=False)
                nc.tensor.matmul(out, a_hi, b_lo, start=False, stop=False)
                return nc.tensor.matmul(out, a_lo, b_hi, start=False, stop=stop)

            def wtile(w, c0, n):
                return w_hi[:, w % RING, c0:c0 + n], w_lo[:, w % RING, c0:c0 + n]

            def split_ready(w):
                pe.wait_ge(split_done, w + 1)

            def ada_rows(g):
                if g:
                    pe.wait_ge(mod_ready, g)
                else:
                    pe.wait_ge(ada_cleared, 1)
                for k in range(KT):
                    s, part = k // 2, k % 4
                    if k % 2 == 0:
                        pe.wait_ge(a_loaded[s], 16 * g + 16)
                    ins = nc.tensor.matmul(bank[6][32 * part:32 * part + 2, :], cs[:, g // (MODS // AGRP), k, :],
                                           a_raw[:, s, (k % 2) * 512:(k % 2 + 1) * 512], start=(k < 4), stop=(k >= 4),
                                           tile_position=(0, 32 * part))
                    if k % 2:
                        ins.then_inc(a_used, 1)

            def ada_columns(g):
                pe.wait_ge(ada_copied, g + 1)
                for m in range(AGRP):
                    ins = nc.tensor.matmul(bank[6][:, 2 * m:2 * m + 2], ada_s[:, m * P:(m + 1) * P], cc("of_cond"),
                                           start=True, stop=True)
                ins.then_inc(ada_turned, 1)

            def sums(name, tiles_of, select):
                b = write_tile(pe, ("sum", name))
                n = select.shape[1]
                for t, parts in enumerate(tiles_of):
                    for k, part in enumerate(parts):
                        ins = nc.tensor.matmul(b[:, t * n:(t + 1) * n], part, select, start=(k == 0),
                                               stop=(k == len(parts) - 1))
                ins.then_inc(full_of(("sum", name)), 1)

            def spread(name, cols, m=P):
                b = write_tile(pe, name)
                for t, c in enumerate(cols):
                    ins = nc.tensor.matmul(b[0:m, t * P:(t + 1) * P], c, ident, start=True, stop=True)
                ins.then_inc(full_of(name), 1)

            def column(c, m=P):
                return stat[:, c:c + 1].broadcast_to([P, m])

            def norm_sums(n):
                b = write_tile(pe, ("sum", ("norm", n)))
                at = SQ_ORDER.index(n)
                ks = [0, *range(POOLED[n], KT)]
                ks = ks[1:] + ks[:1] if POOLED[n] < KT - 1 else ks
                for k in ks:
                    if k:
                        pe.wait_ge(sq_ready, KT * at + k + 1)
                    else:
                        pe.wait_ge(added, sum(POOLED[m] - 1 for m in SQ_ORDER[:at + 1]))
                    for t in range(2):
                        ins = nc.tensor.matmul(b[:, t:t + 1], sq_of(n)[:, k, t * P:(t + 1) * P], ones,
                                               start=(k == ks[0] and t == 0), stop=(k == ks[-1] and t == 1))
                ins.then_inc(full_of(("sum", ("norm", n))), 1)

            def norm_spread(n):
                pe.wait_ge(inv_ready, STAT_ORDER.index(("norm", n)) + 1)
                c0 = STATS["norm", n][0]
                spread(("inv", n), [column(c0), column(c0 + 1)])

            def norm(n):
                norm_sums(n)
                norm_spread(n)

            def project(name, w, rhs, n, after_norm=None):
                b = write_tile(pe, name)
                split_ready(w)
                for k in range(KT):
                    if after_norm is not None:
                        pe.wait_ge(hlo_ready, KT * after_norm + k + 1)
                    a = wtile(w, k * P, P)
                    ins = split3(b[:, 0:n], a[0], a[1], rhs(h_hi, k), rhs(h_lo, k), k == 0, k == KT - 1)
                ins.then_inc(w_used, 1)

            def project_four(names, w, rhs, order, ready):
                banks = [write_tile(pe, name) for name in names]
                split_ready(w + len(names) - 1)
                for k in order:
                    pe.wait_ge(*ready(k))
                    for j, b in enumerate(banks):
                        a = wtile(w + j, k * P, P)
                        ins = split3(b[:, 0:T], a[0], a[1], rhs(h_hi, k), rhs(h_lo, k), k == order[0], k == order[-1])
                        if k == order[-1]:
                            ins.then_inc(w_used, 1)

            def both(h, k):
                return h[:, k, :]

            def xs(h, k):
                return h[:, k, T:2 * T]

            def mixed(h, k):
                return h[:, k, 0:T]

            def attention(name, heads, at0, rows, values, ada_at):
                def scores(j):
                    for n in (2 * j, 2 * j + 1):
                        b = write_tile(pe, (name, "sc", n))
                        q, k = rows(2 * (j // 2) + n % 2)
                        t = j % 2
                        nc.tensor.matmul(b[:, :], q[:, t * P:(t + 1) * P], k, start=True, stop=True)\
                            .then_inc(full_of((name, "sc", n)), 1)

                def turn(n):
                    b = write_tile(pe, (name, "tr", n))
                    pe.wait_ge(prob_ready, at0 + n + 1)
                    for kt in range(4):
                        ins = nc.tensor.transpose(b[:, kt * P:(kt + 1) * P], prob[:, n % PROBS, kt * P:(kt + 1) * P],
                                                  ident)
                    ins.then_inc(full_of((name, "tr", n)), 1)

                def weigh(j):
                    p, t = j // 2, j % 2
                    pe.wait_ge(pT_ready, at0 + 2 * j + 2)
                    b = write_tile(pe, (name, "o", p)) if t == 0 else bank[tiles[(name, "o", p)][0]]
                    for kt in range(4):
                        for e in range(2):
                            ins = nc.tensor.matmul(b[e * VH:(e + 1) * VH, t * P:(t + 1) * P], values(2 * p + e, kt),
                                                   probT[:, j % 2, e, kt, :], start=(kt == 0), stop=(kt == 3))
                            if kt == 3:
                                ins.then_inc(pv_done, 1)

                scores(0)
                for j in range(heads):
                    if j + 1 < heads:
                        scores(j + 1)
                    if j:
                        weigh(j - 1)
                    if j - 1 in ada_at:
                        ada_columns(ada_at[j - 1])
                    turn(2 * j)
                    turn(2 * j + 1)
                    if j in ada_at:
                        ada_rows(ada_at[j])
                weigh(heads - 1)

            def project_out(layer, w0):
                def mixed_ready(k):
                    return (o_lo, 8 * layer + (1 + (k if layer == 2 else (k + 4) % KT)))

                order = list(range(KT)) if layer == 2 else [4, 5, 6, 7, 0, 1, 2, 3]
                project_four([("out", layer, j) for j in range(4)], w0, mixed, order, mixed_ready)
                for j in range(4, KT):
                    if layer == 0 and j == 5:
                        norm_sums(5)
                    project(("out", layer, j), w0 + j, mixed, T)

            def ffn(layer):
                w0, g0 = (W_FF0, W_FF1, W_FF2)[layer], FT * layer
                if layer == 0:
                    pe.wait_ge(const_ready, 3)
                for b4 in range(4):
                    b = write_tile(pe, ("acc", layer, b4))
                    for q4 in range(4):
                        nc.tensor.matmul(b[:, q4 * P:(q4 + 1) * P], zero_r[:, :], zero_r[:, :], start=(q4 == 0),
                                         stop=False)
                def turn(i, splits_on=True):
                    def up(s):
                        b = tiles[("up", layer, s)][0]
                        pe.wait_ge(ff_mul, 2 * i + (g0 + s + 1))
                        write_tile(pe, ("up", layer, s))
                        if layer == 2:
                            write_tile(pe, ("gate", s))
                        for e in range(2):
                            w = w0 + 2 * s + e
                            pe.wait_ge(split_done, 6 * i + (w + 1))
                            out = (bank[b][:, e * T:(e + 1) * T] if layer < 2 else bank[b][:, 0:T] if e
                                   else bank[tiles["gate", s][0]][:, 0:T])
                            for k in range(KT):
                                if s == 0 and e == 0:
                                    pe.wait_ge(hlo_ready, KT * (2, 4, 7)[layer] + k + 1)
                                a = wtile(w, k * P, P)
                                ins = split3(out, a[0], a[1], xs(h_hi, k), xs(h_lo, k),
                                             k == 0, k == KT - 1)
                            ins.then_inc(w_used, 1)

                    def down(s):
                        w = w0 + 4 + s
                        pe.wait_ge(split_done, 6 * i + (w + 1))
                        pe.wait_ge(ff_lo, 2 * i + (g0 + s + 1))
                        for j in range(KT):
                            b = bank[tiles[("acc", layer, j // 2)][0]]
                            a = wtile(w, j * P, P)
                            out = b[:, (j % 2) * T:(j % 2 + 1) * T]
                            ins = split3(out, a[0], a[1], g_hi[:, s, :], g_lo[:, s, :], False, False)
                        ins.then_inc(w_used, 1)

                    up(0)
                    up(1)
                    down(0)
                    down(1)

                with pe.Fori(0, FT // 2 - (layer == 2)) as i:
                    turn(i)
                if layer == 2:
                    turn(FT // 2 - 1, splits_on=False)
                for b4 in range(4):
                    name = ("acc", layer, b4)
                    for q4 in range(4):
                        ins = nc.tensor.matmul(bank[tiles[name][0]][:, q4 * P:(q4 + 1) * P], zero_r[:, :], zero_r[:, :],
                                               start=False, stop=(q4 == 3))
                    ins.then_inc(full_of(name), 1)

            pe.wait_ge(cs_ready, 1)
            for g in range(4):
                ada_rows(g)
                if g == 0:
                    pe.wait_ge(s_con, 16)
                ada_columns(g)
                if 0 < g < 3:
                    norm_sums(g - 1)
            norm_spread(0)
            norm_spread(1)
            for j in range(N_IN0):
                if j == 7:
                    pe.wait_ge(hlo_ready, 2 * KT)
                if j < 7:
                    project(("in0", j), W_IN0 + j, xs, T, after_norm=0 if j == 0 else None)
                else:
                    project(("in0", j), W_IN0 + j, both, 2 * T)
                if j in ADA_IN0:
                    ada_rows(ADA_IN0[j])
                if j - 1 in ADA_IN0:
                    ada_columns(ADA_IN0[j - 1])
            lsq = sq[:, :, :].rearrange("p k t -> p (k t)")
            pe.wait_ge(lsq_ready, 1)
            sums("kv", [[lsq[:, k * 512 + t * P:k * 512 + (t + 1) * P] for k in range(KVL_T)] for t in range(4)],
                 ones)
            pe.wait_ge(lsq_ready, 2)
            sums("ql", [[lsq[:, 1024 + k * T + t * P:1024 + k * T + (t + 1) * P] for k in range(QL_T)]
                        for t in range(2)], ones)
            ada_rows(ADA_LATENT[0])
            pe.wait_ge(lat_ready, N_IN0 - 1)
            for g in range(FN_T):
                b = write_tile(pe, ("dft1", g))
                for t in range(2):
                    ins = nc.tensor.matmul(b[:, t * T:(t + 1) * T], fu[:, g, t * P:(t + 1) * P], cc("dft_c"),
                                           start=True, stop=True)
                ins.then_inc(full_of(("dft1", g)), 1)
            ada_columns(ADA_LATENT[0])
            pe.wait_ge(inv_ready, STAT_ORDER.index("ql") + 1)
            c0 = STATS["kv"][0]
            spread(("inv", "kv"), [column(c0 + t) for t in range(4)])
            c0 = STATS["ql"][0]
            spread(("inv", "ql"), [column(c0 + t) for t in range(2)])
            ada_rows(ADA_LATENT[1])
            for g in range(FN_T):
                b = write_tile(pe, ("dft2", g))
                pe.wait_ge(f1_ready, g + 1)
                n = 0
                for part in range(2):
                    for t in range(2):
                        ins = nc.tensor.matmul(b[:, 0:T], f1[:, g, t, part * P:(part + 1) * P],
                                               cc("dft_n", (2 * part + t) * T, (2 * part + t + 1) * T),
                                               start=(n == 0), stop=(n == 3))
                        n += 1
                ins.then_inc(full_of(("dft2", g)), 1)
            ada_columns(ADA_LATENT[1])
            def ckvn(h, k):
                return h[:, 2 * k:2 * k + 2, T:2 * T]

            def unit_products(u):
                b = write_tile(pe, ("pj", u))
                if u < 4:
                    pe.wait_ge(llo_ready, KVL_T + QL_T)
                    for e in range(2):
                        for k in range(QL_T):
                            n = QL_T * (2 * u + e) + k
                            split_ready(W_UQ + n // KT)
                            a = wtile(W_UQ + n // KT, (n % KT) * P, P)
                            ins = split3(b[:, e * T:(e + 1) * T], a[0], a[1], h_hi[:, 4 + k, T:2 * T],
                                         h_lo[:, 4 + k, T:2 * T], k == 0, k == QL_T - 1)
                else:
                    split_ready(W_UK)
                    for k in range(KVL_T):
                        a = wtile(W_UK, ((u - 4) * KVL_T + k) * P, P)
                        ins = split3(b[:, :], a[0], a[1], ckvn(h_hi, k), ckvn(h_lo, k), k == 0, k == KVL_T - 1)
                if u < 7:
                    ins.then_inc(full_of(("pj", u)), 1)
                else:
                    ins.then_inc(w_used, 1)

            def unit_sums(u):
                pe.wait_ge(usq_ready, u + 1)
                if u < 4:
                    b = write_tile(pe, ("sum", "mq")) if u == 0 else bank[tiles["sum", "mq"][0]]
                    for e in range(2):
                        for t in range(2):
                            c = 2 * (2 * u + e) + t
                            ins = nc.tensor.matmul(b[:, c:c + 1], usq[:, u % 2, e * T + t * P:e * T + (t + 1) * P],
                                                   cc("of_query"), start=True, stop=True)
                    if u == 3:
                        ins.then_inc(full_of(("sum", "mq")), 1)
                        pe.wait_ge(full_of(("sum", "mq")), tiles["sum", "mq"][1][1])
                        pe.sem_inc(w_used, N_UQ)
                else:
                    b = bank[tiles["sum", "mk"][0]]
                    if u == 4:
                        write_tile(pe, ("sum", "mk"))
                        pe.wait_ge(krsq_ready, 1)
                        for t in range(4):
                            nc.tensor.matmul(b[:, t * MLA_H:(t + 1) * MLA_H], kr_sq[:, t * P:(t + 1) * P], cc("of_rope"),
                                             start=(t == 0), stop=False)
                    for t in range(4):
                        c = t * MLA_H + 2 * (u - 4)
                        ins = nc.tensor.matmul(b[:, c:c + 2], usq[:, u % 2, t * P:(t + 1) * P], cc("of_pair"),
                                               start=False, stop=(u == 7 and t == 3))
                    if u == 7:
                        ins.then_inc(full_of(("sum", "mk")), 1)

            unit_products(0)
            for u in range(8):
                if u == 3:
                    unit_sums(3)
                    unit_products(4)
                else:
                    if u + 1 < 8:
                        unit_products(u + 1)
                    unit_sums(u)
                if u in ADA_UNITS:
                    ada_rows(ADA_UNITS[u])
                elif u - 1 in ADA_UNITS:
                    ada_columns(ADA_UNITS[u - 1])
            split_ready(W_UV)
            for t in range(4):
                b = write_tile(pe, ("v0", t))
                for k in range(KVL_T):
                    at = (2 * k + t // 2, T + (t % 2) * P)
                    xh, xl = (h[:, at[0], at[1]:at[1] + P] for h in (h_hi, h_lo))
                    a = wtile(W_UV, k * 512, 512)
                    ins = split3(b[:, :], xh, xl, a[0], a[1], k == 0, k == KVL_T - 1)
                ins.then_inc(full_of(("v0", t)) if t < 3 else w_used, 1)
            pe.wait_ge(inv_ready, STAT_ORDER.index("mk") + 1)
            c0 = STATS["mk"][0]
            for h in range(MLA_H):
                spread(("inv", "mk", h), [column(c0 + t * MLA_H + h, QK) for t in range(4)], QK)
            pe.wait_ge(v_ready, 4)
            pe.wait_ge(head_ready, MLA_H)
            attention("mla", MLA_H, 0, lambda h: (querT[0:QK, h, :], keysT[0:QK, h, :]),
                      lambda h, kt: vals0[:, kt, h * VH:(h + 1) * VH], ADA_MLA)
            project_out(0, W_OUT0)
            norm(2)
            ffn(0)
            norm(3)
            project_four([("in1", j) for j in range(4)], W_IN1, xs, range(KT), lambda k: (hlo_ready, 3 * KT + k + 1))
            for j in range(3, N_IN1):
                if j > 3:
                    project(("in1", j), W_IN1 + j, xs, T)
                if j in ADA_IN1:
                    ada_rows(ADA_IN1[j])
                if j - 1 in ADA_IN1:
                    ada_columns(ADA_IN1[j - 1])
                if j == 15:
                    pe.wait_ge(conf_ready, 9)
                    pe.wait_ge(pool_taps, added_to(len(POOL_TAPS) - 1))
                    for half in range(2):
                        b = write_tile(pe, ("csum", half))
                        nc.tensor.matmul(b[:, :], ones.broadcast_to([P, P]),
                                         cacc[:, 2 * half:2 * half + 2, :].rearrange("p g t -> p (g t)"),
                                         start=True, stop=True).then_inc(full_of(("csum", half)), 1)
                if j == 17:
                    pe.wait_ge(csq_ready, 2)
                    sums("conf", [[csq[:, g, t * P:(t + 1) * P]] for g in range(CG) for t in range(2)], ones)
            pe.wait_ge(inv_ready, STAT_ORDER.index("conf") + 1)
            c0 = STATS["conf"][0]
            for half in range(2):
                spread(("inv", "conf", half), [column(c0 + 4 * half + t) for t in range(4)])
            project_out(1, W_OUT1)
            norm(4)
            norm_spread(5)
            ffn(1)
            norm(6)
            def spread_qk(i):
                pe.wait_ge(inv_ready, STAT_ORDER.index(("qk", i)) + 1)
                c0 = STATS["qk", i][0]
                b = write_tile(pe, ("inv", "qk", i))
                for t in range(4 if i < 8 else 2):
                    for e in range(2):
                        ins = nc.tensor.matmul(b[e * NA_D:(e + 1) * NA_D, t * P:(t + 1) * P],
                                               column(c0 + 2 * t + e, NA_D), ident, start=True, stop=True)
                ins.then_inc(full_of(("inv", "qk", i)), 1)

            for j in range(17):
                if j < 16:
                    project(("qk", j), W_K2 + j, both if j < 8 else xs, 2 * T if j < 8 else T,
                            after_norm=6 if j == 0 else None)
                if j:
                    i = j - 1
                    pe.wait_ge(usq_ready, 8 + i + 1)
                    sums(("qk", i), [[nsq[:, i % 2, t * P:(t + 1) * P]] for t in range(4 if i < 8 else 2)], cc("of_pair"))
                if j > 1:
                    spread_qk(j - 2)
            spread_qk(15)
            for half in range(2):
                banks = [write_tile(pe, ("v2", half, t)) for t in range(4)]
                for q4 in range(4):
                    w = W_V2 + 4 * half + q4
                    split_ready(w)
                    for e in range(2):
                        k = 2 * q4 + e
                        a = wtile(w, e * 512, 512)
                        for t in range(4):
                            ins = split3(banks[t][:, :], h_hi[:, k, t * P:(t + 1) * P], h_lo[:, k, t * P:(t + 1) * P],
                                         a[0], a[1], k == 0, k == KT - 1)
                            if k == KT - 1 and t < 3:
                                ins.then_inc(full_of(("v2", half, t)), 1)
                    ins.then_inc(w_used, 1)
            pe.wait_ge(v_ready, 12)
            pe.wait_ge(head_ready, MLA_H + 16)
            attention("na", NA_H, 16,
                      lambda h: (querT[(h % 2) * NA_D:(h % 2 + 1) * NA_D, h // 2, :],
                                 keysT[(h % 2) * NA_D:(h % 2 + 1) * NA_D, h // 2, :]),
                      lambda h, kt: vals[:, kt, h * NA_D:(h + 1) * NA_D], ADA_NA)
            project_out(2, W_OUT2)
            norm(7)
            ffn(2)


def pack_weights(i):
    w = np.zeros((N_W, P, BLK), np.float32)

    def across(at, m, tiles=None):
        n = m.shape[1] // P
        w[at:at + n] = m.reshape(KT, P, n, P).transpose(2, 1, 0, 3).reshape(n, P, BLK)

    def ffn(at, w1, w3, w2):
        b = w[at:at + 3 * FT].reshape(FT // 2, 6, P, BLK)
        for e, m in enumerate((w1, w3)):
            up = m.reshape(KT, P, FT // 2, 2, P).transpose(2, 3, 1, 0, 4).reshape(FT // 2, 2, P, BLK)
            b[:, e], b[:, 2 + e] = up[:, 0], up[:, 1]
        down = w2.reshape(FT // 2, 2, P, BLK)
        b[:, 4], b[:, 5] = down[:, 0], down[:, 1]

    a = i["a_w_in"][0]
    q, kv, kr, fn = np.split(a, [QL_T * P, (QL_T + KVL_T) * P, (QL_T + KVL_T) * P + ROPE_D], axis=1)
    swapped = np.r_[QK - ROPE_D // 2:QK, NOPE:QK - ROPE_D // 2]
    across(W_IN0, np.concatenate([q, fn, kv, np.zeros((D, NOPE), np.float32), kr, kr[:, swapped - NOPE]], axis=1))
    uq = i["a_w_uq"][0].reshape(QL_T, P, MLA_H, QK)
    uq = np.concatenate([uq, uq[..., swapped]], axis=-1).transpose(2, 0, 1, 3)
    w[W_UQ:W_UQ + N_UQ] = uq.reshape(N_UQ, KT, P, P).transpose(0, 2, 1, 3).reshape(N_UQ, P, BLK)
    uk = i["a_w_uk"][0].reshape(KVL_T, P, MLA_H // 2, P)
    w[W_UK] = uk.transpose(1, 2, 0, 3).reshape(P, BLK)
    w[W_UV] = i["a_w_uv"][0].reshape(KVL_T, P, 512).transpose(1, 0, 2).reshape(P, BLK)
    across(W_OUT0, i["a_w_out"][0])
    ffn(W_FF0, i["ffn_w1"][0], i["ffn_w3"][0], i["ffn_w2"][0])
    a, gate, sb_, scc, sx = np.split(i["b_w_in"][0], 5, axis=1)

    def woven(u, v):
        return np.stack([u.reshape(D, 4, P), v.reshape(D, 4, P)], axis=2).reshape(D, 8 * P)

    across(W_IN1, np.concatenate([woven(gate, a), woven(scc, sx), sb_], axis=1))
    across(W_OUT1, i["b_w_out"][0])
    ffn(W_FF1, i["ffn_w1"][1], i["ffn_w3"][1], i["ffn_w2"][1])
    q, k, v = np.split(i["l0_na_w_qkv_2"], 3, axis=1)
    across(W_K2, k)
    across(W_Q2, q)
    w[W_V2:W_V2 + 8] = v.reshape(4, 2, P, 2, 512).transpose(3, 0, 2, 1, 4).reshape(8, P, BLK)
    across(W_OUT2, i["l0_na_w_o_2"])
    up = i["l0_ffn_w_up_2"]
    ffn(W_FF2, up[:, F_FF:], up[:, :F_FF], i["l0_ffn_w_down_2"])
    return w


def pack_ada(i):
    m = np.stack([i["ada_w"][0], i["ada_w"][1], i["l0_w_mod_2"]])
    m = m.reshape(LAYERS, AGRP, 2, P, MODS // AGRP, AGRP * P)
    return np.ascontiguousarray(m.transpose(0, 4, 1, 3, 2, 5).reshape(N_A, P, BLK))


def by_partition(v):
    return np.moveaxis(v.reshape(*v.shape[:-1], -1, P), -1, 0).reshape(P, -1)


def pack_params(i):
    t = np.zeros((P, N_PARAMS), np.float32)

    def put(name, a):
        c0, c1 = PARAMS[name]
        assert a.shape[1] == c1 - c0, name
        t[:a.shape[0], c0:c1] = a

    pairs = [(i["c"][0], i["c_ctx"]), (i["c"][0], i["c_ctx"]), (i["c_2"][0], i["c_ctx_2"])]
    c = np.stack([np.stack([u.reshape(KT, P), v.reshape(KT, P)], axis=-1) for u, v in pairs])
    put("c", c.transpose(2, 0, 1, 3).reshape(P, -1))
    put("ada_b", by_partition(np.stack([i["ada_b"][0], i["ada_b"][1], i["l0_b_mod_2"]])))
    put("norm1", by_partition(np.stack([i["norm1_g"][0], i["norm1_g"][1], i["l0_norm1_2"]])))
    put("norm2", by_partition(np.stack([i["norm2_g"][0], i["norm2_g"][1], i["l0_norm2_2"]])))
    put("q_ln", by_partition(i["a_q_ln_g"][0]))
    put("kv_ln", by_partition(i["a_kv_ln_g"][0]))
    swapped = np.r_[0:QK, QK - ROPE_D // 2:QK, NOPE:QK - ROPE_D // 2]
    put("q_norm", i["a_q_norm_g"][0][swapped][:, None])
    put("k_norm", i["a_k_norm_g"][0][swapped][:, None])
    put("k_nope", np.tile(i["a_k_norm_g"][0][:NOPE], 2)[:, None])
    put("conf_dw", i["b_conf_dw"][0].reshape(CONF_K, CG, P).transpose(2, 1, 0).reshape(P, -1))
    put("conf_b", by_partition(i["b_conf_dw_b"][0]))
    put("ln_g", by_partition(i["b_conf_ln_g"][0]))
    put("ln_b", by_partition(i["b_conf_ln_b"][0]))
    put("sc_dw", i["b_sc_dw"][0].reshape(SC_K, CG, P).transpose(2, 1, 0).reshape(P, -1))
    put("na_q", np.tile(i["l0_na_q_gain_2"], 2)[:, None])
    put("na_k", np.tile(i["l0_na_k_gain_2"], 2)[:, None])
    conv = np.concatenate([i["l0_ffn_conv_w_2"], i["l0_ffn_conv_b_2"][None]])
    put("ff_conv", conv.reshape(4, FT, P).transpose(2, 1, 0).reshape(P, -1))
    return t


def feature_major(x):
    return np.ascontiguousarray(x[0].reshape(T, KT, P).transpose(2, 1, 0))


def pack_rpb(rpb):
    rows = rpb[:, WIN // 2 - ROWS:WIN // 2 - 1 + ROWS, :]
    side = (TOEP - rpb.shape[2]) // 2
    t = np.pad(rows[:, ::-1], ((0, 0), (0, 0), (side, side))).transpose(0, 2, 1)
    return np.pad(t.reshape(-1), (0, 64))


def kernel(**inputs):
    import concourse.bacc as bacc
    from concourse.bass_utils import run_bass_kernel_spmd as run

    i = {k: np.asarray(v) for k, v in inputs.items()}
    arrays = {
        "weights": pack_weights(i), "ada": pack_ada(i), "xt": feature_major(i["x"]),
        "ctx1": feature_major(i["ctx"]), "ctx2": feature_major(i["ctx_2"]), "params": pack_params(i),
        "consts": constant_table(), "rpb": pack_rpb(i["l0_na_rpb_2"])}
    nc = bacc.Bacc("TRN2", target_bir_lowering=False, num_devices=1)
    args = [nc.dram_tensor(n, a.shape, mybir.dt.from_np(a.dtype), kind="ExternalInput").ap()
            for n, a in arrays.items()]
    out = nc.dram_tensor("out_t", (P, KT, T), mybir.dt.float32, kind="ExternalOutput").ap()
    program(nc, *args, out)
    got = run(nc, [arrays], core_ids=[0]).results[0]["out_t"]
    return got.transpose(2, 1, 0).reshape(1, T, D)
```
